# Optimizing a Trainium2 kernel written in Bass

```python
import jax, jax.numpy as jnp
from jax import lax
import numpy as np
import math

D_MODEL = 2048
BATCH = 1
SEQ = 256
DEPTH = 1

CONV_CH = 1024
CONV_K = 31
N_HEADS = 8
QK_NOPE = 128
QK_ROPE = 64
V_HEAD = 128
QK_HEAD = QK_NOPE + QK_ROPE
Q_LORA = 768
KV_LORA = 512
ATTN_CH = N_HEADS * V_HEAD
MIX_WIDTH = CONV_CH + ATTN_CH
IN_COLS = 2 * CONV_CH + Q_LORA + KV_LORA + QK_ROPE
ROPE_THETA = 10000.0
Q_BLOCK = 128
D_FF = ((8 * D_MODEL // 3 + 255) // 256) * 256
EPS = 1e-6


def rmsnorm(x, g):
    xf = x.astype(jnp.float32)
    y = xf * lax.rsqrt(jnp.mean(xf * xf, axis=-1, keepdims=True) + EPS)
    return (y * g.astype(jnp.float32)).astype(x.dtype)

def layernorm(x, g, b):
    xf = x.astype(jnp.float32)
    mu = jnp.mean(xf, axis=-1, keepdims=True)
    var = jnp.mean(jnp.square(xf - mu), axis=-1, keepdims=True)
    y = (xf - mu) * lax.rsqrt(var + EPS)
    return (y * g.astype(jnp.float32) + b.astype(jnp.float32)).astype(x.dtype)

def rope_tables(positions, dtype):
    inv_freq = ROPE_THETA ** (-jnp.arange(0, QK_ROPE, 2, dtype=jnp.float32) / QK_ROPE)
    ang = positions.astype(jnp.float32)[..., None] * inv_freq
    return jnp.cos(ang).astype(dtype), jnp.sin(ang).astype(dtype)

def apply_rope(x, cos, sin):
    x1, x2 = jnp.split(x, 2, axis=-1)
    return jnp.concatenate([x1 * cos - x2 * sin, x2 * cos + x1 * sin], axis=-1)

def causal_depthwise_conv(u, w, b):
    y = lax.conv_general_dilated(
        u, w[:, None, :], window_strides=(1,), padding=[(CONV_K - 1, 0)],
        dimension_numbers=("NWC", "WIO", "NWC"), feature_group_count=u.shape[-1])
    return y + b

def causal_attention(q, k, v):
    B, S, H, Dq = q.shape
    nblk = S // Q_BLOCK
    qb = q.reshape(B, nblk, Q_BLOCK, H, Dq).transpose(1, 0, 2, 3, 4)
    kpos = jnp.arange(S)
    scale = Dq ** -0.5
    neg = jnp.finfo(jnp.float32).min

    def one_block(args):
        i, qi = args
        s = jnp.einsum('bqhd,bkhd->bhqk', qi, k).astype(jnp.float32) * scale
        qpos = i * Q_BLOCK + jnp.arange(Q_BLOCK)
        s = jnp.where(kpos[None, :] <= qpos[:, None], s, neg)
        p = jax.nn.softmax(s, axis=-1).astype(v.dtype)
        return jnp.einsum('bhqk,bkhd->bqhd', p, v)

    out = lax.map(one_block, (jnp.arange(nblk), qb))
    return out.transpose(1, 0, 2, 3, 4).reshape(B, S, H * v.shape[-1])

def first_inputs(seed: int = 0) -> dict:
    key = jax.random.key(seed)
    ks = jax.random.split(key, 24)
    f = jnp.float32
    L = DEPTH

    def w(k, shape, fan_in):
        return jax.random.normal(k, shape, f) * (fan_in ** -0.5)

    def gain(k, n):
        return jnp.ones((L, n), f) + 0.05 * jax.random.normal(k, (L, n), f)

    x = jax.random.normal(ks[0], (BATCH, SEQ, D_MODEL), f)
    offset = jax.random.randint(ks[1], (BATCH, 1), 0, 1024, dtype=jnp.int32)
    positions = offset + jnp.arange(SEQ, dtype=jnp.int32)[None, :]
    return {
        "x": x,
        "positions": positions,
        "pre_mix_norm": gain(ks[2], D_MODEL),
        "w_in": w(ks[3], (L, D_MODEL, IN_COLS), D_MODEL),
        "q_norm": gain(ks[4], Q_LORA),
        "w_uq": w(ks[5], (L, Q_LORA, N_HEADS * QK_HEAD), Q_LORA),
        "kv_norm": gain(ks[6], KV_LORA),
        "w_ukv": w(ks[7], (L, KV_LORA, N_HEADS * (QK_NOPE + V_HEAD)), KV_LORA),
        "conv_w": w(ks[8], (L, CONV_K, CONV_CH), CONV_K),
        "conv_b": 0.02 * jax.random.normal(ks[9], (L, CONV_CH), f),
        "conv_ln_g": gain(ks[10], CONV_CH),
        "conv_ln_b": 0.02 * jax.random.normal(ks[11], (L, CONV_CH), f),
        "conv_out_norm": gain(ks[12], CONV_CH),
        "attn_out_norm": gain(ks[13], ATTN_CH),
        "w_out": w(ks[14], (L, MIX_WIDTH, D_MODEL), MIX_WIDTH),
        "post_mix_norm": gain(ks[15], D_MODEL),
        "pre_ffn_norm": gain(ks[16], D_MODEL),
        "w_gate": w(ks[17], (L, D_MODEL, D_FF), D_MODEL),
        "w_up": w(ks[18], (L, D_MODEL, D_FF), D_MODEL),
        "w_down": w(ks[19], (L, D_FF, D_MODEL), D_FF),
        "post_ffn_norm": gain(ks[20], D_MODEL),
    }

def first_block(x, positions, pre_mix_norm, w_in, q_norm, w_uq, kv_norm, w_ukv,
              conv_w, conv_b, conv_ln_g, conv_ln_b, conv_out_norm, attn_out_norm,
              w_out, post_mix_norm, pre_ffn_norm, w_gate, w_up, w_down, post_ffn_norm):
    B, S, _ = x.shape
    cos, sin = rope_tables(positions, x.dtype)
    c1 = 2 * CONV_CH
    c2 = c1 + Q_LORA
    c3 = c2 + KV_LORA
    for l in range(DEPTH):
        h = rmsnorm(x, pre_mix_norm[l])
        z = h @ w_in[l]
        conv_in, q_lat, kv_lat, k_rope = z[..., :c1], z[..., c1:c2], z[..., c2:c3], z[..., c3:]

        a, g = jnp.split(conv_in, 2, axis=-1)
        u = a * jax.nn.sigmoid(g)
        u = causal_depthwise_conv(u, conv_w[l], conv_b[l])
        u = jax.nn.silu(layernorm(u, conv_ln_g[l], conv_ln_b[l]))

        q = (rmsnorm(q_lat, q_norm[l]) @ w_uq[l]).reshape(B, S, N_HEADS, QK_HEAD)
        q_nope, q_pe = q[..., :QK_NOPE], q[..., QK_NOPE:]
        q_pe = apply_rope(q_pe, cos[:, :, None, :], sin[:, :, None, :])
        kv = (rmsnorm(kv_lat, kv_norm[l]) @ w_ukv[l]).reshape(B, S, N_HEADS, QK_NOPE + V_HEAD)
        k_nope, v = kv[..., :QK_NOPE], kv[..., QK_NOPE:]
        k_pe = apply_rope(k_rope, cos, sin)
        k_pe = jnp.broadcast_to(k_pe[:, :, None, :], (B, S, N_HEADS, QK_ROPE))
        q_full = jnp.concatenate([q_nope, q_pe], axis=-1)
        k_full = jnp.concatenate([k_nope, k_pe], axis=-1)
        attn = causal_attention(q_full, k_full, v)

        mix = jnp.concatenate([rmsnorm(u, conv_out_norm[l]),
                               rmsnorm(attn, attn_out_norm[l])], axis=-1) @ w_out[l]
        x = x + rmsnorm(mix, post_mix_norm[l])

        hf = rmsnorm(x, pre_ffn_norm[l])
        ff = (jax.nn.silu(hf @ w_gate[l]) * (hf @ w_up[l])) @ w_down[l]
        x = x + rmsnorm(ff, post_ffn_norm[l])
    return x


HEAD_DIM = 128
N_GDN_HEADS = 8
N_MOBA_HEADS = 8
GDN_WIDTH = N_GDN_HEADS * HEAD_DIM
MOBA_WIDTH = N_MOBA_HEADS * HEAD_DIM
MIX_WIDTH_2 = GDN_WIDTH + MOBA_WIDTH
IN_PROJ_WIDTH = 4 * GDN_WIDTH + 2 * N_GDN_HEADS + 3 * MOBA_WIDTH
GDN_CONV = 4
GDN_CHUNK = 64
MOBA_BLOCK = 256
MOBA_TOPK = 3
MOBA_Q_CHUNK = 64
REL_BUCKETS = 32
REL_MAX_DIST = 128
MEM_LEN = 256
N_XATTN_HEADS = 4
XATTN_WIDTH = N_XATTN_HEADS * HEAD_DIM
D_FF_2 = 5632
FFN_CONV = 3
NEG = -1e30


def rmsnorm_2(x, g):
    xf = x.astype(jnp.float32)
    y = xf * lax.rsqrt(jnp.mean(xf * xf, axis=-1, keepdims=True) + EPS)
    return (y * g.astype(jnp.float32)).astype(x.dtype)

def l2norm(x):
    xf = x.astype(jnp.float32)
    return (xf * lax.rsqrt(jnp.sum(xf * xf, axis=-1, keepdims=True) + EPS)).astype(x.dtype)

def causal_dwconv(x, w):
    K = w.shape[0]
    S = x.shape[1]
    xp = jnp.pad(x, ((0, 0), (K - 1, 0), (0, 0)))
    return sum(xp[:, j:j + S] * w[j] for j in range(K))

def rel_bucket(rel):
    n = jnp.maximum(-rel, 0)
    max_exact = REL_BUCKETS // 2
    nf = jnp.maximum(n, 1).astype(jnp.float32)
    large = max_exact + (jnp.log(nf / max_exact) / math.log(REL_MAX_DIST / max_exact)
                         * (REL_BUCKETS - max_exact)).astype(jnp.int32)
    large = jnp.minimum(large, REL_BUCKETS - 1)
    return jnp.where(n < max_exact, n, large)

def gated_delta_rule(q, k, v, g, beta):
    out_dtype = v.dtype
    B, H, S, Dk = q.shape
    Dv = v.shape[-1]
    C = GDN_CHUNK
    N = S // C
    f32 = jnp.float32
    q = (q.astype(f32) * Dk ** -0.5).reshape(B, H, N, C, Dk)
    k = k.astype(f32).reshape(B, H, N, C, Dk)
    v = v.astype(f32).reshape(B, H, N, C, Dv)
    g = g.astype(f32).reshape(B, H, N, C)
    beta = beta.astype(f32).reshape(B, H, N, C)
    G = jnp.cumsum(g, axis=-1)
    tri_incl = jnp.tril(jnp.ones((C, C), dtype=bool))
    tri_strict = jnp.tril(jnp.ones((C, C), dtype=bool), -1)
    decay = jnp.exp(jnp.where(tri_incl, G[..., :, None] - G[..., None, :], NEG))
    kb = k * beta[..., None]
    A = jnp.where(tri_strict, jnp.einsum('bhnid,bhnjd->bhnij', kb, k) * decay, 0.0)
    eye = jnp.eye(C, dtype=f32)
    T = lax.linalg.triangular_solve(eye + A, jnp.broadcast_to(eye, A.shape),
                                    left_side=True, lower=True)
    u = jnp.einsum('bhnij,bhnjd->bhnid', T, v * beta[..., None])
    w = jnp.einsum('bhnij,bhnjd->bhnid', T, kb * jnp.exp(G)[..., None])
    qk = jnp.einsum('bhnid,bhnjd->bhnij', q, k) * decay
    q_dec = q * jnp.exp(G)[..., None]
    k_dec = k * jnp.exp(G[..., -1:] - G)[..., None]
    g_last = jnp.exp(G[..., -1])

    def step(state, xs):
        q_i, k_i, u_i, w_i, qk_i, gl_i = xs
        v_new = u_i - jnp.einsum('bhck,bhkv->bhcv', w_i, state)
        o_i = (jnp.einsum('bhck,bhkv->bhcv', q_i, state)
               + jnp.einsum('bhij,bhjv->bhiv', qk_i, v_new))
        state = state * gl_i[..., None, None] + jnp.einsum('bhck,bhcv->bhkv', k_i, v_new)
        return state, o_i

    xs = tuple(jnp.moveaxis(t, 2, 0) for t in (q_dec, k_dec, u, w, qk, g_last))
    state0 = jnp.zeros((B, H, Dk, Dv), f32)
    _, o = lax.scan(step, state0, xs)
    o = jnp.moveaxis(o, 0, 2).reshape(B, H, S, Dv)
    return o.astype(out_dtype)

def moba_attention(q, k, v, rel_bias):
    B, H, S, Dh = q.shape
    nb = -(-S // MOBA_BLOCK)
    s_pad = nb * MOBA_BLOCK
    pad = ((0, 0), (0, 0), (0, s_pad - S), (0, 0))
    k_blocks = jnp.pad(k, pad).reshape(B, H, nb, MOBA_BLOCK, Dh)
    v_blocks = jnp.pad(v, pad).reshape(B, H, nb, MOBA_BLOCK, Dh)
    k_mean = jnp.mean(k_blocks.astype(jnp.float32), axis=3).astype(k.dtype)
    n_sel = min(MOBA_TOPK, nb)
    scale = Dh ** -0.5
    n_chunks = S // MOBA_Q_CHUNK
    offs = jnp.arange(MOBA_BLOCK)
    rb_t = rel_bias.T
    head_idx = jnp.arange(H)[:, None, None, None]

    def per_batch(args):
        qb, kb, vb, kmb = args

        def per_chunk(c):
            q0 = c * MOBA_Q_CHUNK
            qc = lax.dynamic_slice_in_dim(qb, q0, MOBA_Q_CHUNK, axis=1)
            q_pos = q0 + jnp.arange(MOBA_Q_CHUNK)
            own = q0 // MOBA_BLOCK
            gate = jnp.einsum('hqd,hnd->hqn', qc, kmb).astype(jnp.float32)
            gate = jnp.where(jnp.arange(nb) < own, gate, NEG)
            _, idx = lax.top_k(gate, n_sel)
            valid = jnp.arange(n_sel) < own
            k_sel = jax.vmap(lambda blk, ix: blk[ix])(kb, idx)
            v_sel = jax.vmap(lambda blk, ix: blk[ix])(vb, idx)
            pos_sel = idx[..., None] * MOBA_BLOCK + offs
            bias_sel = rb_t[head_idx, rel_bucket(pos_sel - q_pos[None, :, None, None])]
            logit_sel = (jnp.einsum('hqd,hqnkd->hqnk', qc, k_sel).astype(jnp.float32) * scale
                         + bias_sel.astype(jnp.float32))
            logit_sel = jnp.where(valid[None, None, :, None], logit_sel, NEG)
            k_own = lax.dynamic_index_in_dim(kb, own, axis=1, keepdims=False)
            v_own = lax.dynamic_index_in_dim(vb, own, axis=1, keepdims=False)
            pos_own = own * MOBA_BLOCK + offs
            rel_own = pos_own[None, :] - q_pos[:, None]
            logit_own = (jnp.einsum('hqd,hkd->hqk', qc, k_own).astype(jnp.float32) * scale
                         + rb_t[:, rel_bucket(rel_own)].astype(jnp.float32))
            logit_own = jnp.where((rel_own <= 0)[None], logit_own, NEG)
            logits = jnp.concatenate(
                [logit_sel.reshape(H, MOBA_Q_CHUNK, n_sel * MOBA_BLOCK), logit_own], axis=-1)
            p = jax.nn.softmax(logits, axis=-1).astype(v.dtype)
            p_sel = p[..., :n_sel * MOBA_BLOCK].reshape(H, MOBA_Q_CHUNK, n_sel, MOBA_BLOCK)
            p_own = p[..., n_sel * MOBA_BLOCK:]
            return (jnp.einsum('hqnk,hqnkd->hqd', p_sel, v_sel)
                    + jnp.einsum('hqk,hkd->hqd', p_own, v_own))

        o = lax.map(per_chunk, jnp.arange(n_chunks))
        return o.transpose(1, 0, 2, 3).reshape(H, S, Dh)

    return lax.map(per_batch, (q, k_blocks, v_blocks, k_mean))

def to_heads(t, n_heads):
    B, S, _ = t.shape
    return t.reshape(B, S, n_heads, HEAD_DIM).transpose(0, 2, 1, 3)

def hybrid_mixer(x, norm_g, w_in, gdn_conv_w, a_log, dt_bias, gdn_norm_g,
                 moba_norm_g, rel_bias, w_out):
    B, S, _ = x.shape
    h = rmsnorm_2(x, norm_g)
    proj = h @ w_in
    i0 = 3 * GDN_WIDTH
    i1 = i0 + GDN_WIDTH
    i2 = i1 + N_GDN_HEADS
    i3 = i2 + N_GDN_HEADS
    qkv_a, z_a, b_a, a_a, qkv_b = (proj[..., :i0], proj[..., i0:i1], proj[..., i1:i2],
                                   proj[..., i2:i3], proj[..., i3:])
    qkv_a = jax.nn.silu(causal_dwconv(qkv_a, gdn_conv_w))
    q_a, k_a, v_a = [to_heads(t, N_GDN_HEADS) for t in jnp.split(qkv_a, 3, axis=-1)]
    beta = jax.nn.sigmoid(b_a).transpose(0, 2, 1)
    g = (-jnp.exp(a_log) * jax.nn.softplus(a_a + dt_bias)).transpose(0, 2, 1)
    o_a = gated_delta_rule(l2norm(q_a), l2norm(k_a), v_a, g, beta).transpose(0, 2, 1, 3)
    o_a = rmsnorm_2(o_a, gdn_norm_g) * jax.nn.silu(z_a.reshape(B, S, N_GDN_HEADS, HEAD_DIM))
    q_b, k_b, v_b = [to_heads(t, N_MOBA_HEADS) for t in jnp.split(qkv_b, 3, axis=-1)]
    o_b = moba_attention(q_b, k_b, v_b, rel_bias).transpose(0, 2, 1, 3)
    o_b = rmsnorm_2(o_b, moba_norm_g)
    o = jnp.concatenate([o_a.reshape(B, S, GDN_WIDTH), o_b.reshape(B, S, MOBA_WIDTH)], axis=-1)
    return o @ w_out

def cross_attention(x, mem, norm_g, mem_norm_g, w_xq, w_xkv, w_xo):
    B, S, _ = x.shape
    M = mem.shape[1]
    q = (rmsnorm_2(x, norm_g) @ w_xq).reshape(B, S, N_XATTN_HEADS, HEAD_DIM)
    kv = rmsnorm_2(mem, mem_norm_g) @ w_xkv
    k, v = [t.reshape(B, M, N_XATTN_HEADS, HEAD_DIM) for t in jnp.split(kv, 2, axis=-1)]
    logits = jnp.einsum('bshd,bmhd->bhsm', q, k).astype(jnp.float32) * HEAD_DIM ** -0.5
    p = jax.nn.softmax(logits, axis=-1).astype(v.dtype)
    o = jnp.einsum('bhsm,bmhd->bshd', p, v).reshape(B, S, XATTN_WIDTH)
    return o @ w_xo

def conv_ffn(x, norm_g, w_gate, w_up, conv_w, conv_b, w_down):
    h = rmsnorm_2(x, norm_g)
    gate = causal_dwconv(h @ w_gate, conv_w) + conv_b
    return (jax.nn.silu(gate) * (h @ w_up)) @ w_down

def second_inputs(seed: int = 0) -> dict:
    key = jax.random.key(seed)
    ks = jax.random.split(key, 24)
    f32 = jnp.float32
    L = DEPTH

    def nrm(k, shape, scale):
        return jax.random.normal(k, shape, f32) * scale

    def gain(k, shape):
        return 1.0 + 0.02 * jax.random.normal(k, shape, f32)

    dt = jnp.exp(jax.random.uniform(ks[6], (L, N_GDN_HEADS), f32, math.log(1e-3), math.log(1e-1)))
    return {
        "x": nrm(ks[0], (BATCH, SEQ, D_MODEL), 1.0),
        "mem": nrm(ks[1], (BATCH, MEM_LEN, D_MODEL), 1.0),
        "mix_norm_g": gain(ks[2], (L, D_MODEL)),
        "w_in": nrm(ks[3], (L, D_MODEL, IN_PROJ_WIDTH), D_MODEL ** -0.5),
        "gdn_conv_w": nrm(ks[4], (L, GDN_CONV, 3 * GDN_WIDTH), GDN_CONV ** -0.5),
        "gdn_a_log": jnp.log(jax.random.uniform(ks[5], (L, N_GDN_HEADS), f32, 1.0, 16.0)),
        "gdn_dt_bias": dt + jnp.log(-jnp.expm1(-dt)),
        "gdn_norm_g": gain(ks[7], (L, HEAD_DIM)),
        "moba_norm_g": gain(ks[8], (L, HEAD_DIM)),
        "rel_bias": nrm(ks[9], (REL_BUCKETS, N_MOBA_HEADS), 0.5),
        "w_out": nrm(ks[10], (L, MIX_WIDTH_2, D_MODEL), MIX_WIDTH_2 ** -0.5),
        "xattn_norm_g": gain(ks[11], (L, D_MODEL)),
        "mem_norm_g": gain(ks[12], (L, D_MODEL)),
        "w_xq": nrm(ks[13], (L, D_MODEL, XATTN_WIDTH), D_MODEL ** -0.5),
        "w_xkv": nrm(ks[14], (L, D_MODEL, 2 * XATTN_WIDTH), D_MODEL ** -0.5),
        "w_xo": nrm(ks[15], (L, XATTN_WIDTH, D_MODEL), XATTN_WIDTH ** -0.5),
        "ffn_norm_g": gain(ks[16], (L, D_MODEL)),
        "w_gate": nrm(ks[17], (L, D_MODEL, D_FF_2), D_MODEL ** -0.5),
        "w_up": nrm(ks[18], (L, D_MODEL, D_FF_2), D_MODEL ** -0.5),
        "ffn_conv_w": nrm(ks[19], (L, FFN_CONV, D_FF_2), FFN_CONV ** -0.5),
        "ffn_conv_b": nrm(ks[20], (L, D_FF_2), 0.02),
        "w_down": nrm(ks[21], (L, D_FF_2, D_MODEL), D_FF_2 ** -0.5),
        "final_norm_g": gain(ks[22], (D_MODEL,)),
    }

def second_block(x, mem, mix_norm_g, w_in, gdn_conv_w, gdn_a_log, gdn_dt_bias, gdn_norm_g,
              moba_norm_g, rel_bias, w_out, xattn_norm_g, mem_norm_g, w_xq, w_xkv, w_xo,
              ffn_norm_g, w_gate, w_up, ffn_conv_w, ffn_conv_b, w_down, final_norm_g):
    for l in range(DEPTH):
        x = x + hybrid_mixer(x, mix_norm_g[l], w_in[l], gdn_conv_w[l], gdn_a_log[l],
                             gdn_dt_bias[l], gdn_norm_g[l], moba_norm_g[l], rel_bias, w_out[l])
        x = x + cross_attention(x, mem, xattn_norm_g[l], mem_norm_g[l], w_xq[l], w_xkv[l], w_xo[l])
        x = x + conv_ffn(x, ffn_norm_g[l], w_gate[l], w_up[l], ffn_conv_w[l], ffn_conv_b[l], w_down[l])
    return rmsnorm_2(x, final_norm_g)


def setup_inputs(seed=0):
    out = dict(first_inputs(seed))
    for name, value in second_inputs(seed + 1).items():
        if name != "x":
            out[name + "_2"] = value
    return out


def reference(
    x, positions, pre_mix_norm, w_in, q_norm, w_uq, kv_norm, w_ukv, conv_w, conv_b, conv_ln_g,
    conv_ln_b, conv_out_norm, attn_out_norm, w_out, post_mix_norm, pre_ffn_norm, w_gate, w_up,
    w_down, post_ffn_norm, mem_2, mix_norm_g_2, w_in_2, gdn_conv_w_2, gdn_a_log_2,
    gdn_dt_bias_2, gdn_norm_g_2, moba_norm_g_2, rel_bias_2, w_out_2, xattn_norm_g_2,
    mem_norm_g_2, w_xq_2, w_xkv_2, w_xo_2, ffn_norm_g_2, w_gate_2, w_up_2, ffn_conv_w_2,
    ffn_conv_b_2, w_down_2, final_norm_g_2,
):
    x = first_block(
        x, positions, pre_mix_norm, w_in, q_norm, w_uq, kv_norm, w_ukv, conv_w, conv_b,
        conv_ln_g, conv_ln_b, conv_out_norm, attn_out_norm, w_out, post_mix_norm, pre_ffn_norm,
        w_gate, w_up, w_down, post_ffn_norm,
    )
    return second_block(
        x, mem_2, mix_norm_g_2, w_in_2, gdn_conv_w_2, gdn_a_log_2, gdn_dt_bias_2, gdn_norm_g_2,
        moba_norm_g_2, rel_bias_2, w_out_2, xattn_norm_g_2, mem_norm_g_2, w_xq_2, w_xkv_2,
        w_xo_2, ffn_norm_g_2, w_gate_2, w_up_2, ffn_conv_w_2, ffn_conv_b_2, w_down_2,
        final_norm_g_2,
    )


_drawn_inputs = setup_inputs


def setup_inputs(seed=0):
    import zlib

    import numpy as np

    out = dict(_drawn_inputs(seed))
    spreads = {}
    factors = {'conv_ln_b': 3.629,
     'mix_norm_g_2': 4.787,
     'gdn_norm_g_2': 8.0,
     'moba_norm_g_2': 23.018,
     'xattn_norm_g_2': 8.0,
     'mem_norm_g_2': 8.0,
     'ffn_norm_g_2': 6.32,
     'ffn_conv_b_2': 22.25,
     'final_norm_g_2': 8.026}
    for name, (base, spread) in spreads.items():
        noise = np.random.default_rng([zlib.crc32(name.encode()), seed]).standard_normal(out[name].shape)
        drawn = base * np.exp(spread * noise) if base else spread * noise
        out[name] = __import__('jax').numpy.asarray(drawn.astype(out[name].dtype))
    for name, factor in factors.items():
        out[name] = (out[name] * factor).astype(out[name].dtype)
    return out
```

```python
import math
from contextlib import ExitStack

import numpy as np
import concourse.bass as bass
from concourse import mybir

F32 = mybir.dt.float32
F32R = mybir.dt.float32r
I32 = mybir.dt.int32
ACT = mybir.ActivationFunctionType
ALU = mybir.AluOpType
AX = mybir.AxisListType

P = 128
T = 256
TT = T // P
D = 2048
DC = D // P
EPS = 1e-6
H = 8
XH = 4
FF = 5632
FC = FF // P
CONV_K = 31
CC = 8
GDN_K = 4
FFN_K = 3
BUCKETS = 32
MAX_DIST = 128
NEG = -1e30
W = 512
KC = 4
RAW = 4
HALF = 2
HIS = 4
KB = 1024


COLUMNS = {}
_at = 0
for _name, _n in [("pre_mix", 16), ("q_norm", 6), ("kv_norm", 4), ("conv_b", 8), ("conv_ln_g", 8),
                  ("conv_ln_b", 8), ("conv_out", 8), ("attn_out", 8), ("post_mix", 16), ("pre_ffn", 16),
                  ("post_ffn", 16), ("mix2", 16), ("gdn_norm", 1), ("moba_norm", 1), ("xattn", 16),
                  ("mem", 16), ("ffn2", 16), ("ffn_conv_b", 44), ("final", 16), ("conv_w", 8 * CONV_K),
                  ("gdn_conv", 24 * GDN_K), ("ffn_conv", 44 * FFN_K), ("a_log", 1), ("dt_bias", 1),
                  ("eps", 1), ("inv_freq", 1)]:
    COLUMNS[_name] = (_at, _n)
    _at += _n
NCOL = _at


def constants():
    c = {}
    c["ident"] = np.eye(P, dtype=np.float32)
    j, i = np.arange(P)[:, None], np.arange(P)[None, :]
    lv = [((j >> (l + 1)) == (i >> (l + 1))) & (((i >> l) & 1) == 1) & (((j >> l) & 1) == 0) for l in range(7)]
    c["masks"] = np.stack([m.astype(np.float32) for m in lv] + [(i >= j).astype(np.float32)], 1)
    rot = np.zeros((P, P), np.float32)
    dup = np.zeros((P, P), np.float32)
    for b in (0, 64):
        for k in range(32):
            rot[b + 32 + k, b + k] = -1.0
            rot[b + k, b + 32 + k] = 1.0
        for k in range(64):
            dup[64 + k, b + k] = 1.0
    c["rope_m"] = np.stack([rot, dup, dup @ rot], 1)
    q = np.arange(P)[:, None]
    c["causal"] = np.concatenate([np.where(np.arange(P)[None] <= q, 0.0, NEG),
                                  np.where(np.arange(T)[None] <= q + P, 0.0, NEG)], 1).astype(np.float32)
    n = np.arange(T)
    f32 = np.float32
    nf = np.maximum(n, 1).astype(f32)
    large = 16 + (np.log(nf / f32(16)) / f32(math.log(MAX_DIST / 16)) * f32(16)).astype(np.int32)
    bucket = np.where(n < 16, n, np.minimum(large, BUCKETS - 1))
    hot = np.zeros((BUCKETS, 384), np.float32)
    for e in range(T):
        hot[bucket[255 - e], e] = 1.0
    c["hot"] = hot
    neg = np.zeros((H, 384), np.float32)
    neg[:, T:] = NEG
    c["hot_neg"] = neg
    return c


class Gemm:

    def __init__(self, name, turns, groups, x, scale=None):
        self.name, self.turns, self.groups, self.x, self.scale = name, turns, groups, x, scale
        self.tiles = sum(g["tiles"] for g in groups)
        self.banks = sum(len(g["at"]) for g in groups)


class Milestones:

    def __init__(self, sem, names):
        self.sem, self.names, self.n = sem, names, 0

    def reach(self, ins, name):
        assert self.names[self.n] == name, (self.names[self.n], name)
        self.n += 1
        ins.then_inc(self.sem, 1)

    def wait(self, eng, name):
        eng.wait_ge(self.sem, self.names.index(name) + 1)


class Chain:

    def __init__(self, sem):
        self.sem, self.n = sem, 0

    def step(self, ins):
        self.n += 1
        ins.then_inc(self.sem, 1)

    def sync(self, eng):
        eng.wait_ge(self.sem, self.n)

    def link(self, eng, ins):
        self.step(ins)
        self.sync(eng)


def build(nc, A, out):
    with ExitStack() as ctx:
        sem_cache = {}

        def sem(name):
            if name not in sem_cache:
                sem_cache[name] = ctx.enter_context(nc.semaphore(name))
            return sem_cache[name]

        base = (nc.sbuf_base + 31) // 32 * 32
        place = {}

        def sb(name, shape, dt=F32, at=None):
            return nc.alloc_sbuf_tensor_at(name, shape, dt, offset=at)

        top = [base]

        def room(nbytes):
            a = top[0]
            top[0] += (nbytes + 31) // 32 * 32
            assert top[0] <= nc.sbuf_usable_end, (top[0], nc.sbuf_usable_end)
            return a

        xt = sb("xt", [P, DC, T], F32, room(16 * KB))
        a_x2 = room(32 * KB)
        x2 = sb("x2", [P, DC, 2, T], F32R, a_x2)
        tx = sb("tx", [P, 32, T], F32, a_x2)
        a_raw = room(RAW * 8 * KB)
        w_raw = sb("w_raw", [P, RAW, KC, W], F32, a_raw)
        w_lo = sb("w_lo", [P, RAW, KC, W], F32R, a_raw)
        w_hi = sb("w_hi", [P, HIS, HALF, W], F32R, room(HIS * 4 * KB))
        a_ar = room(88 * KB)
        h2 = sb("h2", [P, FC, 2, T], F32R, a_ar)
        ar = sb("ar", [P, 88, T], F32, a_ar)
        cols = sb("cols", [P, NCOL], F32, room(4 * NCOL))
        ident = sb("ident_s", [P, P], F32, room(4 * P))
        ones = sb("ones", [P, P], F32, room(4 * P))
        half = sb("half", [P, 4, T], F32, room(4 * KB))
        gate = sb("gate", [P, 4, T], F32, room(4 * KB))
        up = sb("up", [P, 4, T], F32, room(4 * KB))
        rs_x = sb("rs_x", [P, T], F32, room(KB))
        ssq = sb("ssq", [P, 4, T], F32, room(4 * KB))
        st_y = sb("st_y", [P, T], F32, room(KB))
        st_v = sb("st_v", [P, T], F32, room(KB))
        small = sb("small", [P, 2, 64], F32, room(512))

        def col(name, k=0, n=1, rows=P):
            b, size = COLUMNS[name]
            return cols[0:rows, b + k:b + k + n]

        ps = ctx.enter_context(nc.psum_tensor("ps", [P, 8, W], F32))

        eps_c = col("eps")

        M1 = 0
        MEM = 57
        Z1 = 0
        U1, Q1, K1, V1, VN1, O1 = 27, 36, 48, 56, 64, 72
        KPE, COS, SIN = 80, 81, 82
        causal = sb("causal_s", [P, 384], F32, a_ar + 83 * KB)
        rope_m = sb("rope_s", [P, 3, P], F32, a_ar + 85 * KB)
        rs_kv = ar[:, 87, :]
        pos_i = sb("pos_i", [P, T], I32, a_ar + 72 * KB)
        ZA, ZZ, BA, ZB = 0, 24, 32, 33
        VN2, BI, O2B = 57, 65, 77
        bias2 = sb("bias2", [P, H, 384], F32, a_ar + BI * KB)
        RQK, RBETA, RG = 85, 86, 87
        KBG1, KDEC0, VB, AT, QK, UU, QDEC1, OG = 33, 37, 41, 49, 57, 65, 73, 41
        XK, XV, XVN, XQ, XO = 0, 4, 8, 12, 16
        XM = 20

        rel_hot = sb("rel_hot", [BUCKETS, 384], F32, a_x2 + 8 * KB)
        rel_neg = sb("rel_neg", [H, 384], F32, a_x2 + 10 * KB)
        rel_b = sb("rel_b", [BUCKETS, H], F32, a_x2 + 12 * KB)
        rel_e = sb("rel_e", [H, 384], F32, a_x2 + 13 * KB)
        masks = sb("masks_s", [P, 8, P], F32, a_x2 + 24 * KB)
        rel_d = nc.dram_tensor("rel_d", [H, 384], F32, kind="Internal").ap()
        rel_s = nc.dram_tensor("rel_s", [H, P, 384], F32, kind="Internal").ap()

        def w_cols(w, at, width):
            v = w.rearrange("(c p) n -> p c n", p=P)
            return lambda i, k0, kn: [(slice(0, kn), slice(0, width), v[:, k0:k0 + kn, at:at + width])]

        def w_loop(w, at, step=W):
            v = w.rearrange("(c p) n -> p c n", p=P)
            return lambda i, k0, kn: [(slice(0, kn), slice(0, W), v[:, k0:k0 + kn, bass.ds(i * step + at, W)])]

        def w_heads(w, per, h0, n, off, width):
            v = w.rearrange("(c p) (h d) -> p c h d", p=P, d=per)
            return lambda i, k0, kn: [
                (k, slice(0, n * width), v[:, k0 + k, h0:h0 + n, off:off + width]) for k in range(kn)]

        FULL = [0, 128, 256, 384]

        def group(src, tiles, kc=KC, at=FULL, banks=0, out=None, kind="z", parts=1):
            return dict(src=src, tiles=tiles, kc=kc, at=at, banks=banks, out=out, kind=kind, parts=parts)

        def group_of(g, j):
            for gr in g.groups:
                if gr["t"] <= j < gr["t"] + gr["tiles"]:
                    return gr, j - gr["t"]

        def gr_parts(g, j):
            return group_of(g, j)[0]["parts"]

        def x2c(k):
            return x2[:, k], x2[:, k, 0, :]

        def h2c(k):
            return h2[:, k], h2[:, k, 0, :]

        GEMMS = [
            Gemm("conv_in", 1, [group(w_cols(A["w_in"], c, W), 4, banks=b, out=(ar, Z1 + c // P, 0))
                                for b, c in ((0, 0), (4, 1024), (0, 512), (4, 1536))], x2c, rs_x),
            Gemm("latents", 1, [group(w_cols(A["w_in"], 2048, W), 4, out=(ar, Z1 + 16, 0)),
                                group(w_cols(A["w_in"], 2560, W), 4, banks=4, out=(ar, Z1 + 20, 0)),
                                group(w_cols(A["w_in"], 3072, 320), 4, at=[0, 128, 192], out=(ar, Z1 + 24, 0))],
                 x2c, rs_x),
            Gemm("uq", 1, [group(w_heads(A["w_uq"], 192, 0, 4, 0, 128), 2, 3, out=(ar, Q1, 0), parts=3),
                           group(w_heads(A["w_uq"], 192, 4, 4, 0, 128), 2, 3, banks=4, out=(ar, Q1 + 4, 0), parts=3),
                           group(w_heads(A["w_uq"], 192, 0, 8, 128, 64), 2, 3, out=(ar, Q1 + 8, 0), parts=3)], x2c, rs_x),
            Gemm("ukv", 1, [group(w_heads(A["w_ukv"], 256, 0, 4, 0, 128), 1, out=(ar, K1, 0), parts=4),
                            group(w_heads(A["w_ukv"], 256, 4, 4, 0, 128), 1, banks=4, out=(ar, K1 + 4, 0), parts=4),
                            group(w_heads(A["w_ukv"], 256, 0, 4, 128, 128), 1, out=(ar, V1, 0), parts=4),
                            group(w_heads(A["w_ukv"], 256, 4, 4, 128, 128), 1, banks=4, out=(ar, V1 + 4, 0), parts=4)],
                 lambda k: x2c(6 + k), rs_kv),
            Gemm("w_out", 2, [group(w_loop(A["w_out"], 0 + b * P, 2 * W), 4, banks=b, out=(ar, M1 + b, 8), kind="sum")
                        for b in (0, 4)], x2c),
            Gemm("ffn", 11, [group(w_loop(A["w_gate"], 0), 4, kind="gate"),
                             group(w_loop(A["w_up"], 0), 4, banks=4, kind="up")], x2c, rs_x),
            Gemm("down", 2, [group(w_loop(A["w_down"], 0, 1024), 11, out=(tx, 16, 8), kind="sum"),
                             group(w_loop(A["w_down"], 512, 1024), 11, banks=4, out=(tx, 20, 8), kind="sum")], h2c),
            Gemm("qkv_a", 3, [group(w_loop(A["w_in_2"], 0 + b * P, 2 * W), 4, banks=b, out=(ar, ZA + b, 8))
                        for b in (0, 4)], x2c, rs_x),
            Gemm("z_ba", 1, [group(w_cols(A["w_in_2"], 3072, W), 4, out=(ar, ZZ, 0)),
                             group(w_cols(A["w_in_2"], 3584, W), 4, banks=4, out=(ar, ZZ + 4, 0)),
                             group(w_cols(A["w_in_2"], 4096, 128), 4, at=[0], out=(ar, BA, 0))], x2c, rs_x),
            Gemm("qkv_b", 3, [group(w_loop(A["w_in_2"], 4112 + b * P, 2 * W), 4, banks=b, out=(ar, ZB + b, 8))
                        for b in (0, 4)], x2c, rs_x),
            Gemm("w_out_2", 2, [group(w_loop(A["w_out_2"], 0 + b * P, 2 * W), 4, banks=b, out=(xt, 0 + b, 8), kind="add")
                        for b in (0, 4)], x2c),
            Gemm("xkv", 1, [group(w_cols(A["w_xkv_2"], b * P, W), 4, banks=b, out=(ar, XK + b, 0)) for b in (0, 4)], x2c, rs_x),
            Gemm("xq", 1, [group(w_cols(A["w_xq_2"], 0, W), 4, out=(ar, XQ, 0))], x2c, rs_x),
            Gemm("xo", 1, [group(w_cols(A["w_xo_2"], 512 * n, W), 1, banks=4 * (n % 2), out=(xt, 4 * n, 0), kind="add")
                           for n in range(4)], x2c),
            Gemm("ffn_2", 11, [group(w_loop(A["w_gate_2"], 0), 4, kind="gate2"),
                               group(w_loop(A["w_up_2"], 0), 4, banks=4, kind="up")], x2c, rs_x),
            Gemm("down_2", 2, [group(w_loop(A["w_down_2"], 0, 1024), 11, out=(xt, 0, 8), kind="add"),
                               group(w_loop(A["w_down_2"], 512, 1024), 11, banks=4, out=(xt, 4, 8), kind="add")], h2c),
        ]
        G = {g.name: g for g in GEMMS}
        tiles = prods = banks = groups = hidden = 0
        slots = [0] * RAW
        for n, g in enumerate(GEMMS):
            g.before = GEMMS[n - 1] if n else None
            g.u0, g.p0, g.e0, g.g0, g.f0, g.slot0 = tiles, prods, banks, groups, hidden, list(slots)
            at = bank = 0
            g.per_unit = []
            for k, gr in enumerate(g.groups):
                gr["t"], gr["e"], gr["n"] = at, bank, k
                at += gr["tiles"]
                bank += len(gr["at"])
                g.per_unit += [len(gr["at"])] * (2 * gr["tiles"])
            g.units = 2 * g.tiles
            g.products = sum(g.per_unit)
            g.slot_per = [sum(gr_parts(g, j) for j in range(g.tiles) if j % RAW == s) for s in range(RAW)]
            slots = [a + g.turns * b for a, b in zip(slots, g.slot_per)]
            tiles += g.turns * 2 * g.tiles
            prods += g.turns * g.products
            banks += g.turns * g.banks
            groups += g.turns * len([gr for gr in g.groups if gr["kind"] in ("z", "gate2")])
            hidden += g.turns if g.name.startswith("ffn") else 0

        w_loaded = [sem(f"w_loaded{s}") for s in range(RAW)]
        hi_done = sem("hi_done")
        lo_done = sem("lo_done")
        products = sem("products")
        half_out = sem("half_out")
        bank_free = sem("bank_free")
        group_out = sem("group_out")
        gate_act = sem("gate_act")
        hid_hi = sem("hid_hi")
        hid_pre = sem("hid_pre")
        hid_lo = sem("hid_lo")
        add_half = sem("add_half")
        tap_done = sem("tap_done")
        AHEAD_P, AHEAD_B = 2 * RAW * 4, 8

        def landed(g, i, j):
            s = j % RAW
            n = sum(gr_parts(g, k) for k in range(j + 1) if k % RAW == s)
            return 16 * (g.slot0[s] + n) + i * (16 * g.slot_per[s])

        def used(g, i, u, lag):
            own = g.per_unit[:u]
            if lag <= u:
                back = sum(own[u - lag + 1:])
            else:
                tails = ([g.per_unit] if g.turns > 1 or not g.before else []) + ([g.before.per_unit] if g.before else [])
                back = min(sum((t + own)[len(t) + u - lag + 1:]) for t in tails)
            return AHEAD_P + g.p0 + sum(own) - back + i * g.products

        def slot_lag(g, j):
            if j >= RAW:
                return RAW
            ns = [g.tiles] + ([g.before.tiles] if g.before else [])
            return min(n - max(k for k in range(n) if k % RAW == j) + j for n in ns)

        def load(sp, g):
            def body(i):
                for j in range(g.tiles):
                    gr, jj = group_of(g, j)
                    sp.wait_ge(products, used(g, i, 2 * j, 2 * slot_lag(g, j) - 1))
                    for ks, cs, src in gr["src"](i, jj * gr["kc"], gr["kc"]):
                        sp.dma_start(w_raw[:, j % RAW, ks, cs], src).then_inc(w_loaded[j % RAW], 16)
            if g.turns == 1:
                body(0)
            else:
                with sp.Fori(0, g.turns) as i:
                    body(i)

        def unit(g, u):
            gr, _ = group_of(g, u // 2)
            return gr, u // 2, slice(HALF * (u % 2), HALF if u % 2 == 0 else gr["kc"]), slice(0, gr["at"][-1] + P)

        def split_act(act, g, i, u):
            _, j, ks, cs = unit(g, u)
            if u % 2 == 0:
                act.wait_ge(w_loaded[j % RAW], landed(g, i, j))
            act.wait_ge(products, used(g, i, u, HIS))
            nc.scalar.activation(w_hi[:, u % HIS, 0:ks.stop - ks.start, cs], w_raw[:, j % RAW, ks, cs], ACT.Copy)\
                .then_inc(hi_done, 1)

        def split_dve(dve, g, i, u):
            _, j, ks, cs = unit(g, u)
            dve.wait_ge(hi_done, g.u0 + u + 1 + i * g.units)
            nc.vector.tensor_tensor(w_lo[:, j % RAW, ks, cs], w_raw[:, j % RAW, ks, cs],
                                    w_hi[:, u % HIS, 0:ks.stop - ks.start, cs].bitcast(F32), ALU.subtract)\
                .then_inc(lo_done, 1)

        def evict_act(act, g, i, gr):
            e = g.e0 + gr["e"] + i * g.banks
            M = len(gr["at"])
            act.wait_ge(bank_free, AHEAD_B + e)
            last = AHEAD_P + g.p0 + sum(g.per_unit[:2 * (gr["t"] + gr["tiles"]) - 1]) + i * g.products
            for m in range(M):
                act.wait_ge(products, last + m + 1)
                nc.scalar.activation(half[:, m, :], ps[:, gr["banks"] + m, 0:T], ACT.Copy).then_inc(half_out, 1)
            f = g.f0 + i
            yield
            if gr["kind"] == "gate":
                yield
                act.wait_ge(hid_pre, 3 * f + 1)
                nc.scalar.activation(gate[:], gate[:], ACT.Silu).then_inc(gate_act, 1)
            if gr["kind"] == "gate2":
                for _ in range(3):
                    yield
                act.wait_ge(hid_pre, 3 * f + 1)
                for m in range(4):
                    nc.scalar.activation(gate[:, m, :], conv_y[:, m, :], ACT.Silu,
                                         bias=cols[:, bass.ds(i * 4 + (COLUMNS["ffn_conv_b"][0] + m), 1)])\
                        .then_inc(gate_act, 1)
            if gr["kind"] == "up":
                yield
                yield
                act.wait_ge(hid_pre, 3 * f + 3)
                nc.scalar.activation(h2[:, bass.ds(i * 4, 4), 0, :] if not isinstance(i, int) else h2[:, 4 * i:4 * i + 4, 0, :], up[:], ACT.Copy).then_inc(hid_hi, 1)

        def evict_dve(dve, g, i, gr):
            e = g.e0 + gr["e"] + i * g.banks
            M = len(gr["at"])
            f = g.f0 + i
            kind = gr["kind"]
            if kind == "add":
                _, base_c, step = gr["out"]
                xc = lambda m: chunk(xt, base_c + m, step, i)
                for m in range(M):
                    dve.wait_ge(half_out, e + m + 1)
                    nc.vector.tensor_tensor(xc(m), xc(m), ps[:, gr["banks"] + m, T:2 * T], ALU.add)\
                        .then_inc(add_half, 1)
                a0 = g.a0 + gr["e"] + i * g.banks
                for m in range(M):
                    dve.wait_ge(add_half, a0 + m + 1)
                    nc.vector.tensor_tensor(xc(m), xc(m), half[:, m, :], ALU.add).then_inc(bank_free, 1)
                return
            if kind in ("gate", "gate2"):
                dve.wait_ge(hid_hi, f)
                dst, whole = (lambda m: gate[:, m, :]), gate[:]
            elif kind == "up":
                dst, whole = (lambda m: up[:, m, :]), up[:]
            else:
                where, base_c, step = gr["out"]
                dst = lambda m: chunk(where, base_c + m, step, i)
                whole = chunk(where, base_c, step, i, M)
            for m in range(M):
                dve.wait_ge(half_out, e + m + 1)
                nc.vector.tensor_tensor(dst(m), half[:, m, :], ps[:, gr["banks"] + m, T:2 * T], ALU.add)\
                    .then_inc(bank_free, 1)
            if kind == "sum":
                return
            yield
            dve.wait_ge(bank_free, AHEAD_B + e + M)
            if kind == "z":
                nc.vector.tensor_tensor(whole, whole, bc(g.scale, M), ALU.mult)\
                    .then_inc(group_out, 1)
            elif kind == "gate":
                nc.vector.tensor_tensor(gate[:], gate[:], bc(rs_x, 4), ALU.mult).then_inc(hid_pre, 1)
            elif kind == "gate2":
                nc.vector.tensor_tensor(gate[:], gate[:], bc(rs_x, 4), ALU.mult).then_inc(group_out, 1)
                dve.wait_ge(group_out, g.g0 + 1 + i)
                first_w = COLUMNS["ffn_conv"][0]
                for s in range(FFN_K):
                    for m in range(4):
                        w = cols[:, bass.ds(i * (4 * FFN_K) + (first_w + m * FFN_K + FFN_K - 1 - s), 1)]
                        if s == 0:
                            nc.vector.tensor_scalar(conv_y[:, m, :], gate[:, m, :], w, None, ALU.mult)\
                                .then_inc(tap_done, 1)
                        elif s < FFN_K - 1 or m < 3:
                            nc.vector.scalar_tensor_tensor(
                                conv_y[:, m, s:T], gate[:, m, 0:T - s], w, conv_y[:, m, s:T], ALU.mult, ALU.add)\
                                .then_inc(tap_done, 1)
                        else:
                            dve.wait_ge(tap_done, 4 * FFN_K - 1 + i * (4 * FFN_K - 1))
                            nc.vector.scalar_tensor_tensor(
                                conv_y[:, m, s:T], gate[:, m, 0:T - s], w, conv_y[:, m, s:T], ALU.mult, ALU.add)\
                                .then_inc(hid_pre, 1)
                    if s < FFN_K - 1:
                        yield
                        dve.wait_ge(tap_done, 4 * (s + 1) + i * (4 * FFN_K - 1))
            elif kind == "up":
                nc.vector.tensor_tensor(up[:], up[:], bc(rs_x, 4), ALU.mult).then_inc(hid_pre, 1)
                yield
                dve.wait_ge(hid_pre, 3 * f + 2)
                dve.wait_ge(gate_act, f + 1 if g.name == "ffn" else g.f0 + 4 * i + 4)
                nc.vector.tensor_tensor(up[:], up[:], gate[:], ALU.mult).then_inc(hid_pre, 1)
                yield
                yield
                dve.wait_ge(hid_hi, f + 1)
                for m in range(4):
                    nc.vector.tensor_tensor(chunk(h2[:, :, 1, :], m, 4, i), up[:, m, :],
                                            chunk(h2[:, :, 0, :], m, 4, i).bitcast(F32),
                                            ALU.subtract).then_inc(hid_lo, 1)

        def chunk(where, first, step, i, n=None):
            if isinstance(i, int):
                c = first + i * step
                return where[:, c, :] if n is None else where[:, c:c + n, :]
            c = bass.ds(i * step + first, n or 1)
            return where[:, c, :].rearrange("p a n -> p (a n)") if n is None else where[:, c, :]


        def bc(v, n):
            return (v if isinstance(v, bass.AP) else v[:]).unsqueeze(1).to_broadcast([P, n, T]) if n > 1 else (v if isinstance(v, bass.AP) else v[:]).unsqueeze(1)

        FIRST = 3

        def finish(steps):
            for _ in steps:
                pass

        def ahead(eng, split, evict, g):
            for u in range(FIRST):
                split(eng, g, 0, u)
            if g.before:
                finish(evict(eng, g.before, g.before.turns - 1, g.before.groups[-1]))
            split(eng, g, 0, FIRST)

        def turn(eng, split, evict, g, i, steps=None, first=0, filler=None, fill_from=0, at=None):
            for k, gr in enumerate(g.groups):
                if k:
                    steps = evict(eng, g, i, g.groups[k - 1])
                for n in range(2 * gr["tiles"]):
                    u = 2 * gr["t"] + n
                    if u < first:
                        continue
                    split(eng, g, i, u)
                    if n >= FIRST - 1 and steps:
                        next(steps, None)
                    if filler and k >= fill_from:
                        next(filler, None)
                    if at and at[0] == u:
                        at[1]()
                if steps:
                    finish(steps)
                steps = None

        def run(eng, split, evict, g, filler=None, fill_from=0, at=None):
            turn(eng, split, evict, g, 0, None, FIRST + 1, filler, fill_from, at)
            if g.turns > 1:
                with eng.Fori(1, g.turns) as i:
                    turn(eng, split, evict, g, i, evict(eng, g, i - 1, g.groups[-1]))

        def multiply(pe, g, stat=None):
            before = g.before.groups[-1] if g.before else None
            kept = len(before["at"]) if before and before["banks"] != g.groups[0]["banks"] else 0
            assert kept in (0, 4)
            pe.wait_ge(bank_free, AHEAD_B + g.e0 - kept)

            def body(i, first=0, last=g.units):
                for u in range(first, last):
                    gr, j, ks, _ = unit(g, u)
                    n, jj = u - 2 * gr["t"], j - gr["t"]
                    final = n == 2 * gr["tiles"] - 1
                    pe.wait_ge(lo_done, g.u0 + u + 1 + i * g.units)
                    pe.wait_ge(*g.needs(jj * gr["kc"] + ks.stop))
                    if stat and isinstance(i, int) and gr["banks"] == 4 and n == 0:
                        pe.wait_ge(st_done, STATS[stat][0] + 1)
                    for m, c0 in enumerate(gr["at"]):
                        if n == 0 and (g.turns > 1 or gr["n"] or kept):
                            lag = bank_lag(g, gr, kept)
                            if lag is not None:
                                pe.wait_ge(bank_free, AHEAD_B + g.e0 + gr["e"] + m + 1 - lag + i * g.banks)
                        bank = ps[:, gr["banks"] + m, :]
                        for k in range(ks.start, ks.stop):
                            both, hi = g.x(jj * gr["kc"] + k)
                            nc.tensor.matmul(bank, w_hi[:, u % HIS, k - ks.start, c0:c0 + P],
                                             both.rearrange("p a n -> p (a n)"),
                                             start=(n == 0 and k == 0), stop=False)
                            ins = nc.tensor.matmul(bank[:, T:2 * T], w_lo[:, j % RAW, k, c0:c0 + P], hi,
                                                   start=False, stop=(final and k == ks.stop - 1))
                        ins.then_inc(products, 1)

            if stat:
                body(0, 0, FIRST + 1)
                sum_pe(pe, stat)
                body(0, FIRST + 1)
                if g.turns > 1:
                    with pe.Fori(1, g.turns) as i:
                        body(i)
            elif g.turns == 1:
                body(0)
            else:
                with pe.Fori(0, g.turns) as i:
                    body(i)

        def bank_lag(g, gr, kept):
            order = ([x for x in g.groups] if g.turns > 1 else []) + g.groups[:gr["n"]]
            lag = 0
            for x in reversed(order):
                lag += len(x["at"])
                if x["banks"] == gr["banks"]:
                    return lag
            return lag + kept if kept and gr["banks"] != g.groups[0]["banks"] else None

        STATS = {}
        for name, parts in [("x", 4), ("q", 2), ("kv", 1), ("mean", 2), ("ln", 2), ("conv", 2), ("attn", 2),
                            ("mix", 4), ("ffn", 4), ("ff", 4), ("mix2", 4), ("mem", 4), ("xq", 4),
                            ("ffn2", 4), ("final", 4)]:
            before = list(STATS.values())
            STATS[name] = (len(before), sum(p for _, _, p in before), parts)
        PREPS = {}
        for name, n, first in [("x", 16, 0), ("q", 6, 0), ("kv", 4, 6), ("conv", 8, 0), ("attn", 8, 8),
                               ("ffn", 16, 0), ("mix2", 16, 0), ("gdn", 8, 0), ("moba", 8, 8), ("mem", 16, 0),
                               ("xq", 16, 0), ("xo", 4, 0), ("ffn2", 16, 0)]:
            PREPS[name] = (sum(c for _, c, _ in PREPS.values()), n, first)

        x_hi, x_lo = sem("x_hi"), sem("x_lo")
        squares = sem("squares")
        summed = sem("summed")
        st_sum = sem("st_sum")
        st_var = sem("st_var")
        st_root = sem("st_root")
        st_done = sem("st_done")
        xt_loaded, cols_loaded, aux_loaded = sem("xt_loaded"), sem("cols_loaded"), sem("aux_loaded")
        sq_buf = [gate, up]
        conv_y = ssq

        def needs_of(*names):
            total = sum(PREPS[n][1] for n in names)
            off = PREPS[names[0]][0]
            return lambda k: (x_lo, off + min(k, total))

        for name, preps in [("conv_in", ["x"]), ("latents", ["x"]), ("uq", ["q"]), ("ukv", ["kv"]),
                            ("w_out", ["conv", "attn"]), ("ffn", ["ffn"]), ("qkv_a", ["mix2"]), ("z_ba", ["mix2"]),
                            ("qkv_b", ["mix2"]), ("w_out_2", ["gdn", "moba"]), ("xkv", ["mem"]), ("xq", ["xq"]),
                            ("xo", ["xo"]), ("ffn_2", ["ffn2"])]:
            G[name].needs = needs_of(*preps)
        G["down"].needs = lambda k: (hid_lo, k)
        G["down_2"].needs = lambda k: (hid_lo, FC + k)
        G["ffn"].stat, G["ffn_2"].stat = STATS["ffn"][0], STATS["ffn2"][0]
        adds = 0
        for g in GEMMS:
            g.a0 = adds
            adds += g.turns * g.banks if g.groups[0]["kind"] == "add" else 0

        def prep_act(act, name, src, gain, ready=None, square=None, after=None):
            off, n, first = PREPS[name]
            if after:
                act.wait_ge(products, AHEAD_P + G[after].p0 + G[after].turns * G[after].products)
            for c in range(n):
                if ready:
                    act.wait_ge(*ready(c))
                if gain is None:
                    ins = nc.scalar.activation(x2[:, first + c, 0, :], src(c), ACT.Copy)
                else:
                    ins = nc.scalar.activation(x2[:, first + c, 0, :], src(c), ACT.Copy,
                                               scale=gain(c))
                ins.then_inc(x_hi, 1)
                if square and (c % 4 == 3 or c == n - 1):
                    square_act(act, square, c // 4, src, c - c // 4 * 4 + 1)

        def prep_dve(dve, name, src, gain, square=None):
            off, n, first = PREPS[name]
            for c in range(n):
                dve.wait_ge(x_hi, off + c + 1)
                hi = x2[:, first + c, 0, :].bitcast(F32)
                if gain is None:
                    ins = nc.vector.tensor_tensor(x2[:, first + c, 1, :], src(c), hi, ALU.subtract)
                else:
                    ins = nc.vector.scalar_tensor_tensor(x2[:, first + c, 1, :], src(c), gain(c), hi,
                                                         ALU.mult, ALU.subtract)
                ins.then_inc(x_lo, 1)
                if square and (c % 4 == 3 or c == n - 1):
                    reduce_dve(dve, square, c // 4, c - c // 4 * 4 + 1)

        def square_act(act, name, k, src, n, ready=None):
            _, before, _ = STATS[name]
            if before + k - 1 > 0:
                act.wait_ge(summed, before + max(0, k - 1))
            if ready:
                act.wait_ge(*ready(4 * k + n - 1))
            nc.scalar.activation(sq_buf[k % 2][:, 0:n, :], span(src, 4 * k, n), ACT.Square).then_inc(squares, 1)

        def span(src, c, n):
            return src.whole[:, src.first + c:src.first + c + n, :]

        def reduce_dve(dve, name, k, n, src=None):
            r, before, _ = STATS[name]
            if src is None:
                dve.wait_ge(squares, squares_before(name) + k + 1)
                view = sq_buf[k % 2][:, 0:n, :]
            else:
                view = span(src, 4 * k, n)
            if k == 0 and r:
                dve.wait_ge(st_sum, r)
            nc.vector.tensor_reduce(ssq[:, k, :], view.rearrange("p c t -> p t c"), AX.X, ALU.add)\
                .then_inc(summed, 1)

        def squares_before(name):
            return STATS[name][1] - (STATS["mean"][2] if STATS[name][0] > STATS["mean"][0] else 0)

        def sum_pe(pe, name):
            r, before, parts = STATS[name]
            if r:
                pe.wait_ge(st_done, r)
            pe.wait_ge(summed, before + parts)
            for k in range(parts):
                last = nc.tensor.matmul(ps[:, 7, 0:T], ones[:], ssq[:, k, :], start=(k == 0), stop=(k == parts - 1))
            last.then_inc(st_sum, 1)

        def root_act(act, name, n, rows=P):
            r = STATS[name][0]
            if name == "mean":
                act.wait_ge(st_sum, r + 1)
                nc.scalar.activation(st_y[:], ps[:, 7, 0:T], ACT.Copy, scale=1.0 / n).then_inc(st_root, 1)
                return
            act.wait_ge(st_var, roots_before(name) + 1)
            act_chain.link(act, nc.scalar.activation(st_y[:], st_v[:], ACT.Ln))
            nc.scalar.activation(st_y[:], st_y[:], ACT.Exp, scale=-0.5).then_inc(st_root, 1)

        def roots_before(name):
            r = STATS[name][0]
            return r - (r > STATS["mean"][0])

        def refine_dve(dve, name, n, dst):
            r = STATS[name][0]
            dve.wait_ge(st_sum, r + 1)
            nc.vector.tensor_scalar(st_v[:], ps[:, 7, 0:T], 1.0 / n, EPS, ALU.mult, ALU.add).then_inc(st_var, 1)
            dve.wait_ge(st_root, r + 1)
            for _ in range(2):
                dve_chain.link(dve, nc.vector.tensor_tensor(st_v[:], st_v[:], st_y[:], ALU.mult))
            dve_chain.link(dve, nc.vector.tensor_scalar(st_v[:], st_v[:], -0.5, 1.5, ALU.mult, ALU.add))
            nc.vector.tensor_tensor(dst, st_v[:], st_y[:], ALU.mult).then_inc(st_done, 1)
            dve.wait_ge(st_done, r + 1)

        act_chain = Chain(sem("act_chain"))
        dve_chain = Chain(sem("dve_chain"))

        def source(whole, first):
            f = lambda c: whole[:, first + c, :]
            f.whole, f.first = whole, first
            return f

        def gain_of(name):
            return lambda c: col(name, c)

        def banks_out(name, n=None):
            g = G[name]
            return lambda c: (bank_free, AHEAD_B + g.e0 + c + 1)

        xs = source(xt, 0)

        rope = Milestones(sem("rope_v"), ["f", "ang", "t", "n", "r1", "r2", "r3", "c1", "c2", "c3", "s2"])
        rope_s = Milestones(sem("rope_s"), ["sin", "cos"])
        rope_t = Milestones(sem("rope_t"), ["rot"])
        rope_o = Milestones(sem("rope_o"), ["qs", "ks", "qc", "kc", "q", "k"])
        ang, tmp_n, tmp_r, tmp_c = (ar[:, 73 + k, :] for k in range(4))
        PI = 3.1415925
        C1, C2 = 6.28125, 0.0019350051879882812
        C3 = 2 * math.pi - C1 - C2

        def rope_tables_dve(dve):
            dve.wait_ge(aux_loaded, 16 * N_AUX)
            rope.reach(nc.vector.tensor_copy(tmp_r, pos_i[:]), "f")
            rope.wait(dve, "f")
            rope.reach(nc.vector.tensor_scalar(ang, tmp_r, col("inv_freq"), None, ALU.mult), "ang")
            rope.wait(dve, "ang")
            rope.reach(nc.vector.tensor_scalar(tmp_n, ang, 1 / (2 * math.pi), 12582912.0, ALU.mult, ALU.add), "t")
            rope.wait(dve, "t")
            rope.reach(nc.vector.tensor_scalar(tmp_n, tmp_n, -12582912.0, None, ALU.add), "n")
            rope.wait(dve, "n")
            for k, c in enumerate((C1, C2, C3)):
                rope.reach(nc.vector.scalar_tensor_tensor(tmp_r, tmp_n, -c, ang if k == 0 else tmp_r,
                                                          ALU.mult, ALU.add), f"r{k + 1}")
                rope.wait(dve, f"r{k + 1}")
            rope.reach(nc.vector.tensor_scalar(tmp_c, tmp_r, math.pi / 2, None, ALU.add), "c1")
            rope.wait(dve, "c1")
            rope.reach(nc.vector.tensor_scalar(tmp_n, tmp_c, math.pi, -2 * math.pi, ALU.is_gt, ALU.mult), "c2")
            rope.wait(dve, "c2")
            rope.reach(nc.vector.tensor_tensor(tmp_c, tmp_c, tmp_n, ALU.add), "c3")
            rope.wait(dve, "c3")
            dve_chain.link(dve, nc.vector.tensor_scalar(tmp_c, tmp_c, PI, -PI, ALU.min, ALU.max))
            rope.reach(nc.vector.tensor_scalar(tmp_r, tmp_r, PI, -PI, ALU.min, ALU.max), "s2")

        def rope_tables_act(act):
            rope.wait(act, "s2")
            act.wait_ge(dve_chain.sem, 1)
            rope_s.reach(nc.scalar.activation(ar[:, SIN, :], tmp_r, ACT.Sin), "sin")
            rope_s.reach(nc.scalar.activation(ar[:, COS, :], tmp_c, ACT.Sin), "cos")

        def rope_pe(pe):
            pe.wait_ge(bank_free, AHEAD_B + G["w_out"].e0)
            for c in range(4):
                nc.tensor.matmul(ps[:, 4 + c, 0:T], rope_m[:, 0, :], ar[:, Q1 + 8 + c, :], start=True, stop=True)
            for k in range(2):
                last = nc.tensor.matmul(ps[:, 4 + k, T:2 * T], rope_m[:, 1 + k, :], ar[:, Z1 + 26, :],
                                        start=True, stop=True)
            rope_t.reach(last, "rot")

        def rope_dve(dve):
            rope_s.wait(dve, "cos")
            rope_t.wait(dve, "rot")
            q = ar[:, Q1 + 8:Q1 + 12, :]
            rope_o.reach(nc.vector.tensor_tensor(ar[:, 8:12, :], ps[:, 4:8, 0:T], bc(ar[:, SIN, :], 4), ALU.mult), "qs")
            rope_o.reach(nc.vector.tensor_tensor(ar[:, 12, :], ps[:, 5, T:2 * T], ar[:, SIN, :], ALU.mult), "ks")
            rope_o.reach(nc.vector.tensor_tensor(q, q, bc(ar[:, COS, :], 4), ALU.mult), "qc")
            rope_o.reach(nc.vector.tensor_tensor(ar[:, KPE, :], ps[:, 4, T:2 * T], ar[:, COS, :], ALU.mult), "kc")
            rope_o.wait(dve, "kc")
            rope_o.reach(nc.vector.tensor_tensor(q, q, ar[:, 8:12, :], ALU.add), "q")
            rope_o.reach(nc.vector.tensor_tensor(ar[:, KPE, :], ar[:, KPE, :], ar[:, 12, :], ALU.add), "k")

        u_sig, u_done, tap1 = sem("u_sig"), sem("u_done"), sem("tap1")

        def glu_act(act, k):
            g = G["conv_in"]
            act.wait_ge(group_out, g.g0 + 2 * k + 2)
            v = ar[:, Z1 + 8 + 4 * k:Z1 + 12 + 4 * k, :]
            nc.scalar.activation(v, v, ACT.Sigmoid).then_inc(u_sig, 1)
            yield

        def conv_steps(dve):
            for k in range(2):
                dve.wait_ge(u_sig, k + 1)
                nc.vector.tensor_tensor(ar[:, U1 + 4 * k:U1 + 4 * k + 4, :], ar[:, Z1 + 4 * k:Z1 + 4 * k + 4, :],
                                        ar[:, Z1 + 8 + 4 * k:Z1 + 12 + 4 * k, :], ALU.mult).then_inc(u_done, 1)
                dve.wait_ge(u_done, k + 1)
                yield
                for s in range(CONV_K):
                    if s:
                        dve.wait_ge(tap1, 4 * (k * CONV_K + s))
                    for c in range(4 * k, 4 * k + 4):
                        y, u = ar[:, Z1 + c, :], ar[:, U1 + c, :]
                        w = col("conv_w", c * CONV_K + CONV_K - 1 - s)
                        if s == 0:
                            nc.vector.tensor_scalar(y, u, w, col("conv_b", c), ALU.mult, ALU.add).then_inc(tap1, 1)
                        else:
                            nc.vector.scalar_tensor_tensor(y[:, s:T], u[:, 0:T - s], w, y[:, s:T],
                                                           ALU.mult, ALU.add).then_inc(tap1, 1)
                    yield

        class Attention:

            def __init__(self, name, first, heads, q, k, v, vn, dst, scale, s_buf, pt_buf, widths, bias, pe=None):
                self.name, self.first, self.heads = name, first, heads
                self.q, self.k, self.v, self.vn, self.dst = q, k, v, vn, dst
                self.scale, self.s_buf, self.pt_buf = scale, s_buf, pt_buf
                self.widths, self.bias, self.pe = widths, bias, pe

        ATTN = [
            Attention("latent", 0, H, Q1, K1, V1, VN1, O1, (128 + 64) ** -0.5, ar[:, 8:12, :], ar[:, 12:16, :],
                      (P, T), lambda h: causal[:], pe=True),
            Attention("moba", H, H, ZB, ZB + 8, ZB + 16, VN2, O2B, 128 ** -0.5, tx[:, 0:4, :], tx[:, 4:8, :],
                      (P, T), lambda h: bias2[:, h, :]),
            Attention("cross", 2 * H, XH, XQ, XK, XV, XVN, XO, 128 ** -0.5, ar[:, 36:40, :], ar[:, 40:44, :],
                      (T, T), None),
        ]
        ATTN = {a.name: a for a in ATTN}
        v_turned, v_kept = sem("v_turned"), sem("v_kept")
        scored, biased, maxed = sem("scored"), sem("biased"), sem("maxed")
        exped, p_normed, p_inv = sem("exped"), sem("p_normed"), sem("p_inv")
        p_turned, p_kept = sem("p_turned"), sem("p_kept")
        o_summed, o_kept = sem("o_summed"), sem("o_kept")
        neg_max = small[:, 0, 0:4]
        p_sum = small[:, 0, 4:8]

        def vn(a):
            n = a.heads
            return ar[:, a.vn:a.vn + n, :].rearrange("p c t -> p (c t)")\
                .rearrange("p (k h d) -> p k h d", k=TT, h=n)

        def attention_pe(pe, a, ready):
            for w in ready:
                w(pe)
            pairs0 = a.first // 2
            for hp in range(a.heads // 2):
                n = pairs0 + hp
                if n >= 2:
                    pe.wait_ge(v_kept, n - 1)
                for k in range(TT):
                    for hh in range(2):
                        last = nc.tensor.transpose(ps[:, 4 + n % 2, (2 * k + hh) * P:(2 * k + hh + 1) * P],
                                                   ar[:, a.v + 2 * hp + hh, k * P:(k + 1) * P], ident[:])
                last.then_inc(v_turned, 1)
            w0, w1 = a.widths

            def scores(h):
                n = a.first + h
                if h == 0:
                    pe.wait_ge(v_kept, pairs0 + a.heads // 2)
                if n >= 2:
                    pe.wait_ge(biased, n - 1)
                bank = ps[:, 4 + n % 2, :]
                for t, w, at in ((0, w0, 0), (1, w1, w0)):
                    q = ar[:, a.q + h, t * P:(t + 1) * P]
                    last = nc.tensor.matmul(bank[:, at:at + w], q, ar[:, a.k + h, 0:w], start=True, stop=not a.pe)
                    if a.pe:
                        rows = slice(64 * (h % 2), 64 * (h % 2) + 64)
                        last = nc.tensor.matmul(bank[:, at:at + w], ar[rows, a.q + 8 + h // 2, t * P:(t + 1) * P],
                                                ar[rows, KPE, 0:w], start=False, stop=True)
                last.then_inc(scored, 1)

            scores(0)
            for h in range(a.heads):
                n = a.first + h
                if h + 1 < a.heads:
                    scores(h + 1)
                pe.wait_ge(p_normed, n + 1)
                if n >= 1:
                    pe.wait_ge(p_kept, n)
                s = a.s_buf[:, 2 * (n % 2):2 * (n % 2) + 2, :].rearrange("p c t -> p (c t)")
                for t, at, w in ((0, 0, w0), (1, w0, w1)):
                    for k in range(w // P):
                        last = nc.tensor.transpose(ps[:, 6, k * T + t * P:k * T + (t + 1) * P],
                                                   s[:, at + k * P:at + (k + 1) * P], ident[:])
                last.then_inc(p_turned, 1)
                pe.wait_ge(p_kept, n + 1)
                if n >= 1:
                    pe.wait_ge(o_kept, n)
                pt = a.pt_buf[:, 2 * (n % 2):2 * (n % 2) + 2, :]
                v = vn(a)
                nc.tensor.matmul(ps[:, 7, 0:T], v[:, 0, h, :], pt[:, 0, :], start=True, stop=False)
                q0 = 0 if w0 == T else P
                nc.tensor.matmul(ps[:, 7, q0:T], v[:, 1, h, :], pt[:, 1, q0:T], start=False, stop=True)\
                    .then_inc(o_summed, 1)

        def attention_act(act, a):
            pairs0 = a.first // 2
            for hp in range(a.heads // 2):
                n = pairs0 + hp
                act.wait_ge(v_turned, n + 1)
                nc.scalar.activation(vn(a)[:, :, 2 * hp:2 * hp + 2, :],
                                     ps[:, 4 + n % 2, :].rearrange("p (k h d) -> p k h d", k=TT, h=2),
                                     ACT.Copy).then_inc(v_kept, 1)
            w0, w1 = a.widths

            def out_copy(h):
                n = a.first + h
                act.wait_ge(o_summed, n + 1)
                nc.scalar.activation(ar[:, a.dst + h, :], ps[:, 7, 0:T], ACT.Copy).then_inc(o_kept, 1)

            def probs(h):
                n = a.first + h
                act.wait_ge(maxed, n + 1)
                s = a.s_buf[:, 2 * (n % 2):2 * (n % 2) + 2, :].rearrange("p c t -> p (c t)")
                m = small[:, n % 2, :]
                for t, at, w in ((0, 0, w0), (1, w0, w1)):
                    nc.scalar.activation(s[:, at:at + w], s[:, at:at + w], ACT.Exp, bias=m[:, t:t + 1],
                                         accum_out=m[:, 4 + t:5 + t]).then_inc(exped, 1)

            probs(0)
            for h in range(a.heads):
                n = a.first + h
                if h + 1 < a.heads:
                    probs(h + 1)
                act.wait_ge(p_turned, n + 1)
                if n >= 2:
                    act.wait_ge(o_summed, n - 1)
                pt = a.pt_buf[:, 2 * (n % 2):2 * (n % 2) + 2, :].rearrange("p c t -> p (c t)")
                if w0 == T:
                    ins = nc.scalar.activation(pt, ps[:, 6, :], ACT.Copy)
                else:
                    act_chain.step(nc.scalar.activation(pt[:, T + P:2 * T], ps[:, 6, T + P:2 * T], ACT.Copy))
                    act_chain.sync(act)
                    ins = nc.scalar.activation(pt[:, 0:T], ps[:, 6, 0:T], ACT.Copy)
                ins.then_inc(p_kept, 1)
                out_copy(h)

        def attention_dve(dve, a):
            w0, w1 = a.widths

            def biasing(h):
                n = a.first + h
                dve.wait_ge(scored, n + 1)
                if n >= 2:
                    dve.wait_ge(p_turned, n - 1)
                s = a.s_buf[:, 2 * (n % 2):2 * (n % 2) + 2, :].rearrange("p c t -> p (c t)")[:, 0:w0 + w1]
                bank = ps[:, 4 + n % 2, 0:w0 + w1]
                if a.bias:
                    ins = nc.vector.scalar_tensor_tensor(s, bank, a.scale, a.bias(h), ALU.mult, ALU.add)
                else:
                    ins = nc.vector.tensor_scalar(s, bank, a.scale, None, ALU.mult)
                ins.then_inc(biased, 1)
                dve.wait_ge(biased, n + 1)
                m = small[:, n % 2, :]
                for t, at, w in ((0, 0, w0), (1, w0, w1)):
                    ins = nc.vector.tensor_reduce(m[:, t:t + 1], s[:, at:at + w], AX.X, ALU.max, negate=True)
                    if t == 0:
                        dve_chain.step(ins)
                dve_chain.sync(dve)
                ins.then_inc(maxed, 1)

            biasing(0)
            for h in range(a.heads):
                n = a.first + h
                if h + 1 < a.heads:
                    biasing(h + 1)
                dve.wait_ge(exped, 2 * n + 2)
                m = small[:, n % 2, :]
                s = a.s_buf[:, 2 * (n % 2):2 * (n % 2) + 2, :].rearrange("p c t -> p (c t)")
                nc.vector.reciprocal(m[:, 8:10], m[:, 4:6]).then_inc(p_inv, 1)
                dve.wait_ge(p_inv, n + 1)
                dve_chain.step(nc.vector.tensor_scalar(s[:, 0:w0], s[:, 0:w0], m[:, 8:9], None, ALU.mult))
                dve_chain.sync(dve)
                nc.vector.tensor_scalar(s[:, w0:w0 + w1], s[:, w0:w0 + w1], m[:, 9:10], None, ALU.mult)\
                    .then_inc(p_normed, 1)

        hn_sq, hn_rows, hn_root = sem("hn_sq"), sem("hn_rows"), sem("hn_root")
        hn_var = sem("hn_var")
        hn_done, hn_spread, hn_used = sem("hn_done"), sem("hn_spread"), sem("hn_used")
        SPREADS = {"moba": (0, 1), "l2": (4, 2), "gdn": (12, 1)}
        HN_AT = {"moba": 0, "l2": 1, "gdn": 2}
        HN_SQ = {"moba": 0, "l2": 1, "gdn": 3}

        def headnorm_act(act, name, src, n, scale, sq_at, rows, ready):
            k, s0 = HN_AT[name], HN_SQ[name]
            for w in ready:
                w(act)
            for r in range(n // 8):
                nc.scalar.activation(tx[:, sq_at + 8 * r:sq_at + 8 * r + 8, :], span(src, 8 * r, 8), ACT.Square)\
                    .then_inc(hn_sq, 1)
            act.wait_ge(hn_var, k + 1)
            act_chain.link(act, nc.scalar.activation(st_y[0:16, :], st_v[0:16, :], ACT.Ln))
            nc.scalar.activation(st_y[0:16, :], st_y[0:16, :], ACT.Exp, scale=-0.5).then_inc(hn_root, 1)

        def headnorm_pe(pe, name, n, sq_at, rows):
            k, s0 = HN_AT[name], HN_SQ[name]
            for h in range(n):
                pe.wait_ge(hn_sq, s0 + h // 8 + 1)
                last = nc.tensor.matmul(ps[0:16, 7, 0:T], zsel[:, 15 - h:31 - h], tx[:, sq_at + h, :],
                                        start=(h == 0), stop=(h == n - 1))
            last.then_inc(hn_rows, 1)
            p0, _ = SPREADS[name]
            pe.wait_ge(hn_done, k + 1)
            for hp in range(n // 2):
                if hp >= 4:
                    pe.wait_ge(hn_used, p0 + hp - 3)
                for hh in range(2):
                    last = spread(4 + hp % 4, hh, rows, 2 * hp + hh)
                last.then_inc(hn_spread, 1)

        def spread(bank, hh, rows, h):
            return nc.tensor.matmul(ps[:, bank, hh * T:(hh + 1) * T], ident[0:16, h:h + 1].to_broadcast([16, P]),
                                    rows, start=True, stop=True)

        def headnorm_dve(dve, name, src, n, scale, rows, extra=None):
            k = HN_AT[name]
            dve.wait_ge(hn_rows, k + 1)
            v, y = st_v[0:16, :], st_y[0:16, :]
            nc.vector.tensor_scalar(v, ps[0:16, 7, 0:T], scale, EPS, ALU.mult, ALU.add).then_inc(hn_var, 1)
            dve.wait_ge(hn_root, k + 1)
            for _ in range(2):
                dve_chain.link(dve, nc.vector.tensor_tensor(v, v, y, ALU.mult))
            dve_chain.link(dve, nc.vector.tensor_scalar(v, v, -0.5, 1.5, ALU.mult, ALU.add))
            nc.vector.tensor_tensor(rows, v, y, ALU.mult).then_inc(hn_done, 1)
            p0, _ = SPREADS[name]
            for hp in range(n // 2):
                dve.wait_ge(hn_spread, p0 + hp + 1)
                v2 = span(src, 2 * hp, 2).rearrange("p c t -> p (c t)")
                if extra and hp < 4:
                    ins = nc.vector.scalar_tensor_tensor(v2, v2, extra, ps[:, 4 + hp % 4, :], ALU.mult, ALU.mult)
                else:
                    ins = nc.vector.tensor_tensor(v2, v2, ps[:, 4 + hp % 4, :], ALU.mult)
                ins.then_inc(hn_used, 1)

        rel_in, rel_ps, rel_sb, rel_out, rel_back = (sem(n) for n in ("rel_in", "rel_ps", "rel_sb", "rel_out", "rel_back"))

        def rel_pool(pool):
            g = G["qkv_b"]
            pool.wait_ge(products, AHEAD_P + g.p0 + g.turns * g.products)
            pool.dma_start(rel_hot[:], A["hot"]).then_inc(rel_in, 16)
            pool.dma_start(rel_neg[:], A["hot_neg"]).then_inc(rel_in, 16)
            pool.dma_start(rel_b[:], A["rel_bias_2"]).then_inc(rel_in, 16)
            pool.dma_start(masks[:], A["masks"]).then_inc(mask_in, 16)
            pool.wait_ge(rel_sb, 1)
            pool.dma_start(rel_d, rel_e[:]).then_inc(rel_out, 16)
            pool.wait_ge(rel_out, 16)
            pool.dma_start(rel_s, rel_d.unsqueeze(1).to_broadcast([H, P, 384])).then_inc(rel_out, 16)
            pool.wait_ge(rel_out, 32)
            for h in range(H):
                s = h * P * 384
                pool.dma_start(bias2[:, h, 0:P], bass.AP(rel_s.tensor, s + 255, [[383, P], [1, P]]))\
                    .then_inc(rel_back, 16)
                pool.dma_start(bias2[:, h, P:P + T], bass.AP(rel_s.tensor, s + 127, [[383, P], [1, T]]))\
                    .then_inc(rel_back, 16)

        mask_in = sem("mask_in")

        def rel_pe(pe):
            pe.wait_ge(rel_in, 48)
            nc.tensor.matmul(ps[0:H, 7, 0:384], rel_b[:], rel_hot[:], start=True, stop=True).then_inc(rel_ps, 1)

        def rel_dve(dve):
            dve.wait_ge(rel_ps, 1)
            nc.vector.tensor_tensor(rel_e[:], ps[0:H, 7, 0:384], rel_neg[:], ALU.add).then_inc(rel_sb, 1)

        gc_y, gc_act, gc_tap = sem("gc_y"), sem("gc_act"), sem("gc_tap")

        def gconv_dve(dve):
            for b in range(6):
                if b >= 2:
                    dve.wait_ge(gc_act, b - 1)
                for s in range(GDN_K):
                    if s:
                        dve.wait_ge(gc_tap, b * 15 + 4 * s)
                    for m in range(4):
                        c = 4 * b + m
                        y, u = ar[:, 57 + 4 * (b % 2) + m, :], ar[:, ZA + c, :]
                        w = col("gdn_conv", c * GDN_K + GDN_K - 1 - s)
                        if s == 0:
                            ins = nc.vector.tensor_scalar(y, u, w, None, ALU.mult)
                        else:
                            if s == GDN_K - 1 and m == 3:
                                dve.wait_ge(gc_tap, b * 15 + 15)
                            ins = nc.vector.scalar_tensor_tensor(y[:, s:T], u[:, 0:T - s], w, y[:, s:T],
                                                                 ALU.mult, ALU.add)
                        ins.then_inc(*((gc_y, 1) if s == GDN_K - 1 and m == 3 else (gc_tap, 1)))
                    if s % 2:
                        yield

        def gconv_act(act):
            yield
            yield
            for b in range(6):
                act.wait_ge(gc_y, b + 1)
                nc.scalar.activation(ar[:, ZA + 4 * b:ZA + 4 * b + 4, :],
                                     ar[:, 57 + 4 * (b % 2):61 + 4 * (b % 2), :], ACT.Silu).then_inc(gc_act, 1)
                yield
                yield

        NP = 2 * H
        LV = 7

        def prob(base, t=ar):
            return t[:, base:base + 8, :].rearrange("p c t -> p (c t)").rearrange("p (n k) -> p n k", k=P)

        k_of = lambda h, c: ar[:, ZA + 8 + h, c * P:(c + 1) * P]
        q_of = lambda h, c: ar[:, ZA + h, c * P:(c + 1) * P]
        v_of = lambda h, c: ar[:, ZA + 16 + h, c * P:(c + 1) * P]
        at_, qk_, uu_, vb_ = prob(AT), prob(QK), prob(UU), prob(VB)
        tt_, ww_, bb_, u_ = prob(0, tx), prob(8, tx), prob(16, tx), prob(24, tx)
        dt_ = ww_

        def half_prob(base, t=ar):
            return t[:, base:base + 4, :].rearrange("p c t -> p (c t)").rearrange("p (n k) -> p n k", k=P)

        kbg_, kd_, qd_ = half_prob(KBG1), half_prob(KDEC0), half_prob(QDEC1)
        s1_, wt_ = half_prob(16, tx), half_prob(20, tx)
        row_b, row_g = ar[0:16, RBETA, :], ar[0:16, RG, :]
        g_nat = small[:, :, 16:32]
        G_nat = small[:, :, 32:48]
        b_nat = small[:, :, 48:64]
        gl_nat = small[:, 0, 0:16]
        eg_nat = small[:, 1, 0:16]
        low, high = ps[:, 0:4, :], ps[:, 4:8, :]

        def pb(n0, n=4):
            return ps[:, n0:n0 + n, :].rearrange("p b t -> p (b t)").rearrange("p (n k) -> p n k", k=P)

        levels = range(1, LV)
        gt = Milestones(sem("gdn_pe"), ["g_nat", "G_row", "nat", "kk", "G_rows", "b_rows", "qk", "vt", "kt", "I_T"] +
                        [f"{x}{l}" for l in levels for x in ("W", "TW", "UW")[:3 if l < LV - 1 else 3] if not (l == LV - 1 and x == "TW")] +
                        ["u", "wT", "S1", "wS", "o"])
        gs = Milestones(sem("gdn_act"), ["beta", "ea", "e", "l", "x0", "x1", "dt", "qdec", "vb", "kbg", "kd", "T0"] +
                        [f"W{l}" for l in levels] + ["u", "wT", "S1", "silu_z", "o"])
        gv = Milestones(sem("gdn_dve"), ["ya", "ny", "ab", "m", "sp", "g", "g_nat", "G_row", "nat", "gd", "dt",
                                         "qd", "at1", "at2", "qk1", "qk2", "eb", "B0", "U0"] +
                        [f"{x}{l}" for l in levels for x in ("B", "T", "U") if not (l == LV - 1 and x == "T")] +
                        ["vnew"])

        def gdn_dve(dve):
            ba = ar[0:16, BA, :]
            v0, y0 = st_v[0:16, :], st_y[0:16, :]
            t1 = rs_x[0:16, :]
            gv.reach(nc.vector.tensor_scalar(v0, ba, col("dt_bias", rows=16), None, ALU.add), "ya")
            gv.wait(dve, "ya")
            gv.reach(nc.vector.tensor_scalar(y0, v0, -1.0, None, ALU.mult), "ny")
            gv.wait(dve, "ny")
            gv.reach(nc.vector.tensor_tensor(t1, v0, y0, ALU.max), "ab")
            gv.reach(nc.vector.tensor_scalar(v0, v0, 0.0, None, ALU.max), "m")
            gs.wait(dve, "l")
            gv.wait(dve, "m")
            gv.reach(nc.vector.tensor_tensor(v0, v0, t1, ALU.add), "sp")
            gv.wait(dve, "sp")
            gv.reach(nc.vector.tensor_scalar(v0, v0, small[0:16, 0, 0:1], -1.0, ALU.mult, ALU.mult), "g")
            gt.wait(dve, "g_nat")
            gv.reach(nc.vector.tensor_copy(g_nat, ps[:, 7, 0:32].rearrange("p (c k) -> p c k", c=2)), "g_nat")
            gt.wait(dve, "G_row")
            gv.reach(nc.vector.tensor_copy(row_g, ps[0:16, 6, 0:T]), "G_row")
            gt.wait(dve, "nat")
            dve_chain.link(dve, nc.vector.tensor_copy(G_nat, ps[:, 7, 0:32].rearrange("p (c k) -> p c k", c=2)))
            dve_chain.link(dve, nc.vector.tensor_copy(b_nat, ps[:, 7, 32:64].rearrange("p (c k) -> p c k", c=2)))
            gv.reach(nc.vector.tensor_copy(gl_nat, ps[:, 7, 64:80]), "nat")
            gv.wait(dve, "nat")
            gv.reach(nc.vector.tensor_tensor(gl_nat, gl_nat, G_nat[:, 0, :], ALU.subtract), "gd")
            gt.wait(dve, "G_rows")
            for h in range(H):
                for c in range(2):
                    ins = nc.vector.tensor_scalar(dt_[:, 2 * h + c, :], ps[:, 4 + h // 2, ((h % 2) * 2 + c) * P:((h % 2) * 2 + c + 1) * P],
                                                  G_nat[:, c, 8 + h:9 + h], 0.0, ALU.subtract, ALU.min)
                    if (h, c) != (H - 1, 1):
                        dve_chain.step(ins)
            dve_chain.sync(dve)
            gv.reach(ins, "dt")
            gs.wait(dve, "qdec")
            gv.reach(nc.vector.tensor_tensor(qd_, qd_, ar[:, ZA:ZA + 8, P:T], ALU.mult), "qd")
            gt.wait(dve, "kk")
            gv.reach(nc.vector.tensor_tensor(at_, pb(0), dt_, ALU.mult), "at1")
            gv.wait(dve, "at1")
            gt.wait(dve, "b_rows")
            gv.reach(nc.vector.tensor_tensor(at_, at_, pb(4), ALU.mult), "at2")
            gt.wait(dve, "qk")
            gv.reach(nc.vector.tensor_tensor(qk_, pb(0), dt_, ALU.mult), "qk1")
            gv.wait(dve, "qk1")
            gv.reach(nc.vector.tensor_tensor(qk_, qk_, masks[:, 7:8, :].to_broadcast([P, NP, P]), ALU.mult), "qk2")
            gs.wait(dve, "x1")
            gv.reach(nc.vector.tensor_tensor(eg_nat[:, 0:H], eg_nat[:, H:2 * H], b_nat[:, 1, 0:H], ALU.mult), "eb")
            gv.reach(nc.vector.tensor_tensor(bb_, at_, masks[:, 0:1, :].to_broadcast([P, NP, P]), ALU.mult), "B0")
            gv.wait(dve, "B0")
            gv.reach(nc.vector.tensor_tensor(uu_, ident[:].unsqueeze(1).to_broadcast([P, NP, P]), bb_, ALU.subtract), "U0")
            for l in levels:
                if l > 1:
                    gt.wait(dve, f"W{l - 1}")
                else:
                    gv.wait(dve, "U0")
                gv.reach(nc.vector.tensor_tensor(bb_, at_, masks[:, l:l + 1, :].to_broadcast([P, NP, P]), ALU.mult), f"B{l}")
                if l < LV - 1:
                    gt.wait(dve, f"TW{l}")
                    gt.wait(dve, f"UW{l}")
                    gv.reach(nc.vector.tensor_tensor(tt_, tt_, pb(4), ALU.subtract), f"T{l}")
                gt.wait(dve, f"UW{l}")
                gv.reach(nc.vector.tensor_tensor(uu_, uu_, pb(0), ALU.subtract), f"U{l}")
            gt.wait(dve, "wS")
            gv.reach(nc.vector.tensor_tensor(u_[:, 1:NP:2, :], u_[:, 1:NP:2, :], pb(0, 2), ALU.subtract), "vnew")

        def gdn_act(act):
            nc_a = nc.scalar.activation
            gs.reach(nc_a(row_b, ar[0:16, BA, :], ACT.Sigmoid), "beta")
            gs.reach(nc_a(small[0:16, 0, 0:1], col("a_log", rows=16), ACT.Exp), "ea")
            gv.wait(act, "ab")
            gs.reach(nc_a(rs_x[0:16, :], rs_x[0:16, :], ACT.Exp, scale=-1.0), "e")
            gs.wait(act, "e")
            gs.reach(nc_a(rs_x[0:16, :], rs_x[0:16, :], ACT.Ln, bias=1.0), "l")
            gv.wait(act, "gd")
            gs.reach(nc_a(gl_nat, gl_nat, ACT.Exp), "x0")
            gs.reach(nc_a(eg_nat, G_nat[:, 1, :], ACT.Exp), "x1")
            gv.wait(act, "dt")
            gs.reach(nc_a(dt_, dt_, ACT.Exp), "dt")
            gt.wait(act, "G_rows")
            gs.reach(nc_a(qd_.rearrange("p (b h) k -> p b h k", b=4),
                          ps[:, 4:8, :].rearrange("p b (h c k) -> p b h c k", h=2, c=2)[:, :, :, 1, :], ACT.Exp), "qdec")
            gt.wait(act, "vt")
            for h in range(H):
                for c in range(2):
                    n = 2 * h + c
                    ins = nc_a(vb_[:, n, :], pb(4)[:, n, :], ACT.Copy, scale=b_nat[:, c, h:h + 1])
                    if n < NP - 1:
                        act_chain.step(ins)
            act_chain.sync(act)
            gs.reach(ins, "vb")
            gt.wait(act, "kt")
            gv.wait(act, "eb")
            for h in range(H):
                ins = nc_a(kbg_[:, h, :], pb(0)[:, 2 * h + 1, :], ACT.Copy, scale=eg_nat[:, h:h + 1])
                if h < H - 1:
                    act_chain.step(ins)
            act_chain.sync(act)
            gs.reach(ins, "kbg")
            for h in range(H):
                ins = nc_a(kd_[:, h, :], pb(0)[:, 2 * h, :], ACT.Copy, scale=gl_nat[:, 8 + h:9 + h])
                if h < H - 1:
                    act_chain.step(ins)
            act_chain.sync(act)
            gs.reach(ins, "kd")
            gt.wait(act, "I_T")
            gs.reach(nc_a(tt_, pb(4), ACT.Copy), "T0")
            for l in levels:
                gt.wait(act, f"W{l}")
                gs.reach(nc_a(ww_, pb(0), ACT.Copy), f"W{l}")
            gt.wait(act, "u")
            gs.reach(nc_a(u_, pb(4), ACT.Copy), "u")
            gt.wait(act, "wT")
            gs.reach(nc_a(wt_, pb(0, 2), ACT.Copy), "wT")
            gt.wait(act, "S1")
            gs.reach(nc_a(s1_, pb(2, 2), ACT.Copy), "S1")
            gs.reach(nc_a(ar[:, ZZ:ZZ + 8, :], ar[:, ZZ:ZZ + 8, :], ACT.Silu), "silu_z")
            gt.wait(act, "o")
            gs.reach(nc_a(prob(OG), pb(4), ACT.Copy), "o")

        def gdn_pe(pe):
            mm, tr = nc.tensor.matmul, nc.tensor.transpose
            gv.wait(pe, "g")
            for c in range(2):
                last = tr(ps[:, 7, 16 * c:16 * c + 16], st_v[0:16, c * P:(c + 1) * P], ident[0:16, 0:16])
            gt.reach(last, "g_nat")
            gv.wait(pe, "g_nat")
            pe.wait_ge(mask_in, 16)
            for c in range(2):
                last = mm(ps[0:16, 6, c * P:(c + 1) * P], g_nat[:, c, :], masks[:, 7, :], start=True, stop=True)
            gt.reach(last, "G_row")
            gv.wait(pe, "G_row")
            gs.wait(pe, "beta")
            for k, row in enumerate((row_g, row_b)):
                for c in range(2):
                    tr(ps[:, 7, 32 * k + 16 * c:32 * k + 16 * c + 16], row[:, c * P:(c + 1) * P], ident[0:16, 0:16])
            gt.reach(mm(ps[:, 7, 64:80], ones[:], g_nat[:, 0, :], start=True, stop=True), "nat")
            for n in range(NP):
                last = mm(pb(0)[:, n, :], k_of(n // 2, n % 2), k_of(n // 2, n % 2), start=True, stop=True)
            gt.reach(last, "kk")
            gv.wait(pe, "nat")
            for h in range(H):
                last = spread(4 + h // 2, h % 2, row_g, 8 + h)
            gt.reach(last, "G_rows")
            gv.wait(pe, "dt")
            gs.wait(pe, "qdec")
            for h in range(H):
                last = spread(4 + h // 2, h % 2, row_b, h)
            gt.reach(last, "b_rows")
            gv.wait(pe, "at1")
            for n in range(NP):
                last = mm(pb(0)[:, n, :], k_of(n // 2, n % 2), q_of(n // 2, n % 2), start=True, stop=True)
            gt.reach(last, "qk")
            gv.wait(pe, "at2")
            for n in range(NP):
                last = tr(pb(4)[:, n, :], v_of(n // 2, n % 2), ident[:])
            gt.reach(last, "vt")
            gv.wait(pe, "qk1")
            for n in range(NP):
                last = tr(pb(0)[:, n, :], k_of(n // 2, n % 2), ident[:])
            gt.reach(last, "kt")
            gs.wait(pe, "vb")
            gv.wait(pe, "U0")
            for n in range(NP):
                last = tr(pb(4)[:, n, :], uu_[:, n, :], ident[:])
            gt.reach(last, "I_T")
            gs.wait(pe, "T0")
            gs.wait(pe, "kd")
            for l in levels:
                gv.wait(pe, f"B{l}")
                if l > 1:
                    gv.wait(pe, f"U{l - 1}")
                for n in range(NP):
                    last = mm(pb(0)[:, n, :], bb_[:, n, :], tt_[:, n, :], start=True, stop=True)
                gt.reach(last, f"W{l}")
                gs.wait(pe, f"W{l}")
                if l < LV - 1:
                    for n in range(NP):
                        last = mm(pb(4)[:, n, :], uu_[:, n, :], ww_[:, n, :], start=True, stop=True)
                    gt.reach(last, f"TW{l}")
                for n in range(NP):
                    last = mm(pb(0)[:, n, :], ww_[:, n, :], uu_[:, n, :], start=True, stop=True)
                gt.reach(last, f"UW{l}")
            gv.wait(pe, f"U{LV - 1}")
            for n in range(NP):
                last = mm(pb(4)[:, n, :], uu_[:, n, :], vb_[:, n, :], start=True, stop=True)
            gt.reach(last, "u")
            for h in range(H):
                last = mm(pb(0)[:, h, :], kbg_[:, h, :], uu_[:, 2 * h + 1, :], start=True, stop=True)
            gt.reach(last, "wT")
            gs.wait(pe, "u")
            for h in range(H):
                last = mm(pb(2)[:, h, :], kd_[:, h, :], u_[:, 2 * h, :], start=True, stop=True)
            gt.reach(last, "S1")
            gs.wait(pe, "S1")
            for h in range(H):
                last = mm(pb(0)[:, h, :], wt_[:, h, :], s1_[:, h, :], start=True, stop=True)
            gt.reach(last, "wS")
            gv.wait(pe, "vnew")
            gv.wait(pe, "qd")
            for h in range(H):
                mm(pb(4)[:, 2 * h, :], u_[:, 2 * h, :], qk_[:, 2 * h, :], start=True, stop=True)
                mm(pb(4)[:, 2 * h + 1, :], s1_[:, h, :], qd_[:, h, :], start=True, stop=False)
                last = mm(pb(4)[:, 2 * h + 1, :], u_[:, 2 * h + 1, :], qk_[:, 2 * h + 1, :], start=False, stop=True)
            gt.reach(last, "o")

        block = ctx.enter_context(nc.Block())
        N_AUX = 4
        mem_in, out_done, start_v, start_p = sem("mem_in"), sem("out_done"), sem("start_v"), sem("start_p")
        zsel = sb("zsel", [P, 32], F32, room(128))
        applied, ln_out, x_added, out_ready = sem("applied"), sem("ln_out"), sem("x_added"), sem("out_ready")

        @block.sync
        def _(sp):
            sp.dma_start(xt[:], A["xt"]).then_inc(xt_loaded, 16)
            sp.dma_start(cols[:], A["cols"]).then_inc(cols_loaded, 16)
            for g in GEMMS:
                load(sp, g)

        @block.gpsimd
        def _(pool):
            pool.memset(ones[:], 1.0).then_inc(start_p, 1)
            pool.memset(zsel[:], 0.0).then_inc(start_p, 1)
            pool.wait_ge(start_p, 2)
            pool.memset(zsel[:, 15:16], 1.0).then_inc(start_p, 1)
            pool.dma_start(ident[:], A["ident"]).then_inc(aux_loaded, 16)
            pool.dma_start(pos_i[:], A["positions"].partition_broadcast(P).rearrange("a b t -> a (b t)")).then_inc(aux_loaded, 16)
            pool.dma_start(causal[:], A["causal"]).then_inc(aux_loaded, 16)
            pool.dma_start(rope_m[:], A["rope_m"]).then_inc(aux_loaded, 16)
            rel_pool(pool)
            gt.wait(pool, "o")
            gs.wait(pool, "o")
            pool.dma_start(ar[:, MEM:MEM + DC, :], A["mem"]).then_inc(mem_in, 16)
            pool.wait_ge(out_ready, DC)
            pool.dma_start(out, tx[:, 0:DC, :]).then_inc(out_done, 16)
            pool.wait_ge(out_done, 16)

        def norm(name):
            return {"x": (D, rs_x[:]), "q": (768, rs_x[:]), "kv": (512, rs_kv), "mean": (1024, None),
                    "ln": (1024, st_y[:]), "conv": (1024, st_y[:]), "attn": (1024, st_y[:]), "mix": (D, st_y[:]),
                    "ffn": (D, rs_x[:]), "ff": (D, st_y[:]), "mix2": (D, rs_x[:]), "mem": (D, rs_x[:]),
                    "xq": (D, rs_x[:]), "ffn2": (D, rs_x[:]), "final": (D, st_y[:])}[name]

        def root(act, name):
            root_act(act, name, norm(name)[0])

        def refine(dve, name):
            refine_dve(dve, name, *norm(name))

        def groups_out(name):
            g = G[name]
            n = sum(gr["kind"] == "z" for gr in g.groups)
            return lambda c=None: (group_out, g.g0 + g.turns * n)

        mix_out, ff_out = source(ar, M1), source(tx, 16)
        u_src, attn_src, q_src, kv_src = source(ar, Z1), source(ar, O1), source(ar, Z1 + 16), source(ar, Z1 + 22)
        og_src, moba_src, mem_src, xo_src = source(ar, OG), source(ar, O2B), source(ar, MEM), source(ar, XO)
        l2_src = source(ar, ZA)

        @block.scalar
        def _(act):
            def ahead_(name):
                ahead(act, split_act, evict_act, G[name])

            def run_(name, filler=None, fill_from=0, stat=None):
                run(act, split_act, evict_act, G[name], filler, fill_from,
                    stat and (FIRST + 2, lambda: root(act, stat)))

            def squares_(name, src, ready=None):
                n = STATS[name][2]
                for k in range(n):
                    square_act(act, name, k, src, 4, ready)

            act.wait_ge(aux_loaded, 16 * N_AUX)
            act.wait_ge(cols_loaded, 16)
            ahead_("conv_in")
            prep_act(act, "x", xs, gain_of("pre_mix"), lambda c: (xt_loaded, 16), "x")
            run_("conv_in", glu_act(act, 0), 3, stat="x")
            rope_tables_act(act)
            ahead_("latents")
            finish(glu_act(act, 1))
            run_("latents")
            ahead_("uq")
            prep_act(act, "q", q_src, gain_of("q_norm"), groups_out("latents"), "q", "latents")
            root(act, "q")
            prep_act(act, "kv", kv_src, gain_of("kv_norm"), None, "kv")
            root(act, "kv")
            run_("uq")
            ahead_("ukv")
            run_("ukv")
            ahead_("w_out")
            attention_act(act, ATTN["latent"])
            root(act, "mean")
            squares_("ln", u_src, lambda c: (st_done, STATS["mean"][0] + 1))
            root(act, "ln")
            act.wait_ge(applied, 1)
            for c in range(CC):
                nc.scalar.activation(ar[:, Z1 + c, :], ar[:, Z1 + c, :], ACT.Silu, bias=col("conv_ln_b", c),
                                     scale=col("conv_ln_g", c)).then_inc(ln_out, 1)
            squares_("conv", u_src, lambda c: (ln_out, c + 1))
            root(act, "conv")
            squares_("attn", attn_src, lambda c: (o_kept, c + 1))
            root(act, "attn")
            prep_act(act, "conv", u_src, gain_of("conv_out"), lambda c: (applied, 2), None, "ukv")
            prep_act(act, "attn", attn_src, gain_of("attn_out"), lambda c: (applied, 3))
            run_("w_out")
            ahead_("ffn")
            squares_("mix", mix_out, banks_out("w_out"))
            root(act, "mix")
            prep_act(act, "ffn", xs, gain_of("pre_ffn"), lambda c: (x_added, c + 1), "ffn", "w_out")
            run_("ffn", stat="ffn")
            ahead_("down")
            run_("down")
            ahead_("qkv_a")
            squares_("ff", ff_out, banks_out("down"))
            root(act, "ff")
            prep_act(act, "mix2", xs, gain_of("mix2"), lambda c: (x_added, DC + c + 1), "mix2", "ffn")
            run_("qkv_a", stat="mix2")
            ahead_("z_ba")
            act.wait_ge(*groups_out("qkv_a")())
            filler = gconv_act(act)
            run_("z_ba", filler)
            finish(filler)
            ahead_("qkv_b")
            run_("qkv_b")
            ahead_("w_out_2")
            attention_act(act, ATTN["moba"])
            headnorm_act(act, "moba", moba_src, 8, 1 / P, 16, RQK, [lambda e: e.wait_ge(o_kept, 2 * H)])
            headnorm_act(act, "l2", l2_src, 16, 1.0, 0, RQK, [lambda e: e.wait_ge(gc_act, 6)])
            gdn_act(act)
            headnorm_act(act, "gdn", og_src, 8, 1 / P, 0, RQK, [lambda e: gs.wait(e, "o")])
            prep_act(act, "gdn", og_src, lambda c: col("gdn_norm"), lambda c: (applied, 6))
            prep_act(act, "moba", moba_src, lambda c: col("moba_norm"), lambda c: (hn_used, 4))
            run_("w_out_2")
            ahead_("xkv")
            prep_act(act, "mem", mem_src, gain_of("mem"), lambda c: (mem_in, 16), "mem", "w_out_2")
            run_("xkv", stat="mem")
            ahead_("xq")
            prep_act(act, "xq", xs, gain_of("xattn"), banks_out("w_out_2"), "xq", "xkv")
            run_("xq", stat="xq")
            ahead_("xo")
            attention_act(act, ATTN["cross"])
            prep_act(act, "xo", xo_src, None, lambda c: (o_kept, 2 * H + c + 1), None, "xq")
            run_("xo")
            ahead_("ffn_2")
            prep_act(act, "ffn2", xs, gain_of("ffn2"), banks_out("xo"), "ffn2", "xo")
            run_("ffn_2", stat="ffn2")
            ahead_("down_2")
            run_("down_2")
            g = G["down_2"]
            finish(evict_act(act, g, g.turns - 1, g.groups[-1]))
            squares_("final", xs, banks_out("down_2"))
            root(act, "final")

        @block.vector
        def _(dve):
            def ahead_(name):
                ahead(dve, split_dve, evict_dve, G[name])

            def run_(name, filler=None, fill_from=0, stat=None):
                run(dve, split_dve, evict_dve, G[name], filler, fill_from,
                    stat and (FIRST + 2, lambda: refine(dve, stat)))

            def reduces_(name, src=None):
                n = STATS[name][2]
                for k in range(n):
                    reduce_dve(dve, name, k, 4, src)

            def apply(src, n):
                v = span(src, 0, n)
                nc.vector.tensor_tensor(v, v, bc(st_y, n), ALU.mult).then_inc(applied, 1)
                apply.n += 1
                dve.wait_ge(applied, apply.n)
            apply.n = 0

            def add_norm(name, src, gain):
                reduces_(name)
                refine(dve, name)
                apply(src, DC)
                for c in range(DC):
                    nc.vector.scalar_tensor_tensor(xt[:, c, :], src(c), col(gain, c), xt[:, c, :],
                                                   ALU.mult, ALU.add).then_inc(x_added, 1)

            dve.sem_inc(bank_free, AHEAD_B)
            dve.wait_ge(aux_loaded, 16 * N_AUX)
            dve.wait_ge(cols_loaded, 16)
            ahead_("conv_in")
            prep_dve(dve, "x", xs, gain_of("pre_mix"), "x")
            filler = conv_steps(dve)
            run_("conv_in", filler, 3, stat="x")
            rope_tables_dve(dve)
            ahead_("latents")
            run_("latents", filler)
            ahead_("uq")
            prep_dve(dve, "q", q_src, gain_of("q_norm"), "q")
            refine(dve, "q")
            prep_dve(dve, "kv", kv_src, gain_of("kv_norm"), "kv")
            refine(dve, "kv")
            run_("uq", filler)
            ahead_("ukv")
            run_("ukv", filler)
            ahead_("w_out")
            rope_dve(dve)
            attention_dve(dve, ATTN["latent"])
            finish(filler)
            dve.wait_ge(tap1, CC * CONV_K)
            reduces_("mean", u_src)
            r = STATS["mean"][0]
            dve.wait_ge(st_root, r + 1)
            nc.vector.tensor_tensor(span(u_src, 0, CC), span(u_src, 0, CC), bc(st_y, CC), ALU.subtract)\
                .then_inc(st_done, 1)
            dve.wait_ge(st_done, r + 1)
            reduces_("ln")
            refine(dve, "ln")
            apply(u_src, CC)
            reduces_("conv")
            refine(dve, "conv")
            apply(u_src, CC)
            reduces_("attn")
            refine(dve, "attn")
            apply(attn_src, H)
            prep_dve(dve, "conv", u_src, gain_of("conv_out"))
            prep_dve(dve, "attn", attn_src, gain_of("attn_out"))
            run_("w_out")
            ahead_("ffn")
            add_norm("mix", mix_out, "post_mix")
            prep_dve(dve, "ffn", xs, gain_of("pre_ffn"), "ffn")
            run_("ffn", stat="ffn")
            ahead_("down")
            run_("down")
            ahead_("qkv_a")
            add_norm("ff", ff_out, "post_ffn")
            prep_dve(dve, "mix2", xs, gain_of("mix2"), "mix2")
            run_("qkv_a", stat="mix2")
            ahead_("z_ba")
            dve.wait_ge(*groups_out("qkv_a")())
            filler = gconv_dve(dve)
            run_("z_ba", filler)
            finish(filler)
            ahead_("qkv_b")
            run_("qkv_b")
            ahead_("w_out_2")
            rel_dve(dve)
            dve.wait_ge(rel_back, 16 * 2 * H)
            attention_dve(dve, ATTN["moba"])
            row = ar[0:16, RQK, :]
            headnorm_dve(dve, "moba", moba_src, 8, 1 / P, row)
            headnorm_dve(dve, "l2", l2_src, 16, 1.0, row, extra=P ** -0.5)
            gdn_dve(dve)
            headnorm_dve(dve, "gdn", og_src, 8, 1 / P, row)
            gs.wait(dve, "silu_z")
            dve.wait_ge(hn_used, 16)
            nc.vector.tensor_tensor(span(og_src, 0, H), span(og_src, 0, H), ar[:, ZZ:ZZ + H, :], ALU.mult)\
                .then_inc(applied, 1)
            apply.n += 1
            prep_dve(dve, "gdn", og_src, lambda c: col("gdn_norm"))
            prep_dve(dve, "moba", moba_src, lambda c: col("moba_norm"))
            run_("w_out_2")
            ahead_("xkv")
            prep_dve(dve, "mem", mem_src, gain_of("mem"), "mem")
            run_("xkv", stat="mem")
            ahead_("xq")
            prep_dve(dve, "xq", xs, gain_of("xattn"), "xq")
            run_("xq", stat="xq")
            ahead_("xo")
            attention_dve(dve, ATTN["cross"])
            prep_dve(dve, "xo", xo_src, None)
            run_("xo")
            ahead_("ffn_2")
            prep_dve(dve, "ffn2", xs, gain_of("ffn2"), "ffn2")
            run_("ffn_2", stat="ffn2")
            ahead_("down_2")
            run_("down_2")
            g = G["down_2"]
            finish(evict_dve(dve, g, g.turns - 1, g.groups[-1]))
            reduces_("final")
            refine(dve, "final")
            for c in range(DC):
                nc.vector.scalar_tensor_tensor(tx[:, c, :], xt[:, c, :], col("final", c), st_y[:],
                                               ALU.mult, ALU.mult).then_inc(out_ready, 1)

        @block.tensor
        def _(pe):
            pe.sem_inc(products, AHEAD_P)
            pe.wait_ge(start_p, 3)
            pe.wait_ge(aux_loaded, 16 * N_AUX)
            multiply(pe, G["conv_in"], "x")
            multiply(pe, G["latents"])
            sum_pe(pe, "q")
            sum_pe(pe, "kv")
            multiply(pe, G["uq"])
            multiply(pe, G["ukv"])
            pe.wait_ge(st_done, STATS["kv"][0] + 1)
            rope_pe(pe)
            attention_pe(pe, ATTN["latent"], [lambda e: e.wait_ge(*groups_out("ukv")()),
                                              lambda e: rope_o.wait(e, "k")])
            for name in ("mean", "ln", "conv", "attn"):
                if name == "mean":
                    pe.wait_ge(o_kept, H)
                sum_pe(pe, name)
            multiply(pe, G["w_out"])
            sum_pe(pe, "mix")
            multiply(pe, G["ffn"], "ffn")
            multiply(pe, G["down"])
            sum_pe(pe, "ff")
            multiply(pe, G["qkv_a"], "mix2")
            multiply(pe, G["z_ba"])
            multiply(pe, G["qkv_b"])
            pe.wait_ge(st_done, STATS["mix2"][0] + 1)
            pe.wait_ge(bank_free, AHEAD_B + G["w_out_2"].e0)
            rel_pe(pe)
            attention_pe(pe, ATTN["moba"], [lambda e: e.wait_ge(*groups_out("qkv_b")())])
            pe.wait_ge(o_kept, 2 * H)
            pe.wait_ge(biased, 2 * H)
            headnorm_pe(pe, "moba", 8, 16, ar[0:16, RQK, :])
            pe.wait_ge(hn_used, 4)
            headnorm_pe(pe, "l2", 16, 0, ar[0:16, RQK, :])
            pe.wait_ge(hn_used, 12)
            gdn_pe(pe)
            headnorm_pe(pe, "gdn", 8, 0, ar[0:16, RQK, :])
            multiply(pe, G["w_out_2"])
            multiply(pe, G["xkv"], "mem")
            multiply(pe, G["xq"], "xq")
            pe.wait_ge(st_done, STATS["xq"][0] + 1)
            attention_pe(pe, ATTN["cross"], [lambda e: e.wait_ge(*groups_out("xq")())])
            multiply(pe, G["xo"])
            pe.wait_ge(o_kept, 2 * H + XH)
            multiply(pe, G["ffn_2"], "ffn2")
            multiply(pe, G["down_2"])
            sum_pe(pe, "final")


_IN = ["positions", "w_in", "w_uq", "w_ukv", "w_out", "w_gate", "w_up", "w_down", "w_in_2", "w_out_2",
       "w_xq_2", "w_xkv_2", "w_xo_2", "w_gate_2", "w_up_2", "w_down_2", "rel_bias_2"]
_DROP_LAYER = {n for n in _IN if n.startswith("w_")}


def _chunks(v):
    return np.ascontiguousarray(v.reshape(-1, P).T)


def layout(inputs):
    a = {n: np.asarray(inputs[n]) for n in inputs}
    arrays = {n: a[n][0] if n in _DROP_LAYER else a[n] for n in _IN}
    taps = lambda w: np.ascontiguousarray(w.reshape(w.shape[0], -1, P).transpose(2, 1, 0)).reshape(P, -1)
    heads = lambda v: np.concatenate([np.zeros(H, np.float32), v, np.zeros(P - 2 * H, np.float32)])[:, None]
    half = np.arange(P) % 32
    inv = (np.float32(10000.0) ** (-np.arange(0, 64, 2, dtype=np.float32) / np.float32(64))).astype(np.float32)
    vec = {"pre_mix": "pre_mix_norm", "q_norm": "q_norm", "kv_norm": "kv_norm", "conv_b": "conv_b",
           "conv_ln_g": "conv_ln_g", "conv_ln_b": "conv_ln_b", "conv_out": "conv_out_norm",
           "attn_out": "attn_out_norm", "post_mix": "post_mix_norm", "pre_ffn": "pre_ffn_norm",
           "post_ffn": "post_ffn_norm", "mix2": "mix_norm_g_2", "gdn_norm": "gdn_norm_g_2",
           "moba_norm": "moba_norm_g_2", "xattn": "xattn_norm_g_2", "mem": "mem_norm_g_2",
           "ffn2": "ffn_norm_g_2", "ffn_conv_b": "ffn_conv_b_2", "final": "final_norm_g_2"}
    parts = {k: _chunks(a[v]) for k, v in vec.items()}
    parts["conv_w"] = taps(a["conv_w"][0])
    parts["gdn_conv"] = taps(a["gdn_conv_w_2"][0])
    parts["ffn_conv"] = taps(a["ffn_conv_w_2"][0])
    parts["a_log"] = heads(a["gdn_a_log_2"][0])
    parts["dt_bias"] = heads(a["gdn_dt_bias_2"][0])
    parts["eps"] = np.full((P, 1), EPS, np.float32)
    parts["inv_freq"] = inv[half][:, None]
    for k, (_, n) in COLUMNS.items():
        assert parts[k].shape == (P, n), (k, parts[k].shape)
    arrays["cols"] = np.concatenate([parts[k] for k in COLUMNS], 1)
    arrays["xt"] = np.ascontiguousarray(a["x"][0].T.reshape(DC, P, T).transpose(1, 0, 2))
    arrays["mem"] = np.ascontiguousarray(a["mem_2"][0].T.reshape(DC, P, T).transpose(1, 0, 2))
    arrays.update(constants())
    return {n: np.ascontiguousarray(v) for n, v in arrays.items()}


def kernel(**inputs):
    import concourse.bacc as bacc
    from concourse.bass_utils import run_bass_kernel_spmd

    nc = bacc.Bacc("TRN2", target_bir_lowering=False, num_devices=1)
    arrays = {f"in_{n}": v for n, v in layout(inputs).items()}
    aps = {n[3:]: nc.dram_tensor(n, v.shape, mybir.dt.from_np(v.dtype), kind="ExternalInput").ap()
           for n, v in arrays.items()}
    out = nc.dram_tensor("out_t", [P, DC, T], F32, kind="ExternalOutput").ap()
    build(nc, aps, out)
    r = run_bass_kernel_spmd(nc, [arrays], core_ids=[0])
    y = r.results[0]["out_t"]
    return np.ascontiguousarray(y.transpose(1, 0, 2).reshape(D, T).T)[None]
```

```python
import math
from contextlib import ExitStack

import numpy as np
import concourse.bass as bass
from concourse import mybir

F32 = mybir.dt.float32
F32R = mybir.dt.float32r
I32 = mybir.dt.int32
ACT = mybir.ActivationFunctionType
ALU = mybir.AluOpType
AX = mybir.AxisListType

P = 128
T = 256
TT = T // P
D = 2048
DC = D // P
EPS = 1e-6
H = 8
XH = 4
FF = 5632
FC = FF // P
CONV_K = 31
CC = 8
GDN_K = 4
FFN_K = 3
BUCKETS = 32
MAX_DIST = 128
NEG = -1e30
W = 512
KC = 4
RAW = 4
HALF = 2
HIS = 4
KB = 1024


COLUMNS = {}
_at = 0
for _name, _n in [("pre_mix", 16), ("q_norm", 6), ("kv_norm", 4), ("conv_b", 8), ("conv_ln_g", 8),
                  ("conv_ln_b", 8), ("conv_out", 8), ("attn_out", 8), ("post_mix", 16), ("pre_ffn", 16),
                  ("post_ffn", 16), ("mix2", 16), ("gdn_norm", 1), ("moba_norm", 1), ("xattn", 16),
                  ("mem", 16), ("ffn2", 16), ("ffn_conv_b", 44), ("final", 16), ("conv_w", 8 * CONV_K),
                  ("gdn_conv", 24 * GDN_K), ("ffn_conv", 44 * FFN_K), ("a_log", 1), ("dt_bias", 1),
                  ("inv_freq", 1)]:
    COLUMNS[_name] = (_at, _n)
    _at += _n
NCOL = _at


def constants():
    c = {}
    c["ident"] = np.eye(P, dtype=np.float32)
    j, i = np.arange(P)[:, None], np.arange(P)[None, :]
    lv = [((j >> (l + 1)) == (i >> (l + 1))) & (((i >> l) & 1) == 1) & (((j >> l) & 1) == 0) for l in range(7)]
    c["masks"] = np.stack([m.astype(np.float32) for m in lv] + [(i >= j).astype(np.float32)], 1)
    rot = np.zeros((P, P), np.float32)
    dup = np.zeros((P, P), np.float32)
    for b in (0, 64):
        for k in range(32):
            rot[b + 32 + k, b + k] = -1.0
            rot[b + k, b + 32 + k] = 1.0
        for k in range(64):
            dup[64 + k, b + k] = 1.0
    c["rope_m"] = np.stack([rot, dup, dup @ rot], 1)
    q = np.arange(P)[:, None]
    c["causal"] = np.concatenate([np.where(np.arange(P)[None] <= q, 0.0, NEG),
                                  np.where(np.arange(T)[None] <= q + P, 0.0, NEG)], 1).astype(np.float32)
    n = np.arange(T)
    f32 = np.float32
    nf = np.maximum(n, 1).astype(f32)
    large = 16 + (np.log(nf / f32(16)) / f32(math.log(MAX_DIST / 16)) * f32(16)).astype(np.int32)
    bucket = np.where(n < 16, n, np.minimum(large, BUCKETS - 1))
    hot = np.zeros((BUCKETS, 384), np.float32)
    for e in range(T):
        hot[bucket[255 - e], e] = 1.0
    c["hot"] = hot
    neg = np.zeros((H, 384), np.float32)
    neg[:, T:] = NEG
    c["hot_neg"] = neg
    return c


class Gemm:

    def __init__(self, name, turns, groups, x, scale=None):
        self.name, self.turns, self.groups, self.x, self.scale = name, turns, groups, x, scale
        self.tiles = sum(g["tiles"] for g in groups)
        self.banks = sum(len(g["at"]) for g in groups)


class Milestones:

    def __init__(self, sem, names):
        self.sem, self.names, self.n = sem, names, 0

    def reach(self, ins, name):
        assert self.names[self.n] == name, (self.names[self.n], name)
        self.n += 1
        ins.then_inc(self.sem, 1)

    def wait(self, eng, name):
        eng.wait_ge(self.sem, self.names.index(name) + 1)


class Chain:

    def __init__(self, sem):
        self.sem, self.n = sem, 0

    def step(self, ins):
        self.n += 1
        ins.then_inc(self.sem, 1)

    def sync(self, eng):
        eng.wait_ge(self.sem, self.n)

    def link(self, eng, ins):
        self.step(ins)
        self.sync(eng)


def build(nc, A, out):
    with ExitStack() as ctx:
        def sem(name):
            return ctx.enter_context(nc.semaphore(name))

        base = (nc.sbuf_base + 31) // 32 * 32

        def sb(name, shape, dt=F32, at=None):
            return nc.alloc_sbuf_tensor_at(name, shape, dt, offset=at)

        top = [base]

        def room(nbytes):
            a = top[0]
            top[0] += (nbytes + 31) // 32 * 32
            assert top[0] <= nc.sbuf_usable_end, (top[0], nc.sbuf_usable_end)
            return a

        xt = sb("xt", [P, DC, T], F32, room(16 * KB))
        a_x2 = room(32 * KB)
        x2 = sb("x2", [P, DC, 2, T], F32R, a_x2)
        tx = sb("tx", [P, 32, T], F32, a_x2)
        a_raw = room(RAW * 8 * KB)
        w_raw = sb("w_raw", [P, RAW, KC, W], F32, a_raw)
        w_lo = sb("w_lo", [P, RAW, KC, W], F32R, a_raw)
        w_hi = sb("w_hi", [P, HIS, HALF, W], F32R, room(HIS * 4 * KB))
        a_ar = room(88 * KB)
        h2 = sb("h2", [P, FC, 2, T], F32R, a_ar)
        ar = sb("ar", [P, 88, T], F32, a_ar)
        cols = sb("cols", [P, NCOL], F32, room(4 * NCOL))
        ident = sb("ident_s", [P, P], F32, room(4 * P))
        ones = sb("ones", [P, P], F32, room(4 * P))
        half = sb("half", [P, 4, T], F32, room(4 * KB))
        a_gate, a_up = room(4 * KB), room(4 * KB)
        gate = sb("gate", [P, 4, T], F32, a_gate)
        up = sb("up", [P, 4, T], F32, a_up)
        rs_x = sb("rs_x", [P, T], F32, room(KB))
        ssq = sb("ssq", [P, 4, T], F32, room(4 * KB))
        st_y = sb("st_y", [P, T], F32, room(KB))
        st_v = sb("st_v", [P, T], F32, room(KB))
        small = sb("small", [P, 2, 64], F32, room(512))

        def col(name, k=0, n=1, rows=P):
            b, size = COLUMNS[name]
            return cols[0:rows, b + k:b + k + n]

        ps = ctx.enter_context(nc.psum_tensor("ps", [P, 8, W], F32))

        M1 = 0
        MEM = 57
        Z1 = 0
        U1, Q1, K1, V1, VN1, O1 = 27, 36, 48, 56, 64, 72
        KPE, COS, SIN = 80, 81, 82
        causal = sb("causal_s", [P, 384], F32, a_ar + 83 * KB)
        rope_m = sb("rope_s", [P, 3, P], F32, a_ar + 85 * KB)
        rs_kv = ar[:, 87, :]
        pos_i = sb("pos_i", [P, T], I32, a_ar + 72 * KB)
        ZA, ZZ, BA, ZB = 0, 24, 32, 33
        VN2, BI, O2B = 57, 65, 77
        bias2 = sb("bias2", [P, H, 384], F32, a_ar + BI * KB)
        RQK, RBETA, RG = 85, 86, 87
        KBG1, KDEC0, VB, AT, QK, UU, QDEC1, OG = 33, 37, 41, 49, 57, 65, 73, 41
        XK, XV, XVN, XQ, XO = 0, 4, 8, 12, 16
        XM = 20

        rel_hot = sb("rel_hot", [BUCKETS, 384], F32, a_gate)
        rel_neg = sb("rel_neg", [H, 384], F32, a_gate + 2 * KB)
        rel_b = sb("rel_b", [BUCKETS, H], F32, a_up)
        rel_e = sb("rel_e", [H, 384], F32, a_up + KB)
        masks = sb("masks_s", [P, 8, P], F32, a_x2 + 24 * KB)
        rel_d = nc.dram_tensor("rel_d", [H, 384], F32, kind="Internal").ap()
        rel_s = nc.dram_tensor("rel_s", [H, P, 384], F32, kind="Internal").ap()

        def w_cols(w, at, width):
            v = w.rearrange("(c p) n -> p c n", p=P)
            return lambda i, k0, kn: [(slice(0, kn), slice(0, width), v[:, k0:k0 + kn, at:at + width])]

        def w_loop(w, at, step=W):
            v = w.rearrange("(c p) n -> p c n", p=P)
            return lambda i, k0, kn: [(slice(0, kn), slice(0, W), v[:, k0:k0 + kn, bass.ds(i * step + at, W)])]

        def turned(src):
            return lambda i, k0, kn: src(i, (k0 + DC // 2) % DC, kn)

        def w_heads(w, per, h0, n, off, width):
            v = w.rearrange("(c p) (h d) -> p c h d", p=P, d=per)
            return lambda i, k0, kn: [
                (k, slice(0, n * width), v[:, k0 + k, h0:h0 + n, off:off + width]) for k in range(kn)]

        FULL = [0, 128, 256, 384]

        def group(src, tiles, kc=KC, at=FULL, banks=0, out=None, kind="z", parts=1):
            return dict(src=src, tiles=tiles, kc=kc, at=at, banks=banks, out=out, kind=kind, parts=parts)

        def group_of(g, j):
            for gr in g.groups:
                if gr["t"] <= j < gr["t"] + gr["tiles"]:
                    return gr, j - gr["t"]

        def gr_parts(g, j):
            return group_of(g, j)[0]["parts"]

        def slot(g, j):
            return (j + g.shift) % RAW

        def x2c(k):
            return x2[:, k], x2[:, k, 0, :]

        def h2c(k):
            return h2[:, k], h2[:, k, 0, :]

        GEMMS = [
            Gemm("conv_in", 1, [group(w_cols(A["w_in"], c, W), 4, banks=b, out=(ar, Z1 + c // P, 0))
                                for b, c in ((0, 0), (4, 1024), (0, 512), (4, 1536))], x2c, rs_x),
            Gemm("latents", 1, [group(w_cols(A["w_in"], 2048, W), 4, out=(ar, Z1 + 16, 0)),
                                group(w_cols(A["w_in"], 2560, W), 4, banks=4, out=(ar, Z1 + 20, 0)),
                                group(w_cols(A["w_in"], 3072, 320), 4, at=[0, 128, 192], out=(ar, Z1 + 24, 0))],
                 x2c, rs_x),
            Gemm("uq", 1, [group(w_heads(A["w_uq"], 192, h0, n, off, width), 2, 3, banks=4 * (at == 4), out=(ar, Q1 + at, 0), parts=3)
                           for h0, n, off, width, at in ((0, 4, 0, 128, 0), (4, 4, 0, 128, 4), (0, 8, 128, 64, 8))],
                 x2c, rs_x),
            Gemm("ukv", 1, [group(w_heads(A["w_ukv"], 256, h0, 4, off, 128), 1, banks=b, out=(ar, at + h0, 0), parts=4)
                            for b, h0, off, at in ((4, 0, 0, K1), (0, 4, 0, K1), (4, 0, 128, V1), (0, 4, 128, V1))],
                 lambda k: x2c(6 + k), rs_kv),
            Gemm("w_out", 2, [group(w_loop(A["w_out"], 0 + b * P, 2 * W), 4, banks=b, out=(ar, M1 + b, 8), kind="sum")
                        for b in (0, 4)], x2c),
            Gemm("ffn", 11, [group(w_loop(A["w_gate"], 0), 4, kind="gate"),
                             group(w_loop(A["w_up"], 0), 4, banks=4, kind="up")], x2c, rs_x),
            Gemm("down", 2, [group(w_loop(A["w_down"], 0, 1024), 11, out=(tx, 16, 8), kind="sum"),
                             group(w_loop(A["w_down"], 512, 1024), 11, banks=4, out=(tx, 20, 8), kind="sum")], h2c),
            Gemm("qkv_a", 3, [group(w_loop(A["w_in_2"], 0 + b * P, 2 * W), 4, banks=b, out=(ar, ZA + b, 8))
                        for b in (0, 4)], x2c, rs_x),
            Gemm("z_ba", 1, [group(w_cols(A["w_in_2"], 3072, W), 4, out=(ar, ZZ, 0)),
                             group(w_cols(A["w_in_2"], 3584, W), 4, banks=4, out=(ar, ZZ + 4, 0)),
                             group(w_cols(A["w_in_2"], 4096, 128), 4, at=[0], out=(ar, BA, 0))], x2c, rs_x),
            Gemm("qkv_b", 3, [group(w_loop(A["w_in_2"], 4112 + b * P, 2 * W), 4, banks=b, out=(ar, ZB + b, 8))
                        for b in (0, 4)], x2c, rs_x),
            Gemm("w_out_2", 2, [group(turned(w_loop(A["w_out_2"], b * P, 2 * W)), 4, banks=b, out=(xt, 0 + b, 8), kind="add")
                        for b in (0, 4)], lambda k: x2c((k + 8) % DC)),
            Gemm("xkv", 1, [group(w_cols(A["w_xkv_2"], b * P, W), 4, banks=b, out=(ar, XK + b, 0)) for b in (0, 4)], x2c, rs_x),
            Gemm("xq", 1, [group(w_cols(A["w_xq_2"], 0, W), 4, out=(ar, XQ, 0))], x2c, rs_x),
            Gemm("xo", 1, [group(w_cols(A["w_xo_2"], 512 * n, W), 1, banks=4 * (n % 2), out=(xt, 4 * n, 0), kind="add")
                           for n in range(4)], x2c),
            Gemm("ffn_2", 11, [group(w_loop(A["w_gate_2"], 0), 4, kind="gate2"),
                               group(w_loop(A["w_up_2"], 0), 4, banks=4, kind="up")], x2c, rs_x),
            Gemm("down_2", 2, [group(w_loop(A["w_down_2"], 0, 1024), 11, out=(xt, 0, 8), kind="add"),
                               group(w_loop(A["w_down_2"], 512, 1024), 11, banks=4, out=(xt, 4, 8), kind="add")], h2c),
        ]
        G = {g.name: g for g in GEMMS}
        tiles = prods = banks = groups = hidden = 0
        slots = [0] * RAW
        for n, g in enumerate(GEMMS):
            g.before = GEMMS[n - 1] if n else None
            g.u0, g.p0, g.e0, g.g0, g.f0, g.slot0 = tiles, prods, banks, groups, hidden, list(slots)
            at = bank = 0
            g.per_unit = []
            for k, gr in enumerate(g.groups):
                gr["t"], gr["e"], gr["n"] = at, bank, k
                at += gr["tiles"]
                bank += len(gr["at"])
                g.per_unit += [len(gr["at"])] * (2 * gr["tiles"])
            g.units = 2 * g.tiles
            g.shift = (g.before.shift + g.before.tiles) % RAW if n else 0
            g.products = sum(g.per_unit)
            g.slot_per = [sum(gr_parts(g, j) for j in range(g.tiles) if slot(g, j) == s) for s in range(RAW)]
            slots = [a + g.turns * b for a, b in zip(slots, g.slot_per)]
            tiles += g.turns * 2 * g.tiles
            prods += g.turns * g.products
            banks += g.turns * g.banks
            groups += g.turns * len([gr for gr in g.groups if gr["kind"] in ("z", "gate2")])
            hidden += g.turns if g.name.startswith("ffn") else 0

        w_loaded = [sem(f"w_loaded{s}") for s in range(RAW)]
        hi_done = sem("hi_done")
        lo_done = sem("lo_done")
        products = sem("products")
        half_out = sem("half_out")
        bank_free = sem("bank_free")
        group_out = sem("group_out")
        gate_act = sem("gate_act")
        hid_hi = sem("hid_hi")
        hid_pre = sem("hid_pre")
        hid_lo = sem("hid_lo")
        add_half = sem("add_half")
        tap_done = sem("tap_done")
        AHEAD_P, AHEAD_B = 2 * RAW * 4, 8

        def landed(g, i, j):
            s = slot(g, j)
            n = sum(gr_parts(g, k) for k in range(j + 1) if slot(g, k) == s)
            return 16 * (g.slot0[s] + n) + i * (16 * g.slot_per[s])

        def first_turn(i):
            return isinstance(i, int) and i == 0

        def used(g, i, u, lag):
            own = g.per_unit[:u]
            if lag <= u:
                back = sum(own[u - lag + 1:])
            else:
                tail = g.before.per_unit if g.before and first_turn(i) else g.per_unit
                back = sum((tail + own)[len(tail) + u - lag + 1:])
            return AHEAD_P + g.p0 + sum(own) - back + i * g.products

        def slot_lag(g, i, j):
            if j >= RAW or not g.before:
                return RAW
            last = g.before if first_turn(i) else g
            return j + last.tiles - max(k for k in range(last.tiles) if slot(last, k) == slot(g, j))

        def load(sp, g):
            def body(i):
                for j in range(g.tiles):
                    gr, jj = group_of(g, j)
                    sp.wait_ge(products, used(g, i, 2 * j, 2 * slot_lag(g, i, j) - 1))
                    for ks, cs, src in gr["src"](i, jj * gr["kc"], gr["kc"]):
                        sp.dma_start(w_raw[:, slot(g, j), ks, cs], src).then_inc(w_loaded[slot(g, j)], 16)
            body(0)
            if g.turns > 1:
                with sp.Fori(1, g.turns) as i:
                    body(i)

        def unit(g, u):
            gr, _ = group_of(g, u // 2)
            return gr, u // 2, slice(HALF * (u % 2), HALF if u % 2 == 0 else gr["kc"]), slice(0, gr["at"][-1] + P)

        def split_act(act, g, i, u):
            _, j, ks, cs = unit(g, u)
            if u % 2 == 0:
                act.wait_ge(w_loaded[slot(g, j)], landed(g, i, j))
            act.wait_ge(products, used(g, i, u, HIS))
            nc.scalar.activation(w_hi[:, u % HIS, 0:ks.stop - ks.start, cs], w_raw[:, slot(g, j), ks, cs], ACT.Copy)\
                .then_inc(hi_done, 1)

        def split_dve(dve, g, i, u):
            _, j, ks, cs = unit(g, u)
            dve.wait_ge(hi_done, g.u0 + u + 1 + i * g.units)
            nc.vector.tensor_tensor(w_lo[:, slot(g, j), ks, cs], w_raw[:, slot(g, j), ks, cs],
                                    w_hi[:, u % HIS, 0:ks.stop - ks.start, cs].bitcast(F32), ALU.subtract)\
                .then_inc(lo_done, 1)

        def evict_act(act, g, i, gr):
            e = g.e0 + gr["e"] + i * g.banks
            M = len(gr["at"])
            act.wait_ge(bank_free, AHEAD_B + e)
            last = AHEAD_P + g.p0 + sum(g.per_unit[:2 * (gr["t"] + gr["tiles"]) - 1]) + i * g.products
            for m in range(M):
                act.wait_ge(products, last + m + 1)
                nc.scalar.activation(half[:, m, :], ps[:, gr["banks"] + m, 0:T], ACT.Copy).then_inc(half_out, 1)
            f = g.f0 + i
            yield
            if g.name in STREAM_STAT:
                act.wait_ge(bank_free, AHEAD_B + e + M)
                k = STATS[STREAM_STAT[g.name]][1] + gr["n"] + i * len(g.groups)
                act.wait_ge(summed, k - 1)
                where, base_c, step = gr["out"]
                nc.scalar.activation(sq_buf[gr["n"] % 2][:], chunk(where, base_c, step, i, M), ACT.Square)\
                    .then_inc(squares, 1)
            if gr["kind"] == "gate":
                yield
                act.wait_ge(hid_pre, 3 * f + 1)
                nc.scalar.activation(gate[:], gate[:], ACT.Silu).then_inc(gate_act, 1)
            if gr["kind"] == "gate2":
                for _ in range(3):
                    yield
                act.wait_ge(hid_pre, 3 * f + 1)
                for m in range(4):
                    nc.scalar.activation(gate[:, m, :], conv_y[:, m, :], ACT.Silu,
                                         bias=cols[:, bass.ds(i * 4 + (COLUMNS["ffn_conv_b"][0] + m), 1)])\
                        .then_inc(gate_act, 1)
            if gr["kind"] == "up":
                yield
                yield
                act.wait_ge(hid_pre, 3 * f + 3)
                nc.scalar.activation(h2[:, bass.ds(i * 4, 4), 0, :] if not isinstance(i, int) else h2[:, 4 * i:4 * i + 4, 0, :], up[:], ACT.Copy).then_inc(hid_hi, 1)

        def evict_dve(dve, g, i, gr):
            e = g.e0 + gr["e"] + i * g.banks
            M = len(gr["at"])
            f = g.f0 + i
            kind = gr["kind"]
            if kind == "add":
                _, base_c, step = gr["out"]
                xc = lambda m: chunk(xt, base_c + m, step, i)
                for m in range(M):
                    dve.wait_ge(half_out, e + m + 1)
                    nc.vector.tensor_tensor(xc(m), xc(m), ps[:, gr["banks"] + m, T:2 * T], ALU.add)\
                        .then_inc(add_half, 1)
                a0 = g.a0 + gr["e"] + i * g.banks
                for m in range(M):
                    dve.wait_ge(add_half, a0 + m + 1)
                    nc.vector.tensor_tensor(xc(m), xc(m), half[:, m, :], ALU.add).then_inc(bank_free, 1)
                if g.name in STREAM_STAT:
                    yield
                    yield
                    reduce_group(dve, g, i, gr)
                return
            if kind in ("gate", "gate2"):
                dve.wait_ge(hid_hi, f)
                dst, whole = (lambda m: gate[:, m, :]), gate[:]
            elif kind == "up":
                dst, whole = (lambda m: up[:, m, :]), up[:]
            else:
                where, base_c, step = gr["out"]
                dst = lambda m: chunk(where, base_c + m, step, i)
                whole = chunk(where, base_c, step, i, M)
            for m in range(M):
                dve.wait_ge(half_out, e + m + 1)
                nc.vector.tensor_tensor(dst(m), half[:, m, :], ps[:, gr["banks"] + m, T:2 * T], ALU.add)\
                    .then_inc(bank_free, 1)
            if kind == "sum":
                yield
                yield
                reduce_group(dve, g, i, gr)
                return
            yield
            dve.wait_ge(bank_free, AHEAD_B + e + M)
            if kind == "z":
                nc.vector.tensor_tensor(whole, whole, bc(g.scale, M), ALU.mult)\
                    .then_inc(group_out, 1)
            elif kind == "gate":
                nc.vector.tensor_tensor(gate[:], gate[:], bc(rs_x, 4), ALU.mult).then_inc(hid_pre, 1)
            elif kind == "gate2":
                nc.vector.tensor_tensor(gate[:], gate[:], bc(rs_x, 4), ALU.mult).then_inc(group_out, 1)
                dve.wait_ge(group_out, g.g0 + 1 + i)
                first_w = COLUMNS["ffn_conv"][0]
                for s in range(FFN_K):
                    for m in range(4):
                        w = cols[:, bass.ds(i * (4 * FFN_K) + (first_w + m * FFN_K + FFN_K - 1 - s), 1)]
                        if s == 0:
                            nc.vector.tensor_scalar(conv_y[:, m, :], gate[:, m, :], w, None, ALU.mult)\
                                .then_inc(tap_done, 1)
                        elif s < FFN_K - 1 or m < 3:
                            nc.vector.scalar_tensor_tensor(
                                conv_y[:, m, s:T], gate[:, m, 0:T - s], w, conv_y[:, m, s:T], ALU.mult, ALU.add)\
                                .then_inc(tap_done, 1)
                        else:
                            dve.wait_ge(tap_done, 4 * FFN_K - 1 + i * (4 * FFN_K - 1))
                            nc.vector.scalar_tensor_tensor(
                                conv_y[:, m, s:T], gate[:, m, 0:T - s], w, conv_y[:, m, s:T], ALU.mult, ALU.add)\
                                .then_inc(hid_pre, 1)
                    if s < FFN_K - 1:
                        yield
                        dve.wait_ge(tap_done, 4 * (s + 1) + i * (4 * FFN_K - 1))
            elif kind == "up":
                nc.vector.tensor_tensor(up[:], up[:], bc(rs_x, 4), ALU.mult).then_inc(hid_pre, 1)
                yield
                dve.wait_ge(hid_pre, 3 * f + 2)
                dve.wait_ge(gate_act, f + 1 if g.name == "ffn" else g.f0 + 4 * i + 4)
                nc.vector.tensor_tensor(up[:], up[:], gate[:], ALU.mult).then_inc(hid_pre, 1)
                yield
                yield
                dve.wait_ge(hid_hi, f + 1)
                for m in range(4):
                    nc.vector.tensor_tensor(chunk(h2[:, :, 1, :], m, 4, i), up[:, m, :],
                                            chunk(h2[:, :, 0, :], m, 4, i).bitcast(F32),
                                            ALU.subtract).then_inc(hid_lo, 1)

        def reduce_group(dve, g, i, gr):
            name = STREAM_STAT[g.name]
            dve.wait_ge(squares, squares_before(name) + gr["n"] + i * len(g.groups) + 1)
            dve.wait_ge(st_sum, STATS[name][0])
            nc.vector.tensor_reduce(chunk(ssq, gr["n"], len(g.groups), i),
                                    sq_buf[gr["n"] % 2][:].rearrange("p c t -> p t c"), AX.X, ALU.add)\
                .then_inc(summed, 1)

        def chunk(where, first, step, i, n=None):
            if isinstance(i, int):
                c = first + i * step
                return where[:, c, :] if n is None else where[:, c:c + n, :]
            c = bass.ds(i * step + first, n or 1)
            return where[:, c, :].rearrange("p a n -> p (a n)") if n is None else where[:, c, :]


        def bc(v, n):
            return (v if isinstance(v, bass.AP) else v[:]).unsqueeze(1).to_broadcast([P, n, T]) if n > 1 else (v if isinstance(v, bass.AP) else v[:]).unsqueeze(1)

        FIRST = 3

        def finish(steps):
            for _ in steps:
                pass

        def ahead(eng, split, evict, g, between=None):
            for u in range(FIRST):
                split(eng, g, 0, u)
            if between:
                between()
            if g.before:
                finish(evict(eng, g.before, g.before.turns - 1, g.before.groups[-1]))
            split(eng, g, 0, FIRST)

        def turn(eng, split, evict, g, i, steps=None, first=0, filler=None, fill_from=0, at=None):
            for k, gr in enumerate(g.groups):
                if k:
                    steps = evict(eng, g, i, g.groups[k - 1])
                for n in range(2 * gr["tiles"]):
                    u = 2 * gr["t"] + n
                    if u < first:
                        continue
                    split(eng, g, i, u)
                    if n >= FIRST - 1 and steps:
                        next(steps, None)
                    if filler and k >= fill_from:
                        next(filler, None)
                    if at and at[0] == u:
                        at[1]()
                if steps:
                    finish(steps)
                steps = None

        def run(eng, split, evict, g, filler=None, fill_from=0, at=None):
            turn(eng, split, evict, g, 0, None, FIRST + 1, filler, fill_from, at)
            if filler and g.turns > 1:
                finish(filler)
            if g.turns > 1:
                with eng.Fori(1, g.turns) as i:
                    turn(eng, split, evict, g, i, evict(eng, g, i - 1, g.groups[-1]))

        def multiply(pe, g, *stats, between=None):
            before = g.before.groups[-1] if g.before else None
            kept = len(before["at"]) if before and before["banks"] != g.groups[0]["banks"] else 0
            pe.wait_ge(bank_free, AHEAD_B + g.e0 - (0 if stats else kept))

            def body(i, first=0, last=g.units):
                for u in range(first, last):
                    gr, j, ks, _ = unit(g, u)
                    n, jj = u - 2 * gr["t"], j - gr["t"]
                    final = n == 2 * gr["tiles"] - 1
                    pe.wait_ge(lo_done, g.u0 + u + 1 + i * g.units)
                    pe.wait_ge(*g.needs(jj * gr["kc"] + ks.stop))
                    if stats and first_turn(i) and gr["banks"] == 4 and n == 0 and u > FIRST:
                        pe.wait_ge(st_done, STATS[stats[-1]][0] + 1)
                    for m, c0 in enumerate(gr["at"]):
                        if n == 0 and (g.turns > 1 or gr["n"] or kept):
                            lag = bank_lag(g, gr, kept)
                            if lag is not None:
                                pe.wait_ge(bank_free, AHEAD_B + g.e0 + gr["e"] + m + 1 - lag + i * g.banks)
                        bank = ps[:, gr["banks"] + m, :]
                        for k in range(ks.start, ks.stop):
                            both, hi = g.x(jj * gr["kc"] + k)
                            nc.tensor.matmul(bank, w_hi[:, u % HIS, k - ks.start, c0:c0 + P],
                                             both.rearrange("p a n -> p (a n)"),
                                             start=(n == 0 and k == 0), stop=False)
                            ins = nc.tensor.matmul(bank[:, T:2 * T], w_lo[:, slot(g, j), k, c0:c0 + P], hi,
                                                   start=False, stop=(final and k == ks.stop - 1))
                        ins.then_inc(products, 1)

            if stats:
                between = (FIRST + 1, lambda: [sum_pe(pe, name) for name in stats])
            if between:
                at, extra = between
                body(0, 0, at)
                extra()
                body(0, at)
                if g.turns > 1:
                    with pe.Fori(1, g.turns) as i:
                        body(i)
            elif g.turns == 1:
                body(0)
            else:
                with pe.Fori(0, g.turns) as i:
                    body(i)

        def bank_lag(g, gr, kept):
            order = ([x for x in g.groups] if g.turns > 1 else []) + g.groups[:gr["n"]]
            lag = 0
            for x in reversed(order):
                lag += len(x["at"])
                if x["banks"] == gr["banks"]:
                    return lag
            return lag + kept if kept and gr["banks"] != g.groups[0]["banks"] else None

        STATS = {}
        for name, parts in [("x", 4), ("q", 2), ("kv", 1), ("mean", 2), ("ln", 2), ("conv", 2), ("attn", 2),
                            ("mix", 4), ("ffn", 4), ("ff", 4), ("mix2", 4), ("mem", 4), ("xq", 4),
                            ("ffn2", 4), ("final", 4)]:
            before = list(STATS.values())
            STATS[name] = (len(before), sum(p for _, _, p in before), parts)
        PREPS = {}
        for name, n, first in [("x", 16, 0), ("q", 6, 0), ("kv", 4, 6), ("conv", 8, 0), ("attn", 8, 8),
                               ("ffn", 16, 0), ("mix2", 16, 0), ("moba", 8, 8), ("gdn", 8, 0), ("mem", 16, 0),
                               ("xq", 16, 0), ("xo", 4, 0), ("ffn2", 16, 0)]:
            PREPS[name] = (sum(c for _, c, _ in PREPS.values()), n, first)

        x_hi, x_lo = sem("x_hi"), sem("x_lo")
        squares = sem("squares")
        summed = sem("summed")
        st_sum = sem("st_sum")
        st_var = sem("st_var")
        st_root = sem("st_root")
        st_done = sem("st_done")
        xt_loaded = [sem(f"xt_loaded{k}") for k in range(4)]
        cols_loaded, aux_loaded = sem("cols_loaded"), sem("aux_loaded")
        sq_buf = [gate, up]
        STREAM_STAT = {"w_out": "mix", "down": "ff", "down_2": "final"}
        conv_y = ssq

        def needs_of(*names):
            total = sum(PREPS[n][1] for n in names)
            off = PREPS[names[0]][0]
            return lambda k: (x_lo, off + min(k, total))

        for name, preps in [("conv_in", ["x"]), ("latents", ["x"]), ("uq", ["q"]), ("ukv", ["kv"]),
                            ("w_out", ["conv", "attn"]), ("ffn", ["ffn"]), ("qkv_a", ["mix2"]), ("z_ba", ["mix2"]),
                            ("qkv_b", ["mix2"]), ("w_out_2", ["moba", "gdn"]), ("xkv", ["mem"]), ("xq", ["xq"]),
                            ("xo", ["xo"]), ("ffn_2", ["ffn2"])]:
            G[name].needs = needs_of(*preps)
        G["down"].needs = lambda k: (hid_lo, k)
        G["down_2"].needs = lambda k: (hid_lo, FC + k)
        adds = 0
        for g in GEMMS:
            g.a0 = adds
            adds += g.turns * g.banks if g.groups[0]["kind"] == "add" else 0

        def prep_act(act, name, src, gain, ready=None, square=None, after=None):
            off, n, first = PREPS[name]
            if after:
                act.wait_ge(products, AHEAD_P + G[after].p0 + G[after].turns * G[after].products)
            for c in range(n):
                if ready:
                    act.wait_ge(*ready(c))
                if gain is None:
                    ins = nc.scalar.activation(x2[:, first + c, 0, :], src(c), ACT.Copy)
                else:
                    ins = nc.scalar.activation(x2[:, first + c, 0, :], src(c), ACT.Copy,
                                               scale=gain(c))
                ins.then_inc(x_hi, 1)
                if square and (c % 4 == 3 or c == n - 1):
                    square_act(act, square, c // 4, src, c - c // 4 * 4 + 1)

        def prep_dve(dve, name, src, gain, square=None, c0=0, count=None):
            off, n, first = PREPS[name]
            for c in range(c0, c0 + (count or n)):
                dve.wait_ge(x_hi, off + c + 1)
                hi = x2[:, first + c, 0, :].bitcast(F32)
                if gain is None:
                    ins = nc.vector.tensor_tensor(x2[:, first + c, 1, :], src(c), hi, ALU.subtract)
                else:
                    ins = nc.vector.scalar_tensor_tensor(x2[:, first + c, 1, :], src(c), gain(c), hi,
                                                         ALU.mult, ALU.subtract)
                ins.then_inc(x_lo, 1)
                if square and (c % 4 == 3 or c == n - 1):
                    reduce_dve(dve, square, c // 4, c - c // 4 * 4 + 1)

        def square_act(act, name, k, src, n, ready=None):
            _, before, _ = STATS[name]
            if before + k - 1 > 0:
                act.wait_ge(summed, before + max(0, k - 1))
            if ready:
                act.wait_ge(*ready(4 * k + n - 1))
            nc.scalar.activation(sq_buf[k % 2][:, 0:n, :], span(src, 4 * k, n), ACT.Square).then_inc(squares, 1)

        def span(src, c, n):
            return src.whole[:, src.first + c:src.first + c + n, :]

        def reduce_dve(dve, name, k, n, src=None):
            r, before, _ = STATS[name]
            if src is None:
                dve.wait_ge(squares, squares_before(name) + k + 1)
                view = sq_buf[k % 2][:, 0:n, :]
            else:
                view = span(src, 4 * k, n)
            if k == 0 and r:
                dve.wait_ge(st_sum, r - (name == "kv"))
            nc.vector.tensor_reduce(ssq[:, SUM_AT.get(name, 0) + k, :], view.rearrange("p c t -> p t c"), AX.X, ALU.add)\
                .then_inc(summed, 1)

        def squares_before(name):
            return STATS[name][1] - (STATS["mean"][2] if STATS[name][0] > STATS["mean"][0] else 0)

        SUM_AT = {"kv": 2}
        SUM_BANK = {name: 3 if name in ("mean", "ln", "conv") else 7 for name in STATS}

        def sum_pe(pe, name):
            r, before, parts = STATS[name]
            out = ps[:, SUM_BANK[name], 0:T]
            if r:
                pe.wait_ge(st_done, r)
            pe.wait_ge(summed, before + parts)
            for k in range(parts):
                last = nc.tensor.matmul(out, ones[:], ssq[:, SUM_AT.get(name, 0) + k, :], start=(k == 0), stop=(k == parts - 1))
            last.then_inc(st_sum, 1)

        def root_act(act, name, n, rows=P):
            r = STATS[name][0]
            if name == "mean":
                act.wait_ge(st_sum, r + 1)
                nc.scalar.activation(st_y[:], ps[:, SUM_BANK[name], 0:T], ACT.Copy, scale=1.0 / n).then_inc(st_root, 1)
                return
            act.wait_ge(st_var, roots_before(name) + 1)
            act_chain.link(act, nc.scalar.activation(st_y[:], st_v[:], ACT.Ln))
            nc.scalar.activation(st_y[:], st_y[:], ACT.Exp, scale=-0.5).then_inc(st_root, 1)

        def roots_before(name):
            r = STATS[name][0]
            return r - (r > STATS["mean"][0])

        def refine_dve(dve, name, n, dst):
            r = STATS[name][0]
            dve.wait_ge(st_sum, r + 1)
            nc.vector.tensor_scalar(st_v[:], ps[:, SUM_BANK[name], 0:T], 1.0 / n, EPS, ALU.mult, ALU.add).then_inc(st_var, 1)
            dve.wait_ge(st_root, r + 1)
            for _ in range(2):
                dve_chain.link(dve, nc.vector.tensor_tensor(st_v[:], st_v[:], st_y[:], ALU.mult))
            dve_chain.link(dve, nc.vector.tensor_scalar(st_v[:], st_v[:], -0.5, 1.5, ALU.mult, ALU.add))
            nc.vector.tensor_tensor(dst, st_v[:], st_y[:], ALU.mult).then_inc(st_done, 1)
            dve.wait_ge(st_done, r + 1)

        act_chain = Chain(sem("act_chain"))
        dve_chain = Chain(sem("dve_chain"))

        def source(whole, first):
            f = lambda c: whole[:, first + c, :]
            f.whole, f.first = whole, first
            return f

        def gain_of(name):
            return lambda c: col(name, c)

        def banks_out(name):
            g = G[name]
            return lambda c: (bank_free, AHEAD_B + g.e0 + c + 1)

        xs = source(xt, 0)

        rope = Milestones(sem("rope_v"), ["f", "ang", "t", "n", "r1", "r2", "r3", "c1", "c2", "c3", "s2"])
        rope_s = Milestones(sem("rope_s"), ["sin", "cos"])
        rope_t = Milestones(sem("rope_t"), ["rot"])
        rope_o = Milestones(sem("rope_o"), ["qs", "ks", "qc", "kc", "q", "k"])
        ang, tmp_n, tmp_r, tmp_c = (ar[:, 73 + k, :] for k in range(4))
        PI = 3.1415925
        C1, C2 = 6.28125, 0.0019350051879882812
        C3 = 2 * math.pi - C1 - C2

        def rope_tables_dve(dve):
            dve.wait_ge(aux_loaded, 16 * N_AUX)
            rope.reach(nc.vector.tensor_copy(tmp_r, pos_i[:]), "f")
            rope.wait(dve, "f")
            rope.reach(nc.vector.tensor_scalar(ang, tmp_r, col("inv_freq"), None, ALU.mult), "ang")
            rope.wait(dve, "ang")
            rope.reach(nc.vector.tensor_scalar(tmp_n, ang, 1 / (2 * math.pi), 12582912.0, ALU.mult, ALU.add), "t")
            rope.wait(dve, "t")
            rope.reach(nc.vector.tensor_scalar(tmp_n, tmp_n, -12582912.0, None, ALU.add), "n")
            rope.wait(dve, "n")
            for k, c in enumerate((C1, C2, C3)):
                rope.reach(nc.vector.scalar_tensor_tensor(tmp_r, tmp_n, -c, ang if k == 0 else tmp_r,
                                                          ALU.mult, ALU.add), f"r{k + 1}")
                rope.wait(dve, f"r{k + 1}")
            rope.reach(nc.vector.tensor_scalar(tmp_c, tmp_r, math.pi / 2, None, ALU.add), "c1")
            rope.wait(dve, "c1")
            rope.reach(nc.vector.tensor_scalar(tmp_n, tmp_c, math.pi, -2 * math.pi, ALU.is_gt, ALU.mult), "c2")
            rope.wait(dve, "c2")
            rope.reach(nc.vector.tensor_tensor(tmp_c, tmp_c, tmp_n, ALU.add), "c3")
            rope.wait(dve, "c3")
            dve_chain.link(dve, nc.vector.tensor_scalar(tmp_c, tmp_c, PI, -PI, ALU.min, ALU.max))
            rope.reach(nc.vector.tensor_scalar(tmp_r, tmp_r, PI, -PI, ALU.min, ALU.max), "s2")

        def rope_tables_act(act):
            rope.wait(act, "s2")
            act.wait_ge(dve_chain.sem, 1)
            rope_s.reach(nc.scalar.activation(ar[:, SIN, :], tmp_r, ACT.Sin), "sin")
            rope_s.reach(nc.scalar.activation(ar[:, COS, :], tmp_c, ACT.Sin), "cos")

        def rope_pe(pe):
            pe.wait_ge(bank_free, AHEAD_B + G["w_out"].e0)
            for c in range(4):
                nc.tensor.matmul(ps[:, 4 + c, 0:T], rope_m[:, 0, :], ar[:, Q1 + 8 + c, :], start=True, stop=True)
            for k in range(2):
                last = nc.tensor.matmul(ps[:, 4 + k, T:2 * T], rope_m[:, 1 + k, :], ar[:, Z1 + 26, :],
                                        start=True, stop=True)
            rope_t.reach(last, "rot")

        def rope_dve(dve):
            rope_s.wait(dve, "cos")
            rope_t.wait(dve, "rot")
            q = ar[:, Q1 + 8:Q1 + 12, :]
            rope_o.reach(nc.vector.tensor_tensor(ar[:, 8:12, :], ps[:, 4:8, 0:T], bc(ar[:, SIN, :], 4), ALU.mult), "qs")
            rope_o.reach(nc.vector.tensor_tensor(ar[:, 12, :], ps[:, 5, T:2 * T], ar[:, SIN, :], ALU.mult), "ks")
            rope_o.reach(nc.vector.tensor_tensor(q, q, bc(ar[:, COS, :], 4), ALU.mult), "qc")
            rope_o.reach(nc.vector.tensor_tensor(ar[:, KPE, :], ps[:, 4, T:2 * T], ar[:, COS, :], ALU.mult), "kc")
            rope_o.wait(dve, "kc")
            rope_o.reach(nc.vector.tensor_tensor(q, q, ar[:, 8:12, :], ALU.add), "q")
            rope_o.reach(nc.vector.tensor_tensor(ar[:, KPE, :], ar[:, KPE, :], ar[:, 12, :], ALU.add), "k")

        u_sig, u_done, tap1 = sem("u_sig"), sem("u_done"), sem("tap1")

        def glu_act(act, k):
            g = G["conv_in"]
            act.wait_ge(group_out, g.g0 + 2 * k + 2)
            v = ar[:, Z1 + 8 + 4 * k:Z1 + 12 + 4 * k, :]
            nc.scalar.activation(v, v, ACT.Sigmoid).then_inc(u_sig, 1)
            yield

        def conv_steps(dve):
            for k in range(2):
                dve.wait_ge(u_sig, k + 1)
                nc.vector.tensor_tensor(ar[:, U1 + 4 * k:U1 + 4 * k + 4, :], ar[:, Z1 + 4 * k:Z1 + 4 * k + 4, :],
                                        ar[:, Z1 + 8 + 4 * k:Z1 + 12 + 4 * k, :], ALU.mult).then_inc(u_done, 1)
                dve.wait_ge(u_done, k + 1)
                yield
                mine = range(4 * k, min(4 * k + 4, CV))
                for s in range(CONV_K):
                    if s:
                        dve.wait_ge(tap1, 4 * k * CONV_K + len(mine) * s)
                    for c in mine:
                        y, u = ar[:, Z1 + c, :], ar[:, U1 + c, :]
                        w = col("conv_w", c * CONV_K + CONV_K - 1 - s)
                        if s == 0:
                            nc.vector.tensor_scalar(y, u, w, col("conv_b", c), ALU.mult, ALU.add).then_inc(tap1, 1)
                        else:
                            nc.vector.scalar_tensor_tensor(y[:, s:T], u[:, 0:T - s], w, y[:, s:T],
                                                           ALU.mult, ALU.add).then_inc(tap1, 1)
                    yield

        CV = CC - 2
        diag = tx[:].rearrange("p c t -> p (c t)").rearrange("p (n k) -> p n k", k=P)
        diag_done, conv_pe = sem("diag_done"), sem("conv_pe")

        def diag_act(act):
            act.wait_ge(products, AHEAD_P + G["w_out"].p0)
            act.wait_ge(aux_loaded, 16 * N_AUX)
            for c in range(CV, CC):
                for s in range(CONV_K):
                    nc.scalar.activation(diag[:, (c - CV) * CONV_K + s, :], ident[:], ACT.Copy,
                                         scale=col("conv_w", c * CONV_K + CONV_K - 1 - s)).then_inc(diag_done, 1)

        def long_conv_pe(pe):
            pe.wait_ge(u_done, 2)
            for c in range(CV, CC):
                for s in range(CONV_K):
                    n = (c - CV) * CONV_K + s
                    pe.wait_ge(diag_done, n + 1)
                    last = nc.tensor.matmul(ps[:, c - CV, s:T], diag[:, n, :], ar[:, U1 + c, 0:T - s],
                                            start=(s == 0), stop=(s == CONV_K - 1))
            last.then_inc(conv_pe, 1)

        class Attention:

            def __init__(self, name, first, heads, q, k, v, vn, dst, scale, s_buf, pt_buf, widths, bias, pe=None):
                self.name, self.first, self.heads = name, first, heads
                self.q, self.k, self.v, self.vn, self.dst = q, k, v, vn, dst
                self.scale, self.s_buf, self.pt_buf = scale, s_buf, pt_buf
                self.widths, self.bias, self.pe = widths, bias, pe

        ATTN = [
            Attention("latent", 0, H, Q1, K1, V1, VN1, O1, (128 + 64) ** -0.5, ar[:, 8:12, :], ar[:, 12:16, :],
                      (P, T), lambda h: causal[:], pe=True),
            Attention("moba", H, H, ZB, ZB + 8, ZB + 16, VN2, O2B, 128 ** -0.5, tx[:, 0:4, :], tx[:, 4:8, :],
                      (P, T), lambda h: bias2[:, h, :]),
            Attention("cross", 2 * H, XH, XQ, XK, XV, XVN, XO, 128 ** -0.5, ar[:, 36:40, :], ar[:, 40:44, :],
                      (T, T), None),
        ]
        ATTN = {a.name: a for a in ATTN}
        v_turned, v_kept = sem("v_turned"), sem("v_kept")
        scored, biased, maxed = sem("scored"), sem("biased"), sem("maxed")
        exped, p_normed, p_inv = sem("exped"), sem("p_normed"), sem("p_inv")
        p_turned, p_kept = sem("p_turned"), sem("p_kept")
        o_summed, o_kept = sem("o_summed"), sem("o_kept")

        def vn(a):
            n = a.heads
            return ar[:, a.vn:a.vn + n, :].rearrange("p c t -> p (c t)")\
                .rearrange("p (k h d) -> p k h d", k=TT, h=n)

        def attention_pe(pe, a, ready, filler=None):
            for w in ready:
                w(pe)
            pairs0 = a.first // 2
            for hp in range(a.heads // 2):
                n = pairs0 + hp
                if n >= 2:
                    pe.wait_ge(v_kept, n - 1)
                for k in range(TT):
                    for hh in range(2):
                        last = nc.tensor.transpose(ps[:, 4 + n % 2, (2 * k + hh) * P:(2 * k + hh + 1) * P],
                                                   ar[:, a.v + 2 * hp + hh, k * P:(k + 1) * P], ident[:])
                last.then_inc(v_turned, 1)
            w0, w1 = a.widths

            def scores(h):
                n = a.first + h
                if h == 0:
                    pe.wait_ge(v_kept, pairs0 + a.heads // 2)
                if n >= 2:
                    pe.wait_ge(biased, n - 1)
                bank = ps[:, 4 + n % 2, :]
                for t, w, at in ((0, w0, 0), (1, w1, w0)):
                    q = ar[:, a.q + h, t * P:(t + 1) * P]
                    last = nc.tensor.matmul(bank[:, at:at + w], q, ar[:, a.k + h, 0:w], start=True, stop=not a.pe)
                    if a.pe:
                        rows = slice(64 * (h % 2), 64 * (h % 2) + 64)
                        last = nc.tensor.matmul(bank[:, at:at + w], ar[rows, a.q + 8 + h // 2, t * P:(t + 1) * P],
                                                ar[rows, KPE, 0:w], start=False, stop=True)
                last.then_inc(scored, 1)

            scores(0)
            scores(1)
            for h in range(a.heads):
                n = a.first + h
                pe.wait_ge(p_normed, n + 1)
                if n >= 1:
                    pe.wait_ge(p_kept, n)
                s = a.s_buf[:, 2 * (n % 2):2 * (n % 2) + 2, :].rearrange("p c t -> p (c t)")
                for t, at, w in ((0, 0, w0), (1, w0, w1)):
                    for k in range(w // P):
                        last = nc.tensor.transpose(ps[:, 6, k * T + t * P:k * T + (t + 1) * P],
                                                   s[:, at + k * P:at + (k + 1) * P], ident[:])
                last.then_inc(p_turned, 1)
                if h + 2 < a.heads:
                    scores(h + 2)
                pe.wait_ge(p_kept, n + 1)
                if n >= 1:
                    pe.wait_ge(o_kept, n)
                pt = a.pt_buf[:, 2 * (n % 2):2 * (n % 2) + 2, :]
                v = vn(a)
                nc.tensor.matmul(ps[:, 7, 0:T], v[:, 0, h, :], pt[:, 0, :], start=True, stop=False)
                q0 = 0 if w0 == T else P
                nc.tensor.matmul(ps[:, 7, q0:T], v[:, 1, h, :], pt[:, 1, q0:T], start=False, stop=True)\
                    .then_inc(o_summed, 1)
                if filler:
                    next(filler, None)

        def attention_act(act, a, filler=None):
            pairs0 = a.first // 2
            for hp in range(a.heads // 2):
                n = pairs0 + hp
                act.wait_ge(v_turned, n + 1)
                nc.scalar.activation(vn(a)[:, :, 2 * hp:2 * hp + 2, :],
                                     ps[:, 4 + n % 2, :].rearrange("p (k h d) -> p k h d", k=TT, h=2),
                                     ACT.Copy).then_inc(v_kept, 1)
            w0, w1 = a.widths

            def out_copy(h):
                n = a.first + h
                act.wait_ge(o_summed, n + 1)
                nc.scalar.activation(ar[:, a.dst + h, :], ps[:, 7, 0:T], ACT.Copy).then_inc(o_kept, 1)

            def probs(h):
                n = a.first + h
                act.wait_ge(maxed, n + 1)
                s = a.s_buf[:, 2 * (n % 2):2 * (n % 2) + 2, :].rearrange("p c t -> p (c t)")
                m = small[:, n % 2, :]
                for t, at, w in ((0, 0, w0), (1, w0, w1)):
                    nc.scalar.activation(s[:, at:at + w], s[:, at:at + w], ACT.Exp, bias=m[:, t:t + 1],
                                         accum_out=m[:, 4 + t:5 + t]).then_inc(exped, 1)

            probs(0)
            for h in range(a.heads):
                n = a.first + h
                if h + 1 < a.heads:
                    probs(h + 1)
                act.wait_ge(p_turned, n + 1)
                if n >= 2:
                    act.wait_ge(o_summed, n - 1)
                pt = a.pt_buf[:, 2 * (n % 2):2 * (n % 2) + 2, :].rearrange("p c t -> p (c t)")
                if w0 == T:
                    ins = nc.scalar.activation(pt, ps[:, 6, :], ACT.Copy)
                else:
                    act_chain.step(nc.scalar.activation(pt[:, T + P:2 * T], ps[:, 6, T + P:2 * T], ACT.Copy))
                    act_chain.sync(act)
                    ins = nc.scalar.activation(pt[:, 0:T], ps[:, 6, 0:T], ACT.Copy)
                ins.then_inc(p_kept, 1)
                out_copy(h)
                if filler:
                    next(filler, None)

        def attention_dve(dve, a, filler=None):
            w0, w1 = a.widths

            def biasing(h):
                n = a.first + h
                dve.wait_ge(scored, n + 1)
                if n >= 2:
                    dve.wait_ge(p_turned, n - 1)
                s = a.s_buf[:, 2 * (n % 2):2 * (n % 2) + 2, :].rearrange("p c t -> p (c t)")[:, 0:w0 + w1]
                bank = ps[:, 4 + n % 2, 0:w0 + w1]
                if a.bias:
                    ins = nc.vector.scalar_tensor_tensor(s, bank, a.scale, a.bias(h), ALU.mult, ALU.add)
                else:
                    ins = nc.vector.tensor_scalar(s, bank, a.scale, None, ALU.mult)
                ins.then_inc(biased, 1)
                dve.wait_ge(biased, n + 1)
                m = small[:, n % 2, :]
                for t, at, w in ((0, 0, w0), (1, w0, w1)):
                    ins = nc.vector.tensor_reduce(m[:, t:t + 1], s[:, at:at + w], AX.X, ALU.max, negate=True)
                    if t == 0:
                        dve_chain.step(ins)
                dve_chain.sync(dve)
                ins.then_inc(maxed, 1)

            biasing(0)
            for h in range(a.heads):
                n = a.first + h
                if h + 1 < a.heads:
                    biasing(h + 1)
                dve.wait_ge(exped, 2 * n + 2)
                m = small[:, n % 2, :]
                s = a.s_buf[:, 2 * (n % 2):2 * (n % 2) + 2, :].rearrange("p c t -> p (c t)")
                nc.vector.reciprocal(m[:, 8:10], m[:, 4:6]).then_inc(p_inv, 1)
                dve.wait_ge(p_inv, n + 1)
                dve_chain.step(nc.vector.tensor_scalar(s[:, 0:w0], s[:, 0:w0], m[:, 8:9], None, ALU.mult))
                dve_chain.sync(dve)
                nc.vector.tensor_scalar(s[:, w0:w0 + w1], s[:, w0:w0 + w1], m[:, 9:10], None, ALU.mult)\
                    .then_inc(p_normed, 1)
                if filler:
                    next(filler, None)

        hn_sq, hn_rows, hn_root = sem("hn_sq"), sem("hn_rows"), sem("hn_root")
        hn_var = sem("hn_var")
        hn_done, hn_spread, hn_used = sem("hn_done"), sem("hn_spread"), sem("hn_used")
        SPREADS = {"l2": 0, "moba": 8, "gdn": 12}
        HN_AT = {"l2": 0, "moba": 1, "gdn": 2}
        HN_SQ = {"l2": 0, "moba": 2, "gdn": 3}
        HN_BANK = {"l2": 0, "moba": 4, "gdn": 4}

        def headnorm_act(act, name, src, n, sq_at, ready, between=None):
            k, s0 = HN_AT[name], HN_SQ[name]
            for w in ready:
                w(act)
            for r in range(n // 8):
                nc.scalar.activation(tx[:, sq_at + 8 * r:sq_at + 8 * r + 8, :], span(src, 8 * r, 8), ACT.Square)\
                    .then_inc(hn_sq, 1)
                yield
            if between:
                between()
            act.wait_ge(hn_var, k + 1)
            act_chain.link(act, nc.scalar.activation(st_y[0:16, :], st_v[0:16, :], ACT.Ln))
            nc.scalar.activation(st_y[0:16, :], st_y[0:16, :], ACT.Exp, scale=-0.5).then_inc(hn_root, 1)

        def headnorm_pe(pe, name, n, sq_at, rows):
            k, s0 = HN_AT[name], HN_SQ[name]
            bank0 = HN_BANK[name]
            for h in range(n):
                if h % 8 == 0:
                    pe.wait_ge(hn_sq, s0 + h // 8 + 1)
                last = nc.tensor.matmul(ps[0:16, bank0 + 3, 0:T], zsel[:, 15 - h:31 - h], tx[:, sq_at + h, :],
                                        start=(h == 0), stop=(h == n - 1))
                if h == n - 1:
                    last.then_inc(hn_rows, 1)
                if h % 8 == 7:
                    yield
            p0 = SPREADS[name]
            pe.wait_ge(hn_done, k + 1)
            for hp in range(n // 2):
                if hp >= 4:
                    pe.wait_ge(hn_used, p0 + hp - 3)
                for hh in range(2):
                    last = spread(bank0 + hp % 4, hh, rows, 2 * hp + hh)
                last.then_inc(hn_spread, 1)
                if hp % 2:
                    yield

        def spread(bank, hh, rows, h):
            return nc.tensor.matmul(ps[:, bank, hh * T:(hh + 1) * T], ident[0:16, h:h + 1].to_broadcast([16, P]),
                                    rows, start=True, stop=True)

        def headnorm_dve(dve, name, src, n, scale, rows, extra=None, between=None):
            k, bank0 = HN_AT[name], HN_BANK[name]
            if name == "l2":
                yield
                yield
            dve.wait_ge(hn_rows, k + 1)
            v, y = st_v[0:16, :], st_y[0:16, :]
            nc.vector.tensor_scalar(v, ps[0:16, bank0 + 3, 0:T], scale, EPS, ALU.mult, ALU.add).then_inc(hn_var, 1)
            if between:
                between()
            dve.wait_ge(hn_root, k + 1)
            for _ in range(2):
                dve_chain.link(dve, nc.vector.tensor_tensor(v, v, y, ALU.mult))
            dve_chain.link(dve, nc.vector.tensor_scalar(v, v, -0.5, 1.5, ALU.mult, ALU.add))
            nc.vector.tensor_tensor(rows, v, y, ALU.mult).then_inc(hn_done, 1)
            yield
            p0 = SPREADS[name]
            for hp in range(n // 2):
                dve.wait_ge(hn_spread, p0 + hp + 1)
                v2 = span(src, 2 * hp, 2).rearrange("p c t -> p (c t)")
                if extra and hp < 4:
                    ins = nc.vector.scalar_tensor_tensor(v2, v2, extra, ps[:, bank0 + hp % 4, :], ALU.mult, ALU.mult)
                else:
                    ins = nc.vector.tensor_tensor(v2, v2, ps[:, bank0 + hp % 4, :], ALU.mult)
                ins.then_inc(hn_used, 1)
                if hp % 2:
                    yield

        rel_in, rel_ps, rel_sb, rel_out, rel_back = (sem(n) for n in ("rel_in", "rel_ps", "rel_sb", "rel_out", "rel_back"))

        def rel_pool(pool):
            pool.wait_ge(products, AHEAD_P + G["qkv_a"].p0)
            pool.wait_ge(st_done, STATS["mix2"][0] + 1)
            pool.dma_start(rel_hot[:], A["hot"]).then_inc(rel_in, 16)
            pool.dma_start(rel_neg[:], A["hot_neg"]).then_inc(rel_in, 16)
            pool.dma_start(rel_b[:], A["rel_bias_2"]).then_inc(rel_in, 16)
            pool.wait_ge(rel_sb, 1)
            pool.dma_start(rel_d, rel_e[:]).then_inc(rel_out, 16)
            pool.wait_ge(rel_out, 16)
            pool.dma_start(rel_s, rel_d.unsqueeze(1).to_broadcast([H, P, 384])).then_inc(rel_out, 16)
            pool.wait_ge(rel_out, 32)
            for h in range(H):
                s = h * P * 384
                pool.dma_start(bias2[:, h, 0:P], bass.AP(rel_s.tensor, s + 255, [[383, P], [1, P]]))\
                    .then_inc(rel_back, 16)
                pool.dma_start(bias2[:, h, P:P + T], bass.AP(rel_s.tensor, s + 127, [[383, P], [1, T]]))\
                    .then_inc(rel_back, 16)
            pool.wait_ge(products, AHEAD_P + G["w_out_2"].p0)
            pool.dma_start(masks[:], A["masks"]).then_inc(mask_in, 16)

        mask_in = sem("mask_in")

        def rel_pe(pe):
            pe.wait_ge(rel_in, 48)
            nc.tensor.matmul(ps[0:H, 7, 0:384], rel_b[:], rel_hot[:], start=True, stop=True).then_inc(rel_ps, 1)

        def rel_dve(dve):
            dve.wait_ge(rel_ps, 1)
            nc.vector.tensor_tensor(rel_e[:], ps[0:H, 7, 0:384], rel_neg[:], ALU.add).then_inc(rel_sb, 1)

        gc_y, gc_act, gc_tap = sem("gc_y"), sem("gc_act"), sem("gc_tap")

        def gconv_dve(dve):
            for b in range(6):
                if b >= 2:
                    dve.wait_ge(gc_act, b - 1)
                for s in range(GDN_K):
                    if s:
                        dve.wait_ge(gc_tap, b * 15 + 4 * s)
                    for m in range(4):
                        c = 4 * b + m
                        y, u = ar[:, 57 + 4 * (b % 2) + m, :], ar[:, ZA + c, :]
                        w = col("gdn_conv", c * GDN_K + GDN_K - 1 - s)
                        if s == 0:
                            ins = nc.vector.tensor_scalar(y, u, w, None, ALU.mult)
                        else:
                            if s == GDN_K - 1 and m == 3:
                                dve.wait_ge(gc_tap, b * 15 + 15)
                            ins = nc.vector.scalar_tensor_tensor(y[:, s:T], u[:, 0:T - s], w, y[:, s:T],
                                                                 ALU.mult, ALU.add)
                        ins.then_inc(*((gc_y, 1) if s == GDN_K - 1 and m == 3 else (gc_tap, 1)))
                    yield

        def gconv_act(act):
            for b in range(6):
                for _ in range(GDN_K):
                    yield
                act.wait_ge(gc_y, b + 1)
                nc.scalar.activation(ar[:, ZA + 4 * b:ZA + 4 * b + 4, :],
                                     ar[:, 57 + 4 * (b % 2):61 + 4 * (b % 2), :], ACT.Silu).then_inc(gc_act, 1)

        NP = 2 * H
        LV = 7

        def prob(base, t=ar):
            return t[:, base:base + 8, :].rearrange("p c t -> p (c t)").rearrange("p (n k) -> p n k", k=P)

        k_of = lambda h, c: ar[:, ZA + 8 + h, c * P:(c + 1) * P]
        q_of = lambda h, c: ar[:, ZA + h, c * P:(c + 1) * P]
        v_of = lambda h, c: ar[:, ZA + 16 + h, c * P:(c + 1) * P]
        at_, qk_, uu_, vb_ = prob(AT), prob(QK), prob(UU), prob(VB)
        tt_, ww_, bb_, u_ = prob(0, tx), prob(8, tx), prob(16, tx), prob(24, tx)
        dt_ = ww_

        def half_prob(base, t=ar):
            return t[:, base:base + 4, :].rearrange("p c t -> p (c t)").rearrange("p (n k) -> p n k", k=P)

        kbg_, kd_, qd_ = half_prob(KBG1), half_prob(KDEC0), half_prob(QDEC1)
        s1_, wt_ = half_prob(16, tx), half_prob(20, tx)
        row_b, row_g = ar[0:16, RBETA, :], ar[0:16, RG, :]
        g_nat = small[:, :, 16:32]
        G_nat = small[:, :, 32:48]
        b_nat = small[:, :, 48:64]
        gl_nat = small[:, 0, 0:16]
        eg_nat = small[:, 1, 0:16]

        def part(v, s):
            return v[:, 8 * s:8 * s + 8, :]

        def pb(n0, n=4):
            return ps[:, n0:n0 + n, :].rearrange("p b t -> p (b t)").rearrange("p (n k) -> p n k", k=P)

        levels = range(1, LV)
        gt = Milestones(sem("gdn_pe"), ["g_nat", "G_row", "nat", "kk", "G_rows", "b_rows", "qk", "vt", "kt", "I_T"] +
                        [f"{x}{l}{s}" for l in levels for x, s in (("W", 0), ("W", 1), ("TW", 0), ("UW", 0), ("TW", 1), ("UW", 1))
                         if not (l == LV - 1 and x == "TW")] +
                        ["u", "wT", "S1", "wS", "o"])
        gs = Milestones(sem("gdn_act"), ["beta", "ea", "e", "l", "x0", "x1", "dt", "qdec", "vb", "kbg", "kd", "T0"] +
                        [f"W{l}{s}" for l in levels for s in range(2)] + ["u", "wT", "S1", "silu_z", "o"])
        gv = Milestones(sem("gdn_dve"), ["ya", "ny", "ab", "m", "sp", "g", "g_nat", "G_row", "nat", "gd", "dt",
                                         "qd", "at1", "at2", "qk1", "qk2", "eb", "B0", "U0"] +
                        ["B10", "B11"] +
                        [f"{x}{l + (x == 'B')}{s}" for l in levels
                         for x, s in (("B", 0), ("B", 1), ("T", 0), ("U", 0), ("T", 1), ("U", 1))
                         if not (l == LV - 1 and x in "BT")] +
                        ["vnew"])

        def gdn_dve(dve):
            ba = ar[0:16, BA, :]
            v0, y0 = st_v[0:16, :], st_y[0:16, :]
            t1 = rs_x[0:16, :]
            gv.reach(nc.vector.tensor_scalar(v0, ba, col("dt_bias", rows=16), None, ALU.add), "ya")
            gv.wait(dve, "ya")
            gv.reach(nc.vector.tensor_scalar(y0, v0, -1.0, None, ALU.mult), "ny")
            gv.wait(dve, "ny")
            gv.reach(nc.vector.tensor_tensor(t1, v0, y0, ALU.max), "ab")
            gv.reach(nc.vector.tensor_scalar(v0, v0, 0.0, None, ALU.max), "m")
            gs.wait(dve, "l")
            gv.wait(dve, "m")
            gv.reach(nc.vector.tensor_tensor(v0, v0, t1, ALU.add), "sp")
            gv.wait(dve, "sp")
            gv.reach(nc.vector.tensor_scalar(v0, v0, small[0:16, 0, 0:1], -1.0, ALU.mult, ALU.mult), "g")
            gt.wait(dve, "g_nat")
            gv.reach(nc.vector.tensor_copy(g_nat, ps[:, 7, 0:32].rearrange("p (c k) -> p c k", c=2)), "g_nat")
            gt.wait(dve, "G_row")
            gv.reach(nc.vector.tensor_copy(row_g, ps[0:16, 6, 0:T]), "G_row")
            gt.wait(dve, "nat")
            dve_chain.link(dve, nc.vector.tensor_copy(G_nat, ps[:, 7, 0:32].rearrange("p (c k) -> p c k", c=2)))
            dve_chain.link(dve, nc.vector.tensor_copy(b_nat, ps[:, 7, 32:64].rearrange("p (c k) -> p c k", c=2)))
            gv.reach(nc.vector.tensor_copy(gl_nat, ps[:, 7, 64:80]), "nat")
            gv.wait(dve, "nat")
            gv.reach(nc.vector.tensor_tensor(gl_nat, gl_nat, G_nat[:, 0, :], ALU.subtract), "gd")
            gt.wait(dve, "G_rows")
            for h in range(H):
                for c in range(2):
                    ins = nc.vector.tensor_scalar(dt_[:, 2 * h + c, :], ps[:, 4 + h // 2, ((h % 2) * 2 + c) * P:((h % 2) * 2 + c + 1) * P],
                                                  G_nat[:, c, 8 + h:9 + h], 0.0, ALU.subtract, ALU.min)
                    if (h, c) != (H - 1, 1):
                        dve_chain.step(ins)
            dve_chain.sync(dve)
            gv.reach(ins, "dt")
            gs.wait(dve, "qdec")
            gv.reach(nc.vector.tensor_tensor(qd_, qd_, ar[:, ZA:ZA + 8, P:T], ALU.mult), "qd")
            gt.wait(dve, "kk")
            gv.reach(nc.vector.tensor_tensor(at_, pb(0), dt_, ALU.mult), "at1")
            gv.wait(dve, "at1")
            gt.wait(dve, "b_rows")
            gv.reach(nc.vector.tensor_tensor(at_, at_, pb(4), ALU.mult), "at2")
            gt.wait(dve, "qk")
            gv.reach(nc.vector.tensor_tensor(qk_, pb(0), dt_, ALU.mult), "qk1")
            gv.wait(dve, "qk1")
            gv.reach(nc.vector.tensor_tensor(qk_, qk_, masks[:, 7:8, :].to_broadcast([P, NP, P]), ALU.mult), "qk2")
            gs.wait(dve, "x1")
            gv.reach(nc.vector.tensor_tensor(eg_nat[:, 0:H], eg_nat[:, H:2 * H], b_nat[:, 1, 0:H], ALU.mult), "eb")
            gv.reach(nc.vector.tensor_tensor(bb_, at_, masks[:, 0:1, :].to_broadcast([P, NP, P]), ALU.mult), "B0")
            gv.wait(dve, "B0")
            gv.reach(nc.vector.tensor_tensor(uu_, ident[:].unsqueeze(1).to_broadcast([P, NP, P]), bb_, ALU.subtract), "U0")

            def next_b(l, s):
                gv.reach(nc.vector.tensor_tensor(part(bb_, s), part(at_, s),
                                                 masks[:, l:l + 1, :].to_broadcast([P, NP // 2, P]), ALU.mult), f"B{l}{s}")

            gv.wait(dve, "U0")
            for s in range(2):
                next_b(1, s)
            for l in levels:
                for s in range(2 if l < LV - 1 else 0):
                    gt.wait(dve, f"W{l}{s}")
                    next_b(l + 1, s)
                for s in range(2):
                    if l < LV - 1:
                        gt.wait(dve, f"TW{l}{s}")
                        gt.wait(dve, f"UW{l}{s}")
                        gv.reach(nc.vector.tensor_tensor(part(tt_, s), part(tt_, s), part(pb(4), s), ALU.subtract), f"T{l}{s}")
                    gt.wait(dve, f"UW{l}{s}")
                    gv.reach(nc.vector.tensor_tensor(part(uu_, s), part(uu_, s), part(pb(0), s), ALU.subtract), f"U{l}{s}")
            gt.wait(dve, "wS")
            gv.reach(nc.vector.tensor_tensor(u_[:, 1:NP:2, :], u_[:, 1:NP:2, :], pb(0, 2), ALU.subtract), "vnew")

        def gdn_act(act):
            nc_a = nc.scalar.activation
            gs.reach(nc_a(row_b, ar[0:16, BA, :], ACT.Sigmoid), "beta")
            gs.reach(nc_a(small[0:16, 0, 0:1], col("a_log", rows=16), ACT.Exp), "ea")
            gv.wait(act, "ab")
            gs.reach(nc_a(rs_x[0:16, :], rs_x[0:16, :], ACT.Exp, scale=-1.0), "e")
            gs.wait(act, "e")
            gs.reach(nc_a(rs_x[0:16, :], rs_x[0:16, :], ACT.Ln, bias=1.0), "l")
            gv.wait(act, "gd")
            gs.reach(nc_a(gl_nat, gl_nat, ACT.Exp), "x0")
            gs.reach(nc_a(eg_nat, G_nat[:, 1, :], ACT.Exp), "x1")
            gv.wait(act, "dt")
            gs.reach(nc_a(dt_, dt_, ACT.Exp), "dt")
            gt.wait(act, "G_rows")
            gs.reach(nc_a(qd_.rearrange("p (b h) k -> p b h k", b=4),
                          ps[:, 4:8, :].rearrange("p b (h c k) -> p b h c k", h=2, c=2)[:, :, :, 1, :], ACT.Exp), "qdec")
            gt.wait(act, "vt")
            for h in range(H):
                for c in range(2):
                    n = 2 * h + c
                    ins = nc_a(vb_[:, n, :], pb(4)[:, n, :], ACT.Copy, scale=b_nat[:, c, h:h + 1])
                    if n < NP - 1:
                        act_chain.step(ins)
            act_chain.sync(act)
            gs.reach(ins, "vb")
            gt.wait(act, "kt")
            gv.wait(act, "eb")
            for h in range(H):
                ins = nc_a(kbg_[:, h, :], pb(0)[:, 2 * h + 1, :], ACT.Copy, scale=eg_nat[:, h:h + 1])
                if h < H - 1:
                    act_chain.step(ins)
            act_chain.sync(act)
            gs.reach(ins, "kbg")
            for h in range(H):
                ins = nc_a(kd_[:, h, :], pb(0)[:, 2 * h, :], ACT.Copy, scale=gl_nat[:, 8 + h:9 + h])
                if h < H - 1:
                    act_chain.step(ins)
            act_chain.sync(act)
            gs.reach(ins, "kd")
            gt.wait(act, "I_T")
            gs.reach(nc_a(tt_, pb(4), ACT.Copy), "T0")
            for l in levels:
                for s in range(2):
                    gt.wait(act, f"W{l}{s}")
                    gs.reach(nc_a(part(ww_, s), part(pb(0), s), ACT.Copy), f"W{l}{s}")
            gt.wait(act, "u")
            gs.reach(nc_a(u_, pb(4), ACT.Copy), "u")
            gt.wait(act, "wT")
            gs.reach(nc_a(wt_, pb(0, 2), ACT.Copy), "wT")
            gt.wait(act, "S1")
            gs.reach(nc_a(s1_, pb(2, 2), ACT.Copy), "S1")
            gs.reach(nc_a(ar[:, ZZ:ZZ + 8, :], ar[:, ZZ:ZZ + 8, :], ACT.Silu), "silu_z")
            gt.wait(act, "o")
            gs.reach(nc_a(prob(OG), pb(4), ACT.Copy), "o")

        def gdn_pe(pe):
            mm, tr = nc.tensor.matmul, nc.tensor.transpose
            gv.wait(pe, "g")
            for c in range(2):
                last = tr(ps[:, 7, 16 * c:16 * c + 16], st_v[0:16, c * P:(c + 1) * P], ident[0:16, 0:16])
            gt.reach(last, "g_nat")
            gv.wait(pe, "g_nat")
            pe.wait_ge(mask_in, 16)
            for c in range(2):
                last = mm(ps[0:16, 6, c * P:(c + 1) * P], g_nat[:, c, :], masks[:, 7, :], start=True, stop=True)
            gt.reach(last, "G_row")
            gv.wait(pe, "G_row")
            gs.wait(pe, "beta")
            for k, row in enumerate((row_g, row_b)):
                for c in range(2):
                    tr(ps[:, 7, 32 * k + 16 * c:32 * k + 16 * c + 16], row[:, c * P:(c + 1) * P], ident[0:16, 0:16])
            gt.reach(mm(ps[:, 7, 64:80], ones[:], g_nat[:, 0, :], start=True, stop=True), "nat")
            for n in range(NP):
                last = mm(pb(0)[:, n, :], k_of(n // 2, n % 2), k_of(n // 2, n % 2), start=True, stop=True)
            gt.reach(last, "kk")
            gv.wait(pe, "nat")
            for h in range(H):
                last = spread(4 + h // 2, h % 2, row_g, 8 + h)
            gt.reach(last, "G_rows")
            gv.wait(pe, "dt")
            gs.wait(pe, "qdec")
            for h in range(H):
                last = spread(4 + h // 2, h % 2, row_b, h)
            gt.reach(last, "b_rows")
            gv.wait(pe, "at1")
            for n in range(NP):
                last = mm(pb(0)[:, n, :], k_of(n // 2, n % 2), q_of(n // 2, n % 2), start=True, stop=True)
            gt.reach(last, "qk")
            gv.wait(pe, "at2")
            for n in range(NP):
                last = tr(pb(4)[:, n, :], v_of(n // 2, n % 2), ident[:])
            gt.reach(last, "vt")
            gv.wait(pe, "qk1")
            for n in range(NP):
                last = tr(pb(0)[:, n, :], k_of(n // 2, n % 2), ident[:])
            gt.reach(last, "kt")
            gs.wait(pe, "vb")
            gv.wait(pe, "U0")
            for n in range(NP):
                last = tr(pb(4)[:, n, :], uu_[:, n, :], ident[:])
            gt.reach(last, "I_T")
            gs.wait(pe, "T0")
            gs.wait(pe, "kd")
            for l in levels:
                for s in range(2):
                    gv.wait(pe, f"B{l}{s}")
                    if l > 1:
                        gv.wait(pe, f"U{l - 1}{s}")
                    for n in range(8 * s, 8 * s + 8):
                        last = mm(pb(0)[:, n, :], bb_[:, n, :], tt_[:, n, :], start=True, stop=True)
                    gt.reach(last, f"W{l}{s}")
                for s in range(2):
                    gs.wait(pe, f"W{l}{s}")
                    if l < LV - 1:
                        for n in range(8 * s, 8 * s + 8):
                            last = mm(pb(4)[:, n, :], uu_[:, n, :], ww_[:, n, :], start=True, stop=True)
                        gt.reach(last, f"TW{l}{s}")
                    for n in range(8 * s, 8 * s + 8):
                        last = mm(pb(0)[:, n, :], ww_[:, n, :], uu_[:, n, :], start=True, stop=True)
                    gt.reach(last, f"UW{l}{s}")
            gv.wait(pe, f"U{LV - 1}1")
            for n in range(NP):
                last = mm(pb(4)[:, n, :], uu_[:, n, :], vb_[:, n, :], start=True, stop=True)
            gt.reach(last, "u")
            for h in range(H):
                last = mm(pb(0)[:, h, :], kbg_[:, h, :], uu_[:, 2 * h + 1, :], start=True, stop=True)
            gt.reach(last, "wT")
            gs.wait(pe, "u")
            for h in range(H):
                last = mm(pb(2)[:, h, :], kd_[:, h, :], u_[:, 2 * h, :], start=True, stop=True)
            gt.reach(last, "S1")
            gs.wait(pe, "S1")
            for h in range(H):
                last = mm(pb(0)[:, h, :], wt_[:, h, :], s1_[:, h, :], start=True, stop=True)
            gt.reach(last, "wS")
            gv.wait(pe, "vnew")
            gv.wait(pe, "qd")
            for h in range(H):
                mm(pb(4)[:, 2 * h, :], u_[:, 2 * h, :], qk_[:, 2 * h, :], start=True, stop=True)
                mm(pb(4)[:, 2 * h + 1, :], s1_[:, h, :], qd_[:, h, :], start=True, stop=False)
                last = mm(pb(4)[:, 2 * h + 1, :], u_[:, 2 * h + 1, :], qk_[:, 2 * h + 1, :], start=False, stop=True)
            gt.reach(last, "o")

        def conv_norms_pe(pe):
            sum_pe(pe, "mean")
            yield
            yield
            sum_pe(pe, "ln")
            yield
            yield
            yield
            sum_pe(pe, "conv")
            yield

        def conv_norms_act(act):
            root(act, "mean")
            yield
            for k in range(2):
                square_act(act, "ln", k, u_src, 4, lambda c: (st_done, STATS["mean"][0] + 1))
            yield
            yield
            root(act, "ln")
            yield
            act.wait_ge(applied, 1)
            for c in range(CC):
                nc.scalar.activation(ar[:, Z1 + c, :], ar[:, Z1 + c, :], ACT.Silu, bias=col("conv_ln_b", c),
                                     scale=col("conv_ln_g", c)).then_inc(ln_out, 1)
            yield
            for k in range(2):
                square_act(act, "conv", k, u_src, 4, lambda c: (ln_out, c + 1))
            yield
            root(act, "conv")
            yield
            square_act(act, "attn", 0, attn_src, 4, lambda c: (o_kept, c + 1))
            yield

        def conv_norms_dve(dve):
            dve.wait_ge(conv_pe, 1)
            for c in range(CV, CC):
                nc.vector.tensor_scalar(ar[:, Z1 + c, :], ps[:, c - CV, 0:T], col("conv_b", c), None, ALU.add)\
                    .then_inc(tap1, 1)
            dve.wait_ge(tap1, CV * CONV_K + CC - CV)
            for k in range(2):
                reduce_dve(dve, "mean", k, 4, u_src)
            yield
            r = STATS["mean"][0]
            dve.wait_ge(st_root, r + 1)
            nc.vector.tensor_tensor(span(u_src, 0, CC), span(u_src, 0, CC), bc(st_y, CC), ALU.subtract)\
                .then_inc(st_done, 1)
            dve.wait_ge(st_done, r + 1)
            yield
            for k in range(2):
                reduce_dve(dve, "ln", k, 4)
            yield
            refine(dve, "ln")
            yield
            apply(dve, u_src, CC)
            yield
            for k in range(2):
                reduce_dve(dve, "conv", k, 4)
            yield
            refine(dve, "conv")
            yield
            apply(dve, u_src, CC)
            reduce_dve(dve, "attn", 0, 4)
            yield

        def apply(dve, src, n, first=0):
            v = span(src, first, n)
            nc.vector.tensor_tensor(v, v, bc(st_y, n), ALU.mult).then_inc(applied, 1)
            apply.n += 1
            dve.wait_ge(applied, apply.n)
        apply.n = 0

        block = ctx.enter_context(nc.Block())
        N_AUX = 4
        mem_in, out_done, start_v, start_p = sem("mem_in"), sem("out_done"), sem("start_v"), sem("start_p")
        zsel = sb("zsel", [P, 32], F32, room(128))
        applied, ln_out, x_added, out_ready = sem("applied"), sem("ln_out"), sem("x_added"), sem("out_ready")

        @block.sync
        def _(sp):
            sp.dma_start(cols[:], A["cols"]).then_inc(cols_loaded, 16)
            for g in GEMMS:
                load(sp, g)

        @block.gpsimd
        def _(pool):
            pool.memset(ones[:], 1.0).then_inc(start_p, 1)
            pool.memset(zsel[:], 0.0).then_inc(start_p, 1)
            pool.wait_ge(start_p, 2)
            pool.memset(zsel[:, 15:16], 1.0).then_inc(start_p, 1)
            pool.dma_start(ident[:], A["ident"]).then_inc(aux_loaded, 16)
            pool.dma_start(pos_i[:], A["positions"].partition_broadcast(P).rearrange("a b t -> a (b t)")).then_inc(aux_loaded, 16)
            pool.dma_start(causal[:], A["causal"]).then_inc(aux_loaded, 16)
            pool.dma_start(rope_m[:], A["rope_m"]).then_inc(aux_loaded, 16)
            rel_pool(pool)
            gt.wait(pool, "o")
            gs.wait(pool, "o")
            pool.dma_start(ar[:, MEM:MEM + DC, :], A["mem"]).then_inc(mem_in, 16)

        def norm(name):
            return {"x": (D, rs_x[:]), "q": (768, rs_x[:]), "kv": (512, rs_kv), "mean": (1024, None),
                    "ln": (1024, st_y[:]), "conv": (1024, st_y[:]), "attn": (1024, st_y[:]), "mix": (D, st_y[:]),
                    "ffn": (D, rs_x[:]), "ff": (D, st_y[:]), "mix2": (D, rs_x[:]), "mem": (D, rs_x[:]),
                    "xq": (D, rs_x[:]), "ffn2": (D, rs_x[:]), "final": (D, st_y[:])}[name]

        def root(act, name):
            root_act(act, name, norm(name)[0])

        def refine(dve, name):
            refine_dve(dve, name, *norm(name))

        def groups_out(name):
            g = G[name]
            n = sum(gr["kind"] == "z" for gr in g.groups)
            return lambda c=None: (group_out, g.g0 + g.turns * n)

        mix_out, ff_out = source(ar, M1), source(tx, 16)
        u_src, attn_src, q_src, kv_src = source(ar, Z1), source(ar, O1), source(ar, Z1 + 16), source(ar, Z1 + 22)
        og_src, moba_src, mem_src, xo_src = source(ar, OG), source(ar, O2B), source(ar, MEM), source(ar, XO)
        l2_src = source(ar, ZA)

        @block.scalar
        def _(act):
            def ahead_(name, between=None):
                ahead(act, split_act, evict_act, G[name], between)

            def run_(name, filler=None, fill_from=0, stat=None):
                run(act, split_act, evict_act, G[name], filler, fill_from,
                    stat and (FIRST + 2, lambda: [root(act, name) for name in stat]))

            for k in range(4):
                act.dma_start(xt[:, 4 * k:4 * k + 4, :], A["xt"][:, 4 * k:4 * k + 4, :]).then_inc(xt_loaded[k], 16)
            act.wait_ge(cols_loaded, 16)
            ahead_("conv_in")
            prep_act(act, "x", xs, gain_of("pre_mix"), lambda c: (xt_loaded[c // 4], 16), "x")
            run_("conv_in", glu_act(act, 0), 3, stat=["x"])
            rope_tables_act(act)
            ahead_("latents")
            finish(glu_act(act, 1))
            run_("latents")
            ahead_("uq", lambda: prep_act(act, "q", q_src, gain_of("q_norm"),
                                          lambda c: (group_out, G["latents"].g0 + 2), "q", "latents"))
            prep_act(act, "kv", kv_src, gain_of("kv_norm"), groups_out("latents"), "kv")
            run_("uq", stat=["q", "kv"])
            ahead_("ukv")
            run_("ukv")
            ahead_("w_out")
            diag_act(act)
            attention_act(act, ATTN["latent"], conv_norms_act(act))
            square_act(act, "attn", 1, attn_src, 4, lambda c: (o_kept, c + 1))
            prep_act(act, "conv", u_src, gain_of("conv_out"), lambda c: (applied, 2), None, "ukv")
            root(act, "attn")
            prep_act(act, "attn", attn_src, gain_of("attn_out"), lambda c: (applied, 3))
            run_("w_out")
            ahead_("ffn")
            root(act, "mix")
            prep_act(act, "ffn", xs, gain_of("pre_ffn"), lambda c: (x_added, c + 1), "ffn", "w_out")
            run_("ffn", stat=["ffn"])
            ahead_("down")
            run_("down")
            ahead_("qkv_a")
            root(act, "ff")
            prep_act(act, "mix2", xs, gain_of("mix2"), lambda c: (x_added, DC + c + 1), "mix2", "ffn")
            run_("qkv_a", stat=["mix2"])
            ahead_("z_ba")
            act.wait_ge(*groups_out("qkv_a")())
            filler = gconv_act(act)
            run_("z_ba", filler)
            ahead_("qkv_b")
            run_("qkv_b", filler)
            ahead_("w_out_2")
            l2 = headnorm_act(act, "l2", l2_src, 16, 8, [lambda e: e.wait_ge(gc_act, 6)])
            attention_act(act, ATTN["moba"], l2)
            finish(l2)
            finish(headnorm_act(act, "moba", moba_src, 8, 16, [lambda e: e.wait_ge(o_kept, 2 * H)]))
            gdn_act(act)
            finish(headnorm_act(act, "gdn", og_src, 8, 0, [lambda e: gs.wait(e, "o")],
                                lambda: prep_act(act, "moba", moba_src, lambda c: col("moba_norm"), lambda c: (hn_used, 12))))
            prep_act(act, "gdn", og_src, lambda c: col("gdn_norm"), lambda c: (applied, 3 + 8 + 1))
            run_("w_out_2")
            ahead_("xkv")
            prep_act(act, "mem", mem_src, gain_of("mem"), lambda c: (mem_in, 16), "mem", "w_out_2")
            run_("xkv", stat=["mem"])
            ahead_("xq")
            prep_act(act, "xq", xs, gain_of("xattn"), banks_out("w_out_2"), "xq", "xkv")
            run_("xq", stat=["xq"])
            ahead_("xo")
            attention_act(act, ATTN["cross"])
            prep_act(act, "xo", xo_src, None, lambda c: (o_kept, 2 * H + c + 1), None, "xq")
            run_("xo")
            ahead_("ffn_2")
            prep_act(act, "ffn2", xs, gain_of("ffn2"), banks_out("xo"), "ffn2", "xo")
            run_("ffn_2", stat=["ffn2"])
            ahead_("down_2")
            run_("down_2")
            g = G["down_2"]
            finish(evict_act(act, g, g.turns - 1, g.groups[-1]))
            root(act, "final")
            for k in range(4):
                act.wait_ge(out_ready, 4 * k + 4)
                act.dma_start(out[:, 4 * k:4 * k + 4, :], tx[:, 4 * k:4 * k + 4, :]).then_inc(out_done, 16)
            act.wait_ge(out_done, 64)

        @block.vector
        def _(dve):
            def ahead_(name, between=None):
                ahead(dve, split_dve, evict_dve, G[name], between)

            def run_(name, filler=None, fill_from=0, stat=None):
                run(dve, split_dve, evict_dve, G[name], filler, fill_from,
                    stat and (FIRST + 2, lambda: [refine(dve, name) for name in stat]))

            def add_norm(name, src, gain, prep, pgain):
                refine(dve, name)
                for k in range(DC // 4 + 1):
                    if k < DC // 4:
                        apply(dve, src, 4, 4 * k)
                        for c in range(4 * k, 4 * k + 4):
                            nc.vector.scalar_tensor_tensor(xt[:, c, :], src(c), col(gain, c), xt[:, c, :],
                                                           ALU.mult, ALU.add).then_inc(x_added, 1)
                    if k:
                        prep_dve(dve, prep, xs, gain_of(pgain), prep, 4 * (k - 1), 4)

            dve.sem_inc(bank_free, AHEAD_B)
            dve.wait_ge(cols_loaded, 16)
            ahead_("conv_in")
            prep_dve(dve, "x", xs, gain_of("pre_mix"), "x")
            filler = conv_steps(dve)
            run_("conv_in", filler, 3, stat=["x"])
            rope_tables_dve(dve)
            ahead_("latents")
            run_("latents", filler)
            ahead_("uq", lambda: prep_dve(dve, "q", q_src, gain_of("q_norm"), "q"))
            prep_dve(dve, "kv", kv_src, gain_of("kv_norm"), "kv")
            run_("uq", filler, stat=["q", "kv"])
            ahead_("ukv")
            run_("ukv", filler)
            ahead_("w_out")
            rope_dve(dve)
            finish(filler)
            attention_dve(dve, ATTN["latent"], conv_norms_dve(dve))
            reduce_dve(dve, "attn", 1, 4)
            prep_dve(dve, "conv", u_src, gain_of("conv_out"))
            refine(dve, "attn")
            apply(dve, attn_src, H)
            prep_dve(dve, "attn", attn_src, gain_of("attn_out"))
            run_("w_out")
            ahead_("ffn")
            add_norm("mix", mix_out, "post_mix", "ffn", "pre_ffn")
            run_("ffn", stat=["ffn"])
            ahead_("down")
            run_("down")
            ahead_("qkv_a")
            add_norm("ff", ff_out, "post_ffn", "mix2", "mix2")
            run_("qkv_a", stat=["mix2"])
            ahead_("z_ba")
            dve.wait_ge(*groups_out("qkv_a")())
            filler = gconv_dve(dve)
            run_("z_ba", filler)
            rel_dve(dve)
            ahead_("qkv_b")
            run_("qkv_b", filler)
            ahead_("w_out_2")
            dve.wait_ge(rel_back, 16 * 2 * H)
            row = ar[0:16, RQK, :]
            l2 = headnorm_dve(dve, "l2", l2_src, 16, 1.0, row, extra=P ** -0.5)
            attention_dve(dve, ATTN["moba"], l2)
            finish(l2)
            finish(headnorm_dve(dve, "moba", moba_src, 8, 1 / P, row))
            gdn_dve(dve)
            finish(headnorm_dve(dve, "gdn", og_src, 8, 1 / P, row, None,
                                lambda: prep_dve(dve, "moba", moba_src, lambda c: col("moba_norm"))))
            gs.wait(dve, "silu_z")
            dve.wait_ge(hn_used, 16)
            nc.vector.tensor_tensor(span(og_src, 0, H), span(og_src, 0, H), ar[:, ZZ:ZZ + H, :], ALU.mult)\
                .then_inc(applied, 1)
            prep_dve(dve, "gdn", og_src, lambda c: col("gdn_norm"))
            run_("w_out_2")
            ahead_("xkv")
            prep_dve(dve, "mem", mem_src, gain_of("mem"), "mem")
            run_("xkv", stat=["mem"])
            ahead_("xq")
            prep_dve(dve, "xq", xs, gain_of("xattn"), "xq")
            run_("xq", stat=["xq"])
            ahead_("xo")
            attention_dve(dve, ATTN["cross"])
            prep_dve(dve, "xo", xo_src, None)
            run_("xo")
            ahead_("ffn_2")
            prep_dve(dve, "ffn2", xs, gain_of("ffn2"), "ffn2")
            run_("ffn_2", stat=["ffn2"])
            ahead_("down_2")
            run_("down_2")
            g = G["down_2"]
            finish(evict_dve(dve, g, g.turns - 1, g.groups[-1]))
            refine(dve, "final")
            for c in range(DC):
                nc.vector.scalar_tensor_tensor(tx[:, c, :], xt[:, c, :], col("final", c), st_y[:],
                                               ALU.mult, ALU.mult).then_inc(out_ready, 1)

        @block.tensor
        def _(pe):
            pe.sem_inc(products, AHEAD_P)
            pe.wait_ge(start_p, 3)
            multiply(pe, G["conv_in"], "x")
            multiply(pe, G["latents"])
            multiply(pe, G["uq"], "q", "kv")
            multiply(pe, G["ukv"])
            pe.wait_ge(aux_loaded, 16 * N_AUX)
            rope_pe(pe)
            long_conv_pe(pe)
            attention_pe(pe, ATTN["latent"], [lambda e: e.wait_ge(*groups_out("ukv")()),
                                              lambda e: rope_o.wait(e, "k")], conv_norms_pe(pe))
            sum_pe(pe, "attn")
            multiply(pe, G["w_out"])
            sum_pe(pe, "mix")
            multiply(pe, G["ffn"], "ffn")
            multiply(pe, G["down"])
            sum_pe(pe, "ff")
            multiply(pe, G["qkv_a"], "mix2")
            multiply(pe, G["z_ba"])
            pe.wait_ge(bank_free, AHEAD_B + G["z_ba"].e0 + 8)
            rel_pe(pe)
            pe.wait_ge(rel_sb, 1)
            multiply(pe, G["qkv_b"])
            pe.wait_ge(bank_free, AHEAD_B + G["w_out_2"].e0)
            rows = ar[0:16, RQK, :]
            l2 = headnorm_pe(pe, "l2", 16, 8, rows)
            attention_pe(pe, ATTN["moba"], [lambda e: e.wait_ge(*groups_out("qkv_b")())], l2)
            finish(l2)
            pe.wait_ge(o_kept, 2 * H)
            pe.wait_ge(biased, 2 * H)
            finish(headnorm_pe(pe, "moba", 8, 16, rows))
            pe.wait_ge(hn_used, 12)
            gdn_pe(pe)
            hn = headnorm_pe(pe, "gdn", 8, 0, rows)
            next(hn)
            multiply(pe, G["w_out_2"], between=(2, lambda: finish(hn)))
            multiply(pe, G["xkv"], "mem")
            multiply(pe, G["xq"], "xq")
            pe.wait_ge(st_done, STATS["xq"][0] + 1)
            attention_pe(pe, ATTN["cross"], [lambda e: e.wait_ge(*groups_out("xq")())])
            multiply(pe, G["xo"])
            pe.wait_ge(o_kept, 2 * H + XH)
            multiply(pe, G["ffn_2"], "ffn2")
            multiply(pe, G["down_2"])
            sum_pe(pe, "final")


_IN = ["positions", "w_in", "w_uq", "w_ukv", "w_out", "w_gate", "w_up", "w_down", "w_in_2", "w_out_2",
       "w_xq_2", "w_xkv_2", "w_xo_2", "w_gate_2", "w_up_2", "w_down_2", "rel_bias_2"]
_DROP_LAYER = {n for n in _IN if n.startswith("w_")}


def _chunks(v):
    return np.ascontiguousarray(v.reshape(-1, P).T)


def layout(inputs):
    a = {n: np.asarray(inputs[n]) for n in inputs}
    arrays = {n: a[n][0] if n in _DROP_LAYER else a[n] for n in _IN}
    taps = lambda w: np.ascontiguousarray(w.reshape(w.shape[0], -1, P).transpose(2, 1, 0)).reshape(P, -1)
    heads = lambda v: np.concatenate([np.zeros(H, np.float32), v, np.zeros(P - 2 * H, np.float32)])[:, None]
    half = np.arange(P) % 32
    inv = (np.float32(10000.0) ** (-np.arange(0, 64, 2, dtype=np.float32) / np.float32(64))).astype(np.float32)
    vec = {"pre_mix": "pre_mix_norm", "q_norm": "q_norm", "kv_norm": "kv_norm", "conv_b": "conv_b",
           "conv_ln_g": "conv_ln_g", "conv_ln_b": "conv_ln_b", "conv_out": "conv_out_norm",
           "attn_out": "attn_out_norm", "post_mix": "post_mix_norm", "pre_ffn": "pre_ffn_norm",
           "post_ffn": "post_ffn_norm", "mix2": "mix_norm_g_2", "gdn_norm": "gdn_norm_g_2",
           "moba_norm": "moba_norm_g_2", "xattn": "xattn_norm_g_2", "mem": "mem_norm_g_2",
           "ffn2": "ffn_norm_g_2", "ffn_conv_b": "ffn_conv_b_2", "final": "final_norm_g_2"}
    parts = {k: _chunks(a[v]) for k, v in vec.items()}
    parts["conv_w"] = taps(a["conv_w"][0])
    parts["gdn_conv"] = taps(a["gdn_conv_w_2"][0])
    parts["ffn_conv"] = taps(a["ffn_conv_w_2"][0])
    parts["a_log"] = heads(a["gdn_a_log_2"][0])
    parts["dt_bias"] = heads(a["gdn_dt_bias_2"][0])
    parts["inv_freq"] = inv[half][:, None]
    for k, (_, n) in COLUMNS.items():
        assert parts[k].shape == (P, n), (k, parts[k].shape)
    arrays["cols"] = np.concatenate([parts[k] for k in COLUMNS], 1)
    arrays["xt"] = np.ascontiguousarray(a["x"][0].T.reshape(DC, P, T).transpose(1, 0, 2))
    arrays["mem"] = np.ascontiguousarray(a["mem_2"][0].T.reshape(DC, P, T).transpose(1, 0, 2))
    arrays.update(constants())
    return {n: np.ascontiguousarray(v) for n, v in arrays.items()}


def kernel(**inputs):
    import concourse.bacc as bacc
    from concourse.bass_utils import run_bass_kernel_spmd

    nc = bacc.Bacc("TRN2", target_bir_lowering=False, num_devices=1)
    arrays = {f"in_{n}": v for n, v in layout(inputs).items()}
    aps = {n[3:]: nc.dram_tensor(n, v.shape, mybir.dt.from_np(v.dtype), kind="ExternalInput").ap()
           for n, v in arrays.items()}
    out = nc.dram_tensor("out_t", [P, DC, T], F32, kind="ExternalOutput").ap()
    build(nc, aps, out)
    r = run_bass_kernel_spmd(nc, [arrays], core_ids=[0])
    y = r.results[0]["out_t"]
    return np.ascontiguousarray(y.transpose(1, 0, 2).reshape(D, T).T)[None]
```
